# Optimizing a Trainium2 kernel written in Bass

```python
import math
import jax, jax.numpy as jnp
from jax import lax
import numpy as np

D_MODEL = 1024
BATCH = 1
SEQ = 256
DEPTH = 1
DEC_BATCH = 1
DEC_SEQ = 1024
PAST_LEN = 256

GRID_W = 64
EPS = 1e-6
D_HY = 512
HY_SHORT = 3
N_BANDS = 8
FILT_EMB = 1 + 2 * N_BANDS
FILT_HID = 64
DECAY_SLOW = -math.log(1e-2) / 1.5
DECAY_FAST = -math.log(1e-2) / 0.3
D_FN = 512
N_FN_GROUPS = 4
FN_GROUP = D_FN // N_FN_GROUPS
D_RG = 1024
N_RG_BLOCKS = 8
RG_BLOCK = D_RG // N_RG_BLOCKS
RG_CONV = 4
RG_C = 8.0
D_FF = -(-8 * D_MODEL // (3 * 256)) * 256
D_IN = 3 * D_HY + D_FN + 2 * D_RG + 3 * D_MODEL
SPLITS = (3 * D_HY, 3 * D_HY + D_FN, 3 * D_HY + D_FN + D_RG, 3 * D_HY + D_FN + 2 * D_RG)

kernel_name = 'hybrid_hyena_fnet_rglru_prefix_step'

def rmsnorm(x, g):
    xf = x.astype(jnp.float32)
    y = xf * lax.rsqrt(jnp.mean(xf * xf, axis=-1, keepdims=True) + EPS)
    return (y * g.astype(jnp.float32)).astype(x.dtype)

def depthwise_conv(x, w, b, pad_l, pad_r):
    L = x.shape[1]
    xp = jnp.pad(x, ((0, 0), (pad_l, pad_r), (0, 0)))
    out = b
    for k in range(w.shape[0]):
        out = out + xp[:, k:k + L] * w[k]
    return out

def hyena_filters(L, fw1, fb1, fw2, fb2, fw3, ffreq):
    f32 = jnp.float32
    t = jnp.arange(L, dtype=f32) / L
    ang = 2.0 * math.pi * t[:, None] * jnp.arange(1, N_BANDS + 1, dtype=f32)
    feats = jnp.concatenate([t[:, None], jnp.sin(ang), jnp.cos(ang)], axis=-1)
    freq = ffreq.astype(f32)
    h = jnp.sin(freq * (feats @ fw1.astype(f32) + fb1.astype(f32)))
    h = jnp.sin(freq * (h @ fw2.astype(f32) + fb2.astype(f32)))
    h = (h @ fw3.astype(f32)).reshape(L, 2, 2, D_HY)
    deltas = jnp.linspace(DECAY_SLOW, DECAY_FAST, D_HY, dtype=f32)
    h = h * jnp.exp(-t[:, None] * deltas)[:, None, None, :]
    fwd = h[:, :, 0]
    bwd = h[1:, :, 1][::-1]
    k = jnp.concatenate([fwd, jnp.zeros((1, 2, D_HY), f32), bwd], axis=0)
    k = k * lax.rsqrt(jnp.sum(k * k, axis=0, keepdims=True) + EPS)
    return jnp.fft.rfft(k, axis=0)

def fft_conv(z, kf):
    L = z.shape[1]
    zf = jnp.fft.rfft(z, n=2 * L, axis=1)
    return jnp.fft.irfft(zf * kf, n=2 * L, axis=1)[:, :L]

def hyena_branch(u, conv_w, conv_b, kf, bias):
    u = depthwise_conv(u, conv_w, conv_b, HY_SHORT // 2, HY_SHORT - 1 - HY_SHORT // 2).astype(jnp.float32)
    v, x1, x2 = jnp.split(u, 3, axis=-1)
    bias = bias.astype(jnp.float32)
    z = x1 * (fft_conv(v, kf[:, 0]) + bias[0] * v)
    z = x2 * (fft_conv(z, kf[:, 1]) + bias[1] * z)
    return z

def fnet_branch(u):
    B, L, _ = u.shape
    g = u.astype(jnp.float32).reshape(B, L, N_FN_GROUPS, FN_GROUP)
    return jnp.real(jnp.fft.fft2(g, axes=(1, 3), norm='ortho')).reshape(B, L, D_FN)

def _lin_combine(e1, e2):
    a1, b1 = e1
    a2, b2 = e2
    return a1 * a2, a2 * b1 + b2

def rglru_scan(x, w_r, b_r, w_i, b_i, lam, h0, reverse, reset):
    f32 = jnp.float32
    B, L, _ = x.shape
    xb = x.reshape(B, L, N_RG_BLOCKS, RG_BLOCK)
    r = jax.nn.sigmoid(jnp.einsum('blnc,ncd->blnd', xb, w_r.astype(f32)).reshape(B, L, D_RG) + b_r.astype(f32))
    i = jax.nn.sigmoid(jnp.einsum('blnc,ncd->blnd', xb, w_i.astype(f32)).reshape(B, L, D_RG) + b_i.astype(f32))
    log_a = -RG_C * r * jax.nn.softplus(-lam.astype(f32))
    a = jnp.exp(log_a)
    mult = jnp.sqrt(-jnp.expm1(2.0 * log_a))
    if reset:
        mult = mult.at[:, L - 1 if reverse else 0].set(1.0)
    A, Bc = lax.associative_scan(_lin_combine, (a, mult * (i * x)), axis=1, reverse=reverse)
    h = Bc + A * h0[:, None, :]
    final = h[:, 0] if reverse else h[:, -1]
    return h, final

def trunk_layer(x, mod, rg_h0, reset, lp):
    (n1, n2, w_in, hcw, hcb, fw1, fb1, fw2, fb2, fw3, ffreq, hbias, w_a, w_b,
     rcw, rcb, wr, br, wi, bi, lam, w_c, w_o, w_gu, w_down) = lp
    dt = x.dtype
    L = x.shape[1]
    sh1, sc1, g1, sh2, sc2, g2 = jnp.split(mod[:, None, :].astype(dt), 6, axis=-1)
    h = rmsnorm(x, n1) * (1 + sc1) + sh1
    u = h @ w_in
    u_hy, u_fn, u_rx, u_ry, u_g = jnp.split(u, SPLITS, axis=-1)
    kf = hyena_filters(L, fw1, fb1, fw2, fb2, fw3, ffreq)
    y_a = hyena_branch(u_hy, hcw, hcb, kf, hbias).astype(dt) @ w_a
    y_b = fnet_branch(u_fn).astype(dt) @ w_b
    xr = depthwise_conv(u_rx, rcw, rcb, RG_CONV // 2, RG_CONV - 1 - RG_CONV // 2).astype(jnp.float32)
    h_f, s_f = rglru_scan(xr, wr[0], br[0], wi[0], bi[0], lam[0], rg_h0[:, 0], False, reset)
    h_b, s_b = rglru_scan(xr, wr[1], br[1], wi[1], bi[1], lam[1], rg_h0[:, 1], True, reset)
    y_c = ((h_f + h_b).astype(dt) * jax.nn.gelu(u_ry)) @ w_c
    ga, gb, gc = jnp.split(jax.nn.sigmoid(u_g), 3, axis=-1)
    x = x + g1 * ((ga * y_a + gb * y_b + gc * y_c) @ w_o)
    h = rmsnorm(x, n2) * (1 + sc2) + sh2
    gt, up = jnp.split(h @ w_gu, 2, axis=-1)
    x = x + g2 * ((jax.nn.silu(gt) * up) @ w_down)
    return x, jnp.stack([s_f, s_b], axis=1)

def setup_inputs(seed: int = 0) -> dict:
    key = jax.random.key(seed)
    ks = iter(jax.random.split(key, 48))

    def nrm(shape, scale):
        return jax.random.normal(next(ks), shape, jnp.float32) * scale

    D = D_MODEL
    lam_u = jax.random.uniform(next(ks), (DEPTH, 2, D_RG), jnp.float32, 0.9, 0.999)
    return {
        'x_prompt': nrm((BATCH, SEQ, D), 1.0),
        'x_sample': nrm((DEC_BATCH, DEC_SEQ, D), 1.0),
        'c': nrm((DEC_BATCH, D), 1.0),
        'state_rglru': nrm((DEC_BATCH, DEPTH, 2, D_RG), 0.5),
        'c_ctx': nrm((D,), 1.0),
        'norm1_g': 1.0 + nrm((DEPTH, D), 0.02),
        'norm2_g': 1.0 + nrm((DEPTH, D), 0.02),
        'w_ada': nrm((DEPTH, D, 6 * D), 0.5 * D ** -0.5),
        'b_ada': nrm((DEPTH, 6 * D), 0.01),
        'w_in': nrm((DEPTH, D, D_IN), D ** -0.5),
        'hy_conv_w': nrm((DEPTH, HY_SHORT, 3 * D_HY), HY_SHORT ** -0.5),
        'hy_conv_b': nrm((DEPTH, 3 * D_HY), 0.01),
        'hy_f_w1': nrm((DEPTH, FILT_EMB, FILT_HID), FILT_EMB ** -0.5),
        'hy_f_b1': nrm((DEPTH, FILT_HID), 0.1),
        'hy_f_w2': nrm((DEPTH, FILT_HID, FILT_HID), FILT_HID ** -0.5),
        'hy_f_b2': nrm((DEPTH, FILT_HID), 0.1),
        'hy_f_w3': nrm((DEPTH, FILT_HID, 4 * D_HY), FILT_HID ** -0.5),
        'hy_f_freq': 1.0 + nrm((DEPTH, FILT_HID), 0.1),
        'hy_bias': nrm((DEPTH, 2, D_HY), 0.1),
        'w_a': nrm((DEPTH, D_HY, D), D_HY ** -0.5),
        'w_b': nrm((DEPTH, D_FN, D), D_FN ** -0.5),
        'rg_conv_w': nrm((DEPTH, RG_CONV, D_RG), RG_CONV ** -0.5),
        'rg_conv_b': nrm((DEPTH, D_RG), 0.01),
        'rg_wr': nrm((DEPTH, 2, N_RG_BLOCKS, RG_BLOCK, RG_BLOCK), RG_BLOCK ** -0.5),
        'rg_br': nrm((DEPTH, 2, D_RG), 0.01),
        'rg_wi': nrm((DEPTH, 2, N_RG_BLOCKS, RG_BLOCK, RG_BLOCK), RG_BLOCK ** -0.5),
        'rg_bi': nrm((DEPTH, 2, D_RG), 0.01),
        'rg_lam': jnp.log(lam_u) - jnp.log1p(-lam_u),
        'w_c': nrm((DEPTH, D_RG, D), D_RG ** -0.5),
        'w_o': nrm((DEPTH, D, D), D ** -0.5),
        'w_gu': nrm((DEPTH, D, 2 * D_FF), D ** -0.5),
        'w_down': nrm((DEPTH, D_FF, D), D_FF ** -0.5),
        'final_g': 1.0 + nrm((D,), 0.02),
    }

def reference(x_prompt, x_sample, c, state_rglru, c_ctx, norm1_g, norm2_g, w_ada, b_ada, w_in,
              hy_conv_w, hy_conv_b, hy_f_w1, hy_f_b1, hy_f_w2, hy_f_b2, hy_f_w3, hy_f_freq, hy_bias,
              w_a, w_b, rg_conv_w, rg_conv_b, rg_wr, rg_br, rg_wi, rg_bi, rg_lam, w_c, w_o,
              w_gu, w_down, final_g):
    xp = x_prompt
    xs = x_sample
    ctx_states = []
    for l in range(DEPTH):
        lp = (norm1_g[l], norm2_g[l], w_in[l], hy_conv_w[l], hy_conv_b[l], hy_f_w1[l], hy_f_b1[l],
              hy_f_w2[l], hy_f_b2[l], hy_f_w3[l], hy_f_freq[l], hy_bias[l], w_a[l], w_b[l],
              rg_conv_w[l], rg_conv_b[l], rg_wr[l], rg_br[l], rg_wi[l], rg_bi[l], rg_lam[l],
              w_c[l], w_o[l], w_gu[l], w_down[l])
        mod_ctx = jax.nn.silu(c_ctx[None, :]) @ w_ada[l] + b_ada[l]
        mod_lat = jax.nn.silu(c) @ w_ada[l] + b_ada[l]
        xp, st = trunk_layer(xp, mod_ctx, jnp.zeros((xp.shape[0], 2, D_RG), jnp.float32), True, lp)
        ctx_states.append(st)
        xs, _ = trunk_layer(xs, mod_lat, state_rglru[:, l].astype(jnp.float32), False, lp)
    y_prompt = rmsnorm(xp, final_g)
    y_sample = rmsnorm(xs, final_g)
    new_state_rglru = jnp.stack(ctx_states, axis=1).astype(x_prompt.dtype)
    return (y_prompt, y_sample, new_state_rglru)


_drawn_inputs = setup_inputs


def setup_inputs(seed=0):
    import zlib

    import numpy as np

    out = dict(_drawn_inputs(seed))
    spreads = {}
    factors = {'state_rglru': 8.0,
     'norm1_g': 3.687,
     'norm2_g': 8.0,
     'rg_br': 29.325,
     'rg_bi': 26.166,
     'final_g': 7.554,
     'rg_conv_b': 6.258}
    for name, (base, spread) in spreads.items():
        noise = np.random.default_rng([zlib.crc32(name.encode()), seed]).standard_normal(out[name].shape)
        drawn = base * np.exp(spread * noise) if base else spread * noise
        out[name] = __import__('jax').numpy.asarray(drawn.astype(out[name].dtype))
    for name, factor in factors.items():
        out[name] = (out[name] * factor).astype(out[name].dtype)
    return out
```

```python
import math
from contextlib import ExitStack

import numpy as np

import concourse.bass as bass
from concourse import mybir

F32 = mybir.dt.float32
F32R = mybir.dt.float32r
ALU = mybir.AluOpType
ACT = mybir.ActivationFunctionType
AX_X = mybir.AxisListType.X

P = 128
D = 1024
KD = D // P
LAT, CTX = 1024, 256
T = LAT + CTX
NL, NC = LAT // P, CTX // P
NT = NL + NC
PIECES = [(0, 512, 0), (512, 1024, 0), (1024, 1280, 1)]
SEQS = [(0, LAT, 0), (LAT, T, 1)]
D_HY = 512
CH = D_HY // P
D_FF = 2816
FF = D_FF // P
D_IN = 7168
EPS = 1e-6
RG_C = 8.0
FILT_EMB, FILT_HID = 17, 64
FH = 9 + 3
PAD_LAT, PAD_CTX, PAD_T = 2, 2 + LAT + 2, 2 + LAT + 2 + CTX + 2
HALF_GROUPS = 24
ADA_FIRST = 8
FIRST_MIX = 3
MIX_BANKS = 5

V_N1, V_N2, V_FG, V_BADA = 0, KD, 2 * KD, 3 * KD
V_HY = V_BADA + 48
V_LAM = V_HY + 64
V_ALL = V_LAM + 2 * KD
R_CONV, R_CONVB, R_BR, R_BI, R_ST = 512, 516, 517, 519, 521
R_ALL = 523

TILES_L1, TILES_L2, TILES_L3 = 16, 16, 24
TILES_A, TILES_C, TILES_O = 4, 8, 8
L2_TILE0 = TILES_L1
L3_TILE0 = L2_TILE0 + TILES_L2
OUT_TILE0 = L3_TILE0 + TILES_L3
MIX_TILES = OUT_TILE0 + 2 * TILES_A + TILES_C + TILES_O
FFN_STEPS = FF // 2
FFN_TILES = 6

TWO_PI = [6.28125, 0.0019350051879882812, 3.0199e-07]
ROUND = 1.5 * 2.0 ** 23
PI_BELOW = 3.1415925
SCRATCH = [("hy_s", (16, P, T)), ("k_s", (8, P, 2 * FH * P)), ("gate_s", (24, P, T)), ("za_s", (CH, P, T)),
           ("zb_s", (CH, P, T)), ("zc_s", (KD, P, T))]
COS = [math.cos(math.pi * k / 8) for k in range(5)]
SIN = [math.sin(math.pi * k / 8) for k in range(5)]


def real_dft_even(o, z, temp, out):
    e, d = temp(0, 4), temp(4, 8)
    o.add(e, z(0, 4), z(4, 8))
    o.sub(d, z(0, 4), z(4, 8))
    o.sub(out("re4"), temp(0), temp(2))
    o.sub(out("im4"), temp(3), temp(1))
    o.add(temp(8, 10), temp(0, 2), temp(2, 4))
    o.sub(temp(10), temp(5), temp(7))
    o.add(temp(11), temp(5), temp(7))
    o.add(out("re0"), temp(8), temp(9))
    o.sub(out("re8"), temp(8), temp(9))
    o.mul_add(out("re2"), temp(10), COS[2], temp(4))
    o.mul_add(out("re6"), temp(10), -COS[2], temp(4))
    o.mul_add(out("im6"), temp(11), -COS[2], temp(6))
    o.mul_sub(out("im2"), temp(11), -COS[2], temp(6))


def real_dft_odd(o, z, temp, out):
    o.sub(temp(0, 3), z(1, 4), z(7, 4, -1))
    o.add(temp(3, 6), z(1, 4), z(7, 4, -1))
    u = [None, temp(0), temp(1), temp(2)]
    v = [None, temp(3), temp(4), temp(5)]
    o.mul_add(temp(6), u[2], COS[2], z(0))
    o.mul_add(temp(7), u[2], -COS[2], z(0))
    o.mul(temp(8), u[3], COS[3])
    o.mul(temp(9), u[3], -COS[1])
    o.mul_add(temp(8), u[1], COS[1], temp(8))
    o.mul_add(temp(9), u[1], COS[3], temp(9))
    o.add(out("re1"), temp(6), temp(8))
    o.sub(out("re7"), temp(6), temp(8))
    o.add(out("re3"), temp(7), temp(9))
    o.sub(out("re5"), temp(7), temp(9))
    o.mul_add(temp(6), v[2], SIN[2], z(4))
    o.mul_sub(temp(7), v[2], SIN[2], z(4))
    o.mul(temp(8), v[3], -SIN[3])
    o.mul(temp(9), v[3], SIN[1])
    o.mul_add(temp(8), v[1], -SIN[1], temp(8))
    o.mul_add(temp(9), v[1], -SIN[3], temp(9))
    o.sub(out("im1"), temp(8), temp(6))
    o.add(out("im7"), temp(8), temp(6))
    o.sub(out("im3"), temp(9), temp(7))
    o.add(out("im5"), temp(9), temp(7))


def real_dft_context(o, z, out):
    o.add(out("cre0"), z(0), z(1))
    o.sub(out("cre2"), z(0), z(1))
    o.mul(out("cre1"), z(0), 1.0)
    o.mul(out("cim1"), z(1), -1.0)


def inverse_latent(o, b, temp, y):
    rp, rm, ip, im = temp(0, 3), temp(3, 6), temp(6, 9), temp(9, 12)
    low_re, high_re = b("re", 1, 3), b("re", 7, 5)
    low_im, high_im = b("im", 1, 3), b("im", 7, 5)
    o.add(rp, low_re, high_re)
    o.sub(rm, low_re, high_re)
    o.add(ip, low_im, high_im)
    o.sub(im, low_im, high_im)
    o.add(temp(12), b("re0"), b("re8"))
    o.sub(temp(13), b("re0"), b("re8"))
    re4, im4 = b("re4"), b("im4")
    x, w = temp(14), temp(15)
    o.add(x, temp(12), re4)
    o.add(w, temp(0), temp(2))
    o.sub(y(4), x, temp(1))
    o.add(x, x, temp(1))
    o.sub(temp(14 + 2), temp(11), temp(9))
    o.add(y(0), x, w)
    o.add(y(4), y(4), temp(14 + 2))
    for i in (1, 2, 3):
        s = i % 2
        r = [None] + [temp((3 if s else 0) + k) for k in range(3)]
        m = [None] + [temp((6 if s else 9) + k) for k in range(3)]
        terms_x = [(r[2], math.cos(math.pi * i / 4)), (re4, math.cos(math.pi * i / 2)),
                   (m[1], -math.sin(math.pi * i / 8)), (m[3], -math.sin(3 * math.pi * i / 8))]
        terms_w = [(r[3], math.cos(3 * math.pi * i / 8)), (r[1], math.cos(math.pi * i / 8)),
                   (m[2], -math.sin(math.pi * i / 4)), (im4, -math.sin(math.pi * i / 2))]
        terms_x = [(a, c) for a, c in terms_x if abs(c) > 1e-9]
        terms_w = [(a, c) for a, c in terms_w if abs(c) > 1e-9]
        o.mul(w, *terms_w[0])
        o.mul_add(x, *terms_x[0], temp(12 + s))
        for k in (1, 2, 3):
            if k < len(terms_w):
                o.mul_add(w, *terms_w[k], w)
            if k < len(terms_x):
                o.mul_add(x, *terms_x[k], x)
        o.add(y(i), x, w)
        o.sub(y(8 - i), x, w)


def inverse_context(o, b, temp, y):
    o.add(temp(0), b("cre0"), b("cre2"))
    o.sub(temp(1), b("cre0"), b("cre2"))
    o.add(y(0), temp(0), b("cre1"))
    o.sub(y(1), temp(1), b("cim1"))


class Chain:

    def __init__(self, eng, sem):
        self.eng, self.sem, self.n = eng, sem, 0

    def __call__(self, ins):
        ins.then_inc(self.sem, 1)
        self.n += 1
        self.eng.wait_ge(self.sem, self.n)

    def add(self, ins):
        ins.then_inc(self.sem, 1)
        self.n += 1

    def settle(self):
        if self.n:
            self.eng.wait_ge(self.sem, self.n)

    def restart(self):
        self.settle()
        if self.n:
            self.eng.sem_clear(self.sem)
        self.n = 0


class Butterfly:

    def __init__(self, dve, chain):
        self.dve, self.chain = dve, chain

    def add(self, out, a, b):
        self.chain(self.dve.tensor_tensor(out, a, b, ALU.add))

    def sub(self, out, a, b):
        self.chain(self.dve.tensor_tensor(out, a, b, ALU.subtract))

    def mul(self, out, a, c):
        self.chain(self.dve.tensor_scalar(out, a, float(c), None, ALU.mult))

    def mul_add(self, out, a, c, b):
        self.chain(self.dve.scalar_tensor_tensor(out, a, float(c), b, ALU.mult, ALU.add))

    def mul_sub(self, out, a, c, b):
        self.chain(self.dve.scalar_tensor_tensor(out, a, float(c), b, ALU.mult, ALU.subtract))


class MixUnits:

    def __init__(self, base, units):
        self.base, self.units = list(base), units

    def uses(self, b):
        return len([j for j in range(self.units) if j % MIX_BANKS == b])

    def bank(self, j):
        return j % MIX_BANKS

    def nth(self, it, j):
        b = j % MIX_BANKS
        return it * self.uses(b) + (self.base[b] + j // MIX_BANKS)

    def after(self, passes):
        return [self.base[b] + passes * self.uses(b) for b in range(MIX_BANKS)]


def places(buf, width, first=0):
    def at(a, b=None, step=1):
        if b is None:
            return buf[:, first + a, :]
        if step == 1:
            return buf[:, first + a:first + b, :]
        return buf[:, first + a:first + b:-1, :]
    return at


def spectrum_places(buf):
    def at(name):
        if name.startswith("c"):
            return buf[:, 9 + int(name[3:]), :] if name[1:3] == "re" else buf[:, 19, :]
        f = int(name[2:])
        return buf[:, f if name[:2] == "re" else 11 + f, :]
    return at


def inverse_places(buf):
    def at(name, a=None, b=None):
        part = 0 if "re" in name else 1
        if a is not None:
            lo, hi = 2 * (a - 1) + part, 2 * (b - 1) + part
            return buf[:, lo:hi + 1:2, :] if a < b else buf[:, lo:hi - 1:-2, :]
        if name in ("re0", "re8", "cre0", "cre2"):
            return buf[:, 16 + ("re0", "re8", "cre0", "cre2").index(name), :]
        f = 8 if name.startswith("c") else int(name[2:])
        return buf[:, 2 * (f - 1) + part, :]
    return at


HAS_IMAG = [1 <= q <= 7 or q == 10 for q in range(FH)]
IMAG_AT = {q: (19 if q == 10 else 11 + q) for q in range(FH) if HAS_IMAG[q]}
PAIRS = [(1, 2), (3, 4), (5, 6), (7, 10)]
SINGLES = (0, 8, 9, 11)


def build_program(nc, dr):
    ctx = ExitStack()
    with ctx:
        def sem(name):
            return ctx.enter_context(nc.semaphore(name))

        def sb(stack, name, shape, dt=F32):
            return stack.enter_context(nc.sbuf_tensor(name, shape, dt))

        w_raw = [sb(ctx, f"w_raw{s}", [P, D]) for s in range(2)]
        w_hi = [sb(ctx, f"w_hi{s}", [P, D], F32R) for s in range(2)]
        w_lo = [sb(ctx, f"w_lo{s}", [P, D], F32R) for s in range(2)]
        h_hi = sb(ctx, "h_hi", [P, KD, T], F32R)
        h_lo = sb(ctx, "h_lo", [P, KD, T], F32R)
        vec = sb(ctx, "vec", [P, V_ALL])
        mod = sb(ctx, "mod", [P, 48, 2])
        norm_a = sb(ctx, "norm_a", [P, KD, 2])
        fin = sb(ctx, "fin", [P, KD, 2])
        ones = sb(ctx, "ones", [P, P])
        eps = sb(ctx, "eps", [P, 1])
        zero_col = sb(ctx, "zero_col", [P, 1])
        sp_w = sb(ctx, "sp_w", [P, 6, 2 * KD])
        sp_pos = sb(ctx, "sp_pos", [P, 2 * KD])
        sp_neg = sb(ctx, "sp_neg", [P, 2 * KD])
        cvec = sb(ctx, "cvec", [P, KD, 2])
        csilu = sb(ctx, "csilu", [P, KD, 2])
        ps = [ctx.enter_context(nc.psum_tensor(f"ps{b}", [P, 512], F32)) for b in range(8)]

        fwd_stack = ExitStack()
        fwd = sb(fwd_stack, "fwd", [P, FH, 3, P])
        h2f = sb(fwd_stack, "h2f", [FILT_HID, T])
        ada_w = [sb(fwd_stack, f"ada_w{s}", [P, KD * 256]) for s in range(2)]
        ada_row = sb(fwd_stack, "ada_row", [2, 256])
        ident = sb(fwd_stack, "ident", [P, P])

        st = ExitStack()
        x_in = sb(st, "x_in", [P, KD, T])
        sq0 = sb(st, "sq0", [P, T])
        y0 = sb(st, "y0", [P, T])
        rstd0 = sb(st, "rstd0", [P, T])
        f_vec = sb(st, "f_vec", [FILT_HID, 3])
        f_w1 = sb(st, "f_w1", [FILT_EMB, FILT_HID])
        f_w2 = sb(st, "f_w2", [FILT_HID, FILT_HID])
        feats = sb(st, "feats", [FILT_EMB, T])
        h1f = x_in[0:FILT_HID, 7, :]
        arg = x_in[0:FILT_HID, 6, :]
        turns = x_in[0:FILT_HID, 5, :]
        st.close()

        st = ExitStack()
        hin = sb(st, "hin", [P, PAD_T])
        hout = sb(st, "hout", [P, T])
        decay = sb(st, "decay", [P, NT, P])
        w3 = sb(st, "w3", [FILT_HID, 2 * P])
        taps = sb(st, "taps", [P, NT, 2, P])
        tsum = sb(st, "tsum", [P, NT, P])
        kstage = sb(st, "kstage", [P, 2 * FH, P])
        f_a = sb(st, "f_a", [P, 20, P])
        f_t = sb(st, "f_t", [P, 12, P])
        ss_k = sb(st, "ss_k", [P, 2, P])
        rs_k = sb(st, "rs_k", [P, 2, P])
        st.close()
        fwd_l1 = fwd

        st = ExitStack()
        rin = sb(st, "rin", [P, PAD_T])
        xr = sb(st, "xr", [P, T])
        rpack = [sb(st, f"rpack{s}", [P, R_ALL]) for s in range(2)]
        g_ry = sb(st, "g_ry", [P, T])
        r_b = [sb(st, f"r_b{d}", [P, T]) for d in range(2)]
        i_b = [sb(st, f"i_b{d}", [P, T]) for d in range(2)]
        a_b = [sb(st, f"a_b{d}", [P, T]) for d in range(2)]
        t_b = [sb(st, f"t_b{d}", [P, T]) for d in range(2)]
        st.close()

        st = ExitStack()
        fn_ch = sb(st, "fn_ch", [P, 4, P])
        fn_t = sb(st, "fn_t", [P, NT, 2, P])
        fn_u = sb(st, "fn_u", [P, NT, P])
        fn_a = sb(st, "fn_a", [P, 20, P])
        fn_tmp = sb(st, "fn_tmp", [P, 12, P])
        fn_c = sb(st, "fn_c", [P, NT, 2, P])
        fn_y = sb(st, "fn_y", [P, T])
        st.close()
        fwd_stack.close()

        st = ExitStack()
        fwd3 = sb(st, "fwd3", [P, FH, 3, P])
        ident3 = sb(st, "ident3", [P, P])
        inv = sb(st, "inv", [P, FH, 3, P])
        z_b = sb(st, "z_b", [P, T])
        x_b = sb(st, "x_b", [P, T])
        ztok = sb(st, "ztok", [P, FH, P])
        hy_a = sb(st, "hy_a", [P, 2 * FH, P])
        hy_z = sb(st, "hy_z", [P, 2 * FH, P])
        hy_k = sb(st, "hy_k", [P, 2 * FH, P])
        g_st = sb(st, "g_st", [P, T])
        hbias = sb(st, "hbias", [P, 2])
        st.close()

        out_stack = ExitStack()
        x1 = sb(out_stack, "x1", [P, KD, T])
        st = ExitStack()
        z2_hi = sb(st, "z2_hi", [P, 4, T], F32R)
        z2_lo = sb(st, "z2_lo", [P, 4, T], F32R)
        side = [sb(st, f"side{s}", [P, T]) for s in range(2)]
        zraw = sb(st, "zraw", [P, T])
        gated = side
        sq_o = zraw
        st.close()
        st = ExitStack()
        y_n = sb(st, "y_n", [P, T])
        rstd = sb(st, "rstd", [P, T])
        sq_n = sb(st, "sq_n", [P, T])
        st.close()
        st = ExitStack()
        wf_hi = list(w_hi) + [sb(st, f"wf_hi{s}", [P, D], F32R) for s in range(2, 6)]
        wf_lo = list(w_lo) + [sb(st, f"wf_lo{s}", [P, D], F32R) for s in range(2, 6)]
        act_hi = sb(st, "act_hi", [P, 2, T], F32R)
        act_lo = sb(st, "act_lo", [P, 2, T], F32R)
        sil = [sb(st, f"sil{s}", [P, 512]) for s in range(2)]
        a32 = [sb(st, f"a32_{s}", [P, 512]) for s in range(2)]
        st.close()
        out_stack.close()

        vec_in, consts_in, filt_in, cvec_in = sem("vec_in"), sem("consts_in"), sem("filt_in"), sem("cvec_in")
        x_loaded = [sem(f"x_loaded{k}") for k in range(KD)]
        ada_in = [sem(f"ada_in{s}") for s in range(2)]
        raw_in = [sem(f"raw_in{s}") for s in range(2)]
        hpack_in, decay_in, w3_in = sem("hpack_in"), sem("decay_in"), sem("w3_in")
        rpack_in = [sem(f"rpack_in{s}") for s in range(2)]
        fn_const_in, fn_in = sem("fn_const_in"), sem("fn_in")
        hy_const_in, v_in, xg_in, k_in, hbias_in = (sem("hy_const_in"), sem("v_in"), sem("xg_in"), sem("k_in"),
                                                    sem("hbias_in"))
        side_in = [sem(f"side_in{s}") for s in range(2)]
        zraw_in = sem("zraw_in")
        hy_stored, k_stored, zc_stored, zb_stored = (sem("hy_stored"), sem("k_stored"), sem("zc_stored"),
                                                     sem("zb_stored"))
        gate_stored, za_stored, fin_stored, y_stored = (sem("gate_stored"), sem("za_stored"), sem("fin_stored"),
                                                        sem("y_stored"))
        split_done = sem("split_done")
        proj_done = [sem(f"proj_done{b}") for b in range(3)]
        proj_free = [sem(f"proj_free{b}") for b in range(3)]
        mix_done = [sem(f"mix_done{b}") for b in range(MIX_BANKS)]
        mix_free = [sem(f"mix_free{b}") for b in range(MIX_BANKS)]
        act_step, dve_step, pool_step = sem("act_step"), sem("dve_step"), sem("pool_step")
        consts_set, csilu_set, arg_ready, sin_ready = (sem("consts_set"), sem("csilu_set"), sem("arg_ready"),
                                                       sem("sin_ready"))
        ada_row_ready, mod_ready = sem("ada_row_ready"), sem("mod_ready")
        sq_ready, ms_ready, rstd_ready, h32_ready, hi_ready, h_ready = (
            sem("sq_ready"), sem("ms_ready"), sem("rstd_ready"), sem("h32_ready"), sem("hi_ready"), sem("h_ready"))
        hin_zero, hin_ready, hy_conved = sem("hin_zero"), sem("hin_ready"), sem("hy_conved")
        taps_ready, taps_sq, ss_ready, norm_root, fa_ready, k_ready = (
            sem("taps_ready"), sem("taps_sq"), sem("ss_ready"), sem("norm_root"), sem("fa_ready"), sem("k_ready"))
        rin_ready, xr_ready, sp_ready, ri_ready, a2_ready, m2_ready, root_ready, zc_ready = (
            sem("rin_ready"), sem("xr_ready"), sem("sp_ready"), sem("ri_ready"), sem("a2_ready"),
            sem("m2_ready"), sem("root_ready"), sem("zc_ready"))
        sp_e, sp_l = sem("sp_e"), sem("sp_l")
        g_ready, rg_done = sem("g_ready"), sem("rg_done")
        fna_ready, fnc_ready, fny_ready = sem("fna_ready"), sem("fnc_ready"), sem("fny_ready")
        ztok_ready, hya_ready, z_ready, y_ready, b_ready, za_ready, gate_ready, x_used, k_used = (
            sem("ztok_ready"), sem("hya_ready"), sem("z_ready"), sem("y_ready"), sem("b_ready"), sem("za_ready"),
            sem("gate_ready"), sem("x_used"), sem("k_used"))
        zhi_ready, z_split, side_used, merged_done, mhi_ready, m_split, x1_ready, sq1_ready = (
            sem("zhi_ready"), sem("z_split"), sem("side_used"), sem("merged_done"), sem("mhi_ready"),
            sem("m_split"), sem("x1_ready"), sem("sq1_ready"))
        ms2_ready, h2_32, h2_hi, h2_ready = sem("ms2_ready"), sem("h2_32"), sem("h2_hi"), sem("h2_ready")
        f_done = [sem(f"f_done{b}") for b in range(8)]
        f_free = [sem(f"f_free{b}") for b in range(8)]
        sil_ready, a32_ready, ahi_ready, act_ready = sem("sil_ready"), sem("a32_ready"), sem("ahi_ready"), sem("act_ready")
        sq3_ready, ms3_ready, y_out = sem("sq3_ready"), sem("ms3_ready"), sem("y_out")

        u_setup = MixUnits([0] * MIX_BANKS, 6 + 2 * ADA_FIRST)
        u1 = MixUnits(u_setup.after(1), 5 + 1 + 3 + 4 + 3)
        u2 = MixUnits(u1.after(8), 12)
        u_fn = MixUnits(u2.after(8), 5 + 3)
        u3 = MixUnits(u_fn.after(CH), 2 * (3 + 6 + 5))
        u_out = MixUnits(u3.after(CH), 3)
        u_end = MixUnits(u_out.after(1), 3)

        def mix(b):
            return ps[FIRST_MIX + b]

        block = ctx.enter_context(nc.Block())
        stream = dr["weights"]

        @block.sync
        def _(sp):
            def load_tile(t, slot):
                sp.dma_start(w_raw[slot][:], stream[t]).then_inc(raw_in[slot], 16)

            def load_ahead(t, slot):
                sp.wait_ge(split_done, t + 1)
                load_tile(t + 2, slot)

            sp.dma_start(cvec[:], dr["cvec"]).then_inc(cvec_in, 16)
            sp.dma_start(feats[:], dr["feats"]).then_inc(filt_in, 16)
            sp.dma_start(f_w1[:], dr["f_w1"]).then_inc(filt_in, 16)
            sp.dma_start(f_w2[:], dr["f_w2"]).then_inc(filt_in, 16)
            sp.dma_start(f_vec[:], dr["f_vec"]).then_inc(filt_in, 16)
            sp.dma_start(ident[:], dr["ident"]).then_inc(consts_in, 16)
            sp.dma_start(vec[:], dr["vec"]).then_inc(vec_in, 16)
            for g in range(2):
                sp.dma_start(ada_w[g][:], dr["w_ada"][g]).then_inc(ada_in[g], 16)
            for k in range(5):
                sp.dma_start(x_in[:, k, :], dr["x"][k]).then_inc(x_loaded[k], 16)
            sp.wait_ge(sin_ready, 6)
            for k in range(5, KD):
                sp.dma_start(x_in[:, k, :], dr["x"][k]).then_inc(x_loaded[k], 16)
            for g in range(2, ADA_FIRST):
                sp.wait_ge(ada_row_ready, g - 1)
                sp.dma_start(ada_w[g % 2][:], dr["w_ada"][g]).then_inc(ada_in[g % 2], 16)
            sp.dma_start(fwd[:], dr["fwd"]).then_inc(consts_in, 16)
            load_tile(0, 0)
            load_tile(1, 1)
            sp.wait_ge(h_ready, KD)
            with sp.Fori(0, 8) as i:
                sp.wait_ge(taps_ready, i)
                sp.dma_start(decay[:], dr["decay"][i]).then_inc(decay_in, 16)
                sp.dma_start(w3[:], dr["w3"][i]).then_inc(w3_in, 16)
                load_ahead(2 * i, 0)
                for g in range(2):
                    sp.wait_ge(ada_row_ready, 2 * i + (ADA_FIRST - 1 + g))
                    sp.dma_start(ada_w[g][:], dr["w_ada"][2 * i + (ADA_FIRST + g)]).then_inc(ada_in[g], 16)
                sp.wait_ge(hy_conved, 2 * i + 1)
                sp.dma_start(dr["hy_s"][2 * i], hout[:]).then_inc(hy_stored, 16)
                load_ahead(2 * i + 1, 1)
                sp.wait_ge(k_ready, i + 1)
                sp.dma_start(dr["k_s"][i], kstage[:]).then_inc(k_stored, 16)
                sp.wait_ge(hy_conved, 2 * i + 2)
                sp.dma_start(dr["hy_s"][2 * i + 1], hout[:]).then_inc(hy_stored, 16)
            sp.wait_ge(hy_stored, 16 * TILES_L1)
            sp.wait_ge(k_stored, 16 * 8)

            sp.dma_start(rpack[0][:], dr["rpack"][0]).then_inc(rpack_in[0], 16)

            def l2_pass(n, slot, last):
                if not last:
                    sp.wait_ge(zc_ready, n)
                    sp.dma_start(rpack[1 - slot][:], dr["rpack"][n + 1]).then_inc(rpack_in[1 - slot], 16)
                load_ahead(L2_TILE0 + 2 * n, 0)
                load_ahead(L2_TILE0 + 1 + 2 * n, 1)
                sp.wait_ge(zc_ready, n + 1)
                sp.dma_start(dr["zc_s"][n], r_b[0][:]).then_inc(zc_stored, 16)

            with sp.Fori(0, 3) as m:
                l2_pass(2 * m, 0, False)
                l2_pass(2 * m + 1, 1, False)
            l2_pass(6, 0, False)
            l2_pass(7, 1, True)
            sp.wait_ge(zc_stored, 16 * KD)
            sp.dma_start(dr["state_out"], fin[:]).then_inc(fin_stored, 16)

            sp.dma_start(fn_ch[:], dr["fn_ch"]).then_inc(fn_const_in, 16)
            sp.dma_start(fn_t[:], dr["fn_t"]).then_inc(fn_const_in, 16)
            with sp.Fori(0, CH) as c:
                sp.wait_ge(fna_ready, c)
                sp.dma_start(fn_u[:], dr["hy_s"][c + 12]).then_inc(fn_in, 16)
                sp.wait_ge(mix_free[u_fn.bank(7)], u_fn.nth(c, 7) + 1)
                sp.dma_start(dr["zb_s"][c], fn_y[:]).then_inc(zb_stored, 16)
            sp.wait_ge(zb_stored, 16 * CH)

            sp.dma_start(fwd3[:], dr["fwd"]).then_inc(hy_const_in, 16)
            sp.dma_start(ident3[:], dr["ident"]).then_inc(hy_const_in, 16)
            sp.dma_start(inv[:], dr["inv"]).then_inc(hy_const_in, 16)
            with sp.Fori(0, CH) as c:
                t = 6 * c + L3_TILE0
                sp.wait_ge(za_stored, 16 * c)
                sp.dma_start(z_b[:], dr["hy_s"][c]).then_inc(v_in, 16)
                sp.dma_start(hbias[:], dr["hbias"][c]).then_inc(hbias_in, 16)
                for order in range(2):
                    sp.wait_ge(z_ready, 2 * c + order)
                    sp.dma_start(x_b[:], dr["hy_s"][c + (4 + 4 * order)]).then_inc(xg_in, 16)
                    sp.dma_start(hy_k[:], dr["k_s"][c + 4 * order]).then_inc(k_in, 16)
                    for g in range(3):
                        j = 3 * order + g
                        load_ahead(t + j, j % 2)
                        for b in range(3):
                            sp.wait_ge(proj_free[b], t + (j + 2))
                        sp.dma_start(dr["gate_s"][6 * c + j], g_st[:]).then_inc(gate_stored, 16)
                sp.wait_ge(z_ready, 2 * c + 2)
                sp.dma_start(dr["za_s"][c], z_b[:]).then_inc(za_stored, 16)
            sp.wait_ge(za_stored, 16 * CH)
            sp.wait_ge(gate_stored, 16 * TILES_L3)

            def load_side(n, src):
                if 2 <= n < 10 or n >= 26:
                    for b in range(3):
                        sp.wait_ge(proj_free[b], OUT_TILE0 + n)
                elif n >= 10:
                    sp.wait_ge(side_used, n - 9)
                sp.dma_start(side[n % 2][:], src).then_inc(side_in[n % 2], 16)

            def load_z(n, src):
                if n:
                    sp.wait_ge(z_split, n)
                sp.dma_start(zraw[:], src).then_inc(zraw_in, 16)

            z_src = [dr["zb_s"][c] for c in range(4)] + [dr["zc_s"][n] for n in range(8)] + \
                    [dr["za_s"][c] for c in range(4)]
            gate_src = [dr["gate_s"][8 + m] for m in range(8)] + [dr["gate_s"][16 + m] for m in range(8)] + \
                       [dr["gate_s"][m] for m in range(8)] + [dr["x"][m] for m in range(8)]
            for n in range(4):
                load_z(n, z_src[n])
            for n in range(4, 12):
                load_z(n, z_src[n])
                load_side(n - 4, gate_src[n - 4])
                if n % 2:
                    load_ahead(OUT_TILE0 + (n - 5) // 2, (n - 5) // 2 % 2)
            for n in range(12, 16):
                load_z(n, z_src[n])
            for n in range(8):
                load_side(8 + n, gate_src[8 + n])
                load_ahead(OUT_TILE0 + 4 + n, n % 2)
            for n in range(8):
                load_side(16 + n, gate_src[16 + n])
                if n % 2:
                    load_ahead(OUT_TILE0 + 12 + n // 2, n // 2 % 2)
            for n in range(8):
                load_side(24 + n, gate_src[24 + n])
                load_ahead(OUT_TILE0 + 16 + n, n % 2)
            with sp.Fori(0, FFN_STEPS * FFN_TILES // 2 - 1) as m:
                load_ahead(2 * m + MIX_TILES, 0)
                load_ahead(2 * m + (MIX_TILES + 1), 1)
            for k in range(KD):
                sp.wait_ge(y_out, k + 1)
                sp.dma_start(dr["y"][k], x1[:, k, :]).then_inc(y_stored, 16)
            sp.wait_ge(fin_stored, 16)
            sp.wait_ge(y_stored, 16 * KD)

        @block.gpsimd
        def _(pool):
            nc.gpsimd.memset(ones[:], 1.0).then_inc(consts_set, 1)
            nc.gpsimd.memset(eps[:], EPS).then_inc(consts_set, 1)
            nc.gpsimd.memset(zero_col[:], 0.0).then_inc(consts_set, 1)
            pool.wait_ge(consts_set, 3)

            def split(t, slot, hi, lo):
                pool.wait_ge(raw_in[slot % 2], t * 8 + (16 - 8 * (slot % 2)))
                nc.gpsimd.tensor_tensor(hi[:], w_raw[slot % 2][:], zero_col[:].to_broadcast([P, D]),
                                        ALU.add).then_inc(pool_step, 1)
                pool.wait_ge(pool_step, t + 1)
                nc.gpsimd.tensor_tensor(lo[:], w_raw[slot % 2][:], hi[:].bitcast(F32),
                                        ALU.subtract).then_inc(split_done, 1)

            with pool.Fori(0, OUT_TILE0 // 2 + 1) as m:
                for s in range(2):
                    pool.wait_ge(proj_done[2], 2 * m + s)
                    split(2 * m + s, s, w_hi[s], w_lo[s])
            chunks = [2] * TILES_A + [1] * TILES_C + [2] * TILES_A + [1] * TILES_O
            for n in range(2, len(chunks)):
                t = OUT_TILE0 + n
                pool.wait_ge(proj_done[2], OUT_TILE0 + 1 + sum(chunks[:n - 1]))
                split(t, n % 2, w_hi[n % 2], w_lo[n % 2])
            pool.wait_ge(h2_ready, KD)
            for q in range(FFN_TILES):
                split(MIX_TILES + q, q, wf_hi[q], wf_lo[q])
            with pool.Fori(1, FFN_STEPS) as s:
                frees = [(f_done[0], 3 * s - 1), (f_done[1], 3 * s - 1), (f_done[2], 3 * s), (f_done[3], 3 * s),
                         (f_done[7], 6 * s), (f_done[7], 6 * s)]
                for q in range(FFN_TILES):
                    pool.wait_ge(*frees[q])
                    split(FFN_TILES * s + (MIX_TILES + q), q, wf_hi[q], wf_lo[q])

        @block.tensor
        def _(pe):
            mm = nc.tensor.matmul

            def split_product(out, w_pair, x_pair, first, last):
                mm(out, w_pair[0], x_pair[0], start=first, stop=False)
                mm(out, w_pair[0], x_pair[1], start=False, stop=False)
                return mm(out, w_pair[1], x_pair[0], start=False, stop=last)

            def projection(use, ws, xs, cols):
                for b, (a, e, _) in enumerate(PIECES):
                    pe.wait_ge(proj_free[b], use)
                    for k, (w, x) in enumerate(zip(ws, xs)):
                        ins = split_product(ps[b][:, 0:e - a], [w[0][:, cols[k]], w[1][:, cols[k]]],
                                            [x[0][:, a:e], x[1][:, a:e]], k == 0, k == len(ws) - 1)
                    ins.then_inc(proj_done[b], 1)

            h_pairs = [(h_hi[:, k, :], h_lo[:, k, :]) for k in range(KD)]

            def projection_tile(t, slot):
                pe.wait_ge(split_done, t + 1)
                projection(t + 1, [(w_hi[slot], w_lo[slot])] * KD, h_pairs,
                           [slice(k * P, k * P + P) for k in range(KD)])

            def mix_unit(units, it, j):
                b = units.bank(j)
                pe.wait_ge(mix_free[b], units.nth(it, j))
                return mix(b), mix_done[b]

            def ada_row_unit(units, it, j, slot, loads):
                out, done = mix_unit(units, it, j)
                pe.wait_ge(ada_in[slot], loads)
                for k in range(KD):
                    ins = mm(out[0:2, 0:256], csilu[:, k, :], ada_w[slot][:, k * 256:(k + 1) * 256],
                             start=k == 0, stop=k == KD - 1)
                ins.then_inc(done, 1)

            def ada_turn_unit(units, it, j, rows):
                out, done = mix_unit(units, it, j)
                pe.wait_ge(ada_row_ready, rows)
                for q in range(2):
                    ins = mm(out[:, 2 * q:2 * q + 2], ada_row[0:2, q * P:(q + 1) * P], ident[0:2, 0:2],
                             start=True, stop=True)
                ins.then_inc(done, 1)

            pe.wait_ge(filt_in, 64)
            for j, (a, e, _) in enumerate(PIECES):
                out, done = mix_unit(u_setup, 0, j)
                mm(out[0:FILT_HID, 0:e - a], f_w1[:, :], feats[:, a:e], start=True, stop=True).then_inc(done, 1)
            for j, (a, e, _) in enumerate(PIECES):
                out, done = mix_unit(u_setup, 0, 3 + j)
                pe.wait_ge(sin_ready, j + 1)
                mm(out[0:FILT_HID, 0:e - a], f_w2[:, :], h1f[:, a:e], start=True, stop=True).then_inc(done, 1)
            pe.wait_ge(csilu_set, 1)
            pe.wait_ge(consts_in, 16)
            for g in range(ADA_FIRST):
                ada_row_unit(u_setup, 0, 6 + 2 * g, g % 2, 16 * (g // 2 + 1))
                ada_turn_unit(u_setup, 0, 7 + 2 * g, g + 1)
            pe.wait_ge(consts_set, 3)
            for k in range(KD):
                pe.wait_ge(sq_ready, k + 1)
                sq = (sq0, y0)[k % 2]
                for b, (a, e, _) in enumerate(PIECES):
                    ins = mm(ps[b][:, 0:e - a], ones[:], sq[:, a:e], start=k == 0, stop=k == KD - 1,
                             skip_group_check=True)
                    if k == KD - 1:
                        ins.then_inc(proj_done[b], 1)
                if k < KD - 1:
                    ins.then_inc(ms_ready, 1)

            def fwd_unit(units, it, j, block_j, imag, a_buf, mats):
                out, done = mix_unit(units, it, j)
                for s in range(4):
                    q = 4 * block_j + s
                    o = out[:, s * P:(s + 1) * P]
                    re, im = a_buf[:, q, :], a_buf[:, IMAG_AT[q], :] if HAS_IMAG[q] else None
                    terms = [(0, re), (1, im)] if not imag else [(2, re), (0, im)]
                    terms = [x for x in terms if x[1] is not None]
                    for n, (m, part) in enumerate(terms):
                        ins = mm(o, mats[:, q, m, :], part, start=n == 0, stop=n == len(terms) - 1)
                ins.then_inc(done, 1)

            pe.wait_ge(h_ready, KD)
            pe.wait_ge(consts_in, 32)
            with pe.Fori(0, 8) as i:
                pe.wait_ge(w3_in, 16 * i + 16)
                for j in range(5):
                    out, done = mix_unit(u1, i, j)
                    for s in range(2):
                        tile = 2 * j + s
                        ins = mm(out[:, s * 256:(s + 1) * 256], h2f[:, tile * P:(tile + 1) * P], w3[:, :],
                                 start=True, stop=True)
                    ins.then_inc(done, 1)
                projection_tile(2 * i, 0)
                out, done = mix_unit(u1, i, 5)
                pe.wait_ge(ss_ready, i + 1)
                mm(out[:, 0:2 * P], ones[:], ss_k[:, :, :], start=True, stop=True).then_inc(done, 1)
                pe.wait_ge(fa_ready, 2 * i + 1)
                for j in range(3):
                    fwd_unit(u1, i, 6 + j, j, False, f_a, fwd_l1)
                for g in range(2):
                    ada_row_unit(u1, i, 9 + 2 * g, g, 16 * i + 16 * (ADA_FIRST // 2 + 1))
                    ada_turn_unit(u1, i, 10 + 2 * g, 2 * i + (ADA_FIRST + g + 1))
                projection_tile(2 * i + 1, 1)
                pe.wait_ge(fa_ready, 2 * i + 2)
                for j in range(3):
                    fwd_unit(u1, i, 13 + j, j, True, f_a, fwd_l1)

            with pe.Fori(0, KD // 2) as m:
                for s in range(2):
                    n = 2 * m + s
                    projection_tile(2 * n + L2_TILE0, 0)
                    projection_tile(2 * n + (L2_TILE0 + 1), 1)
                    pe.wait_ge(xr_ready, n + 1)
                    pe.wait_ge(rpack_in[s], 16 * m + 16)
                    for j in range(12):
                        out, done = mix_unit(u2, n, j)
                        a, e, _ = PIECES[j % 3]
                        mm(out[:, 0:e - a], rpack[s][:, (j // 3) * P:(j // 3 + 1) * P], xr[:, a:e],
                           start=True, stop=True).then_inc(done, 1)

            pe.wait_ge(fn_const_in, 32)
            with pe.Fori(0, CH) as c:
                pe.wait_ge(fna_ready, c + 1)
                for j in range(5):
                    out, done = mix_unit(u_fn, c, j)
                    for s in range(2):
                        f = 2 * j + s
                        o = out[:, s * 256:(s + 1) * 256]
                        if f >= NL:
                            terms = [(9 + f - NL, 1)]
                        else:
                            g = f if f <= 4 else 8 - f
                            terms = [(2 * g, 1)]
                            if 1 <= g <= 3:
                                terms.append((11 + 2 * g, 0 if f <= 4 else 2))
                        for n, (place, m) in enumerate(terms):
                            ins = mm(o, fn_a[:, place, :], fn_ch[:, m:m + 2, :], start=n == 0,
                                     stop=n == len(terms) - 1)
                    ins.then_inc(done, 1)
                for j in range(5):
                    pe.wait_ge(mix_free[u_fn.bank(j)], u_fn.nth(c, j) + 1)
                for j in range(3):
                    out, done = mix_unit(u_fn, c, 5 + j)
                    for f in range(4 * j, min(4 * j + 4, NT)):
                        for part in range(2):
                            ins = mm(out[:, (f % 4) * P:(f % 4 + 1) * P], fn_c[:, f, part, :],
                                     fn_t[:, f, part, :], start=part == 0, stop=part == 1)
                    ins.then_inc(done, 1)

            pe.wait_ge(hy_const_in, 48)
            with pe.Fori(0, CH) as c:
                for order in range(2):
                    j0 = 14 * order
                    t = 6 * c + (L3_TILE0 + 3 * order)
                    slot = 3 * order % 2
                    if order == 0:
                        pe.wait_ge(v_in, 16 * c + 16)
                    else:
                        pe.wait_ge(z_ready, 2 * c + 1)
                    for j in range(3):
                        out, done = mix_unit(u3, c, j0 + j)
                        for tile in range(4 * j, min(4 * j + 4, NT)):
                            ins = nc.tensor.transpose(out[:, (tile % 4) * P:(tile % 4 + 1) * P],
                                                      z_b[:, tile * P:(tile + 1) * P], ident3[:, :])
                        ins.then_inc(done, 1)
                    projection_tile(t, slot)
                    pe.wait_ge(hya_ready, 2 * c + (order + 1))
                    for j in range(6):
                        fwd_unit(u3, c, j0 + 3 + j, j % 3, j >= 3, hy_a, fwd3)
                    projection_tile(t + 1, 1 - slot)
                    pe.wait_ge(y_ready, 2 * c + (order + 1))
                    for j in range(5):
                        out, done = mix_unit(u3, c, j0 + 9 + j)
                        if j < 4:
                            for s, q in enumerate(PAIRS[j]):
                                o = out[:, s * 256:(s + 1) * 256]
                                mm(o, hy_a[:, q, :], inv[:, q, 1:3, :], start=True, stop=False)
                                ins = mm(o, hy_a[:, FH + q, :], inv[:, q, 0:2, :], start=False, stop=True)
                        else:
                            for s, q in enumerate(SINGLES):
                                o = out[:, s * P:(s + 1) * P]
                                mm(o, hy_a[:, q, :], inv[:, q, 1, :], start=True, stop=False)
                                ins = mm(o, hy_a[:, FH + q, :], inv[:, q, 0, :], start=False, stop=True)
                        ins.then_inc(done, 1)
                    projection_tile(t + 2, slot)

            low = [(h_hi[:, k, :], h_lo[:, k, :]) for k in range(4)]
            high = [(h_hi[:, 4 + k, :], h_lo[:, 4 + k, :]) for k in range(4)] + \
                   [(z2_hi[:, k, :], z2_lo[:, k, :]) for k in range(4)]
            use0 = OUT_TILE0 + 1

            def narrow_tiles(first_tile, first_use):
                with pe.Fori(0, 2) as m:
                    for s in range(2):
                        pe.wait_ge(split_done, 2 * m + (first_tile + s + 1))
                        for q in range(2):
                            projection(4 * m + (first_use + 2 * s + q), [(w_hi[s], w_lo[s])] * 4, low,
                                       [slice((4 * q + k) * P, (4 * q + k + 1) * P) for k in range(4)])

            def wide_tile(t, use, slot):
                pe.wait_ge(split_done, t + 1)
                projection(use, [(w_hi[slot], w_lo[slot])] * KD, high,
                           [slice(k * P, k * P + P) for k in range(KD)])

            pe.wait_ge(z_split, 4)
            narrow_tiles(OUT_TILE0, use0)
            pe.wait_ge(z_split, 12)
            with pe.Fori(0, 4) as m:
                for s in range(2):
                    wide_tile(2 * m + (OUT_TILE0 + 4 + s), 2 * m + (use0 + 8 + s), s)
            pe.wait_ge(z_split, 16)
            narrow_tiles(OUT_TILE0 + 12, use0 + 16)
            pe.wait_ge(m_split, KD)

            def sums2(k):
                pe.wait_ge(sq1_ready, k + 1)
                for b, (a, e, _) in enumerate(PIECES):
                    if k == 0:
                        pe.wait_ge(mix_free[b], u_out.nth(0, b))
                    ins = mm(mix(b)[:, 0:e - a], ones[:], sq_o[:, a:e], start=k == 0, stop=k == KD - 1,
                             skip_group_check=True)
                    if k == KD - 1:
                        ins.then_inc(mix_done[b], 1)
                if k < KD - 1:
                    ins.then_inc(ms2_ready, 1)

            for m in range(KD):
                wide_tile(OUT_TILE0 + 16 + m, use0 + 24 + m, m % 2)
                if m:
                    sums2(m - 1)
            sums2(KD - 1)

            pe.wait_ge(h2_ready, KD)
            for b in range(3):
                pe.wait_ge(proj_free[b], use0 + 32)
            for b in range(MIX_BANKS):
                pe.wait_ge(mix_free[b], u_out.after(1)[b])
            with pe.Fori(0, FFN_STEPS) as s:
                for j in range(2):
                    for p, (a, e, _) in enumerate(PIECES):
                        for up in range(2):
                            q = 2 * j + up
                            if p == 0:
                                pe.wait_ge(split_done, FFN_TILES * s + (MIX_TILES + q + 1))
                            n = 2 * (3 * j + p) + up
                            pe.wait_ge(f_free[n % 4], 3 * s + n // 4)
                            for k in range(KD):
                                ins = split_product(ps[n % 4][:, 0:e - a],
                                                    [wf_hi[q][:, k * P:(k + 1) * P], wf_lo[q][:, k * P:(k + 1) * P]],
                                                    [h_hi[:, k, a:e], h_lo[:, k, a:e]], k == 0, k == KD - 1)
                            ins.then_inc(f_done[n % 4], 1)
                pe.wait_ge(split_done, FFN_TILES * s + (MIX_TILES + FFN_TILES))
                for p, (a, e, _) in enumerate(PIECES):
                    pe.wait_ge(act_ready, 6 * s + (3 + p + 1))
                    for m in range(KD):
                        v = KD * p + m
                        b = 4 + v % 4
                        pe.wait_ge(f_free[b], 6 * s + v // 4)
                        for j in range(2):
                            ins = split_product(ps[b][:, 0:e - a],
                                                [wf_hi[4 + j][:, m * P:(m + 1) * P], wf_lo[4 + j][:, m * P:(m + 1) * P]],
                                                [act_hi[:, j, a:e], act_lo[:, j, a:e]], j == 0, j == 1)
                        ins.then_inc(f_done[b], 1)
            for b in range(3):
                pe.wait_ge(f_free[b], 3 * FFN_STEPS)
            for k in range(KD):
                pe.wait_ge(sq3_ready, k + 1)
                for b, (a, e, _) in enumerate(PIECES):
                    ins = mm(ps[b][:, 0:e - a], ones[:], (sq_n, y_n)[k % 2][:, a:e], start=k == 0,
                             stop=k == KD - 1, skip_group_check=True)
                ins.then_inc(ms3_ready, 1)

        @block.scalar
        def _(act):
            own = Chain(act, act_step)
            fn = nc.scalar.activation

            def take_mix(units, it, j):
                b = units.bank(j)
                act.wait_ge(mix_done[b], units.nth(it, j) + 1)
                return mix(b), mix_free[b]

            def mix_taken(units, it, j):
                act.wait_ge(mix_free[units.bank(j)], units.nth(it, j) + 1)

            def take_proj(use, b):
                act.wait_ge(proj_done[b], use + 1)
                return ps[b], proj_free[b]

            act.wait_ge(cvec_in, 16)
            fn(csilu[:], cvec[:], ACT.Silu).then_inc(csilu_set, 1)
            for j in range(6):
                a, e, _ = PIECES[j % 3]
                act.wait_ge(arg_ready, j + 1)
                fn((h1f if j < 3 else h2f[:, :])[:, a:e], arg[:, a:e], ACT.Sin).then_inc(sin_ready, 1)
            act.wait_ge(sp_ready, 1)
            fn(sp_w[:, 2, :], sp_w[:, 1, :], ACT.Exp).then_inc(sp_e, 1)
            act.wait_ge(sp_ready, 2)
            fn(sp_w[:, 4, :], sp_w[:, 3, :], ACT.Ln).then_inc(sp_l, 1)
            for g in range(ADA_FIRST):
                src, free = take_mix(u_setup, 0, 6 + 2 * g)
                if g:
                    act.wait_ge(mod_ready, g)
                fn(ada_row[0:2, :], src[0:2, 0:256], ACT.Copy).then_inc(own.sem, 1)
                own.n += 1
                own.settle()
                act.sem_inc(free, 1)
                act.sem_inc(ada_row_ready, 1)
            for k in range(KD):
                act.wait_ge(x_loaded[k], 16)
                if k >= 2:
                    act.wait_ge(ms_ready, k - 1)
                fn((sq0, y0)[k % 2][:], x_in[:, k, :], ACT.Square).then_inc(sq_ready, 1)
            act.wait_ge(consts_set, 3)
            for b, (a, e, _) in enumerate(PIECES):
                src, free = take_proj(0, b)
                fn(rstd0[:, a:e], src[:, 0:e - a], ACT.Sqrt, bias=eps[:, 0:1], scale=1.0 / D).then_inc(free, 1)
            for k in range(KD):
                act.wait_ge(h32_ready, k + 1)
                fn(h_hi[:, k, :], x_in[:, k, :], ACT.Copy).then_inc(hi_ready, 1)
            own.restart()

            act.wait_ge(hin_zero, 1)

            def into_padded(use, dst):
                for b, (a, e, seq) in enumerate(PIECES):
                    src, free = take_proj(use, b)
                    at = PAD_CTX if seq else PAD_LAT + a
                    fn(dst[:, at:at + e - a], src[:, 0:e - a], ACT.Copy).then_inc(free, 1)

            with act.Fori(0, 8) as i:
                act.wait_ge(taps_ready, i + 1)
                act.wait_ge(k_stored, 16 * i)
                fn(kstage[:, 0:2 * NT, :], taps[:, :, :, :].rearrange("p n d c -> p (n d) c"),
                   ACT.Square).then_inc(taps_sq, 1)
                act.wait_ge(hy_conved, 2 * i)
                into_padded(2 * i + 1, hin)
                src, free = take_mix(u1, i, 5)
                fn(rs_k[:, :, :], src[:, 0:2 * P].rearrange("p (s c) -> p s c", s=2), ACT.Sqrt,
                   bias=eps[:, 0:1]).then_inc(free, 1)
                for g in range(2):
                    src, free = take_mix(u1, i, 9 + 2 * g)
                    act.wait_ge(mod_ready, 2 * i + (ADA_FIRST + g))
                    own(fn(ada_row[0:2, :], src[0:2, 0:256], ACT.Copy))
                    act.sem_inc(free, 1)
                    act.sem_inc(ada_row_ready, 1)
                act.wait_ge(hy_conved, 2 * i + 1)
                into_padded(2 * i + 2, hin)
                own.restart()

            act.wait_ge(hin_zero, 2)
            with act.Fori(0, KD // 2) as m:
                for s in range(2):
                    n = 2 * m + s
                    act.wait_ge(xr_ready, n)
                    into_padded(2 * n + (L2_TILE0 + 1), rin)
                    act.wait_ge(zc_ready, n)
                    for b, (a, e, _) in enumerate(PIECES):
                        src, free = take_proj(2 * n + (L2_TILE0 + 2), b)
                        fn(g_ry[:, a:e], src[:, 0:e - a], ACT.Gelu_apprx_tanh).then_inc(free, 1)
                    act.wait_ge(zc_stored, 16 * n)
                    for j in range(12):
                        d, which = j // 6, j // 3 % 2
                        a, e, _ = PIECES[j % 3]
                        src, free = take_mix(u2, n, j)
                        bias = (R_BR, R_BI)[which] + d
                        fn((r_b, i_b)[which][d][:, a:e], src[:, 0:e - a], ACT.Sigmoid,
                           bias=rpack[s][:, bias:bias + 1]).then_inc(free, 1)
                    for d in range(2):
                        for j in range(3):
                            mix_taken(u2, n, 6 * d + j)
                        own.add(fn(a_b[d][:], r_b[d][:], ACT.Exp, scale=sp_neg[:, bass.ds(2 * n + d, 1)]))
                        own.add(fn(t_b[d][:], r_b[d][:], ACT.Tanh, scale=sp_pos[:, bass.ds(2 * n + d, 1)]))
                        own.settle()
                        fn(r_b[d][:], a_b[d][:], ACT.Square).then_inc(a2_ready, 1)
                    for d in range(2):
                        act.wait_ge(m2_ready, 2 * n + (d + 1))
                        fn(r_b[d][:], r_b[d][:], ACT.Sqrt).then_inc(root_ready, 1)
                    own.restart()

            with act.Fori(0, CH) as c:
                for j in range(5):
                    src, free = take_mix(u_fn, c, j)
                    fn(fn_c[:, 2 * j:2 * j + 2, :, :].rearrange("p a b c -> p (a b c)"), src[:, 0:512],
                       ACT.Copy).then_inc(free, 1)
                act.wait_ge(zb_stored, 16 * c)
                for j in range(3):
                    src, free = take_mix(u_fn, c, 5 + j)
                    if j < 2:
                        dst = fn_y[:, 0:LAT].rearrange("p (f k) -> p k f", k=NL)[:, 4 * j:4 * j + 4, :]
                        src = src[:, 0:512].rearrange("p (k f) -> p k f", k=4)
                    else:
                        for q in range(2):
                            act.wait_ge(mix_free[u_fn.bank(5 + q)], u_fn.nth(c, 5 + q) + 1)
                        dst = fn_y[:, LAT:T].rearrange("p (f k) -> p k f", k=NC)
                        src = src[:, 0:256].rearrange("p (k f) -> p k f", k=2)
                    fn(dst, src, ACT.Copy).then_inc(free, 1)

            with act.Fori(0, CH) as c:
                for order in range(2):
                    j0 = 14 * order

                    def gate(g):
                        n = 3 * order + g
                        act.wait_ge(gate_stored, 96 * c + 16 * n)
                        for b, (a, e, _) in enumerate(PIECES):
                            src, free = take_proj(6 * c + (L3_TILE0 + 1 + n), b)
                            fn(g_st[:, a:e], src[:, 0:e - a], ACT.Sigmoid).then_inc(free, 1)

                    for j in range(3):
                        src, free = take_mix(u3, c, j0 + j)
                        w = min(4, NT - 4 * j)
                        fn(ztok[:, 4 * j:4 * j + w, :].rearrange("p a c -> p (a c)"), src[:, 0:w * P],
                           ACT.Copy).then_inc(free, 1)
                    gate(0)
                    for j in range(6):
                        src, free = take_mix(u3, c, j0 + 3 + j)
                        fn(hy_z[:, 4 * j:4 * j + 4, :].rearrange("p a c -> p (a c)"), src[:],
                           ACT.Copy).then_inc(free, 1)
                    gate(1)
                    for j in range(5):
                        src, free = take_mix(u3, c, j0 + 9 + j)
                        fn(hy_z[:, 4 * j:4 * j + 4, :].rearrange("p a c -> p (a c)"), src[:],
                           ACT.Copy).then_inc(free, 1)
                    gate(2)

            use0 = OUT_TILE0 + 1
            for n in range(16):
                act.wait_ge(zraw_in, 16 * (n + 1))
                if n == 12:
                    for b in range(3):
                        act.wait_ge(proj_done[b], use0 + 8)
                dst = h_hi[:, n % 12, :] if n % 12 < 8 else z2_hi[:, n - 8, :]
                fn(dst, zraw[:], ACT.Copy).then_inc(zhi_ready, 1)
            for b in range(3):
                act.wait_ge(proj_done[b], use0 + 16)
            for m in range(KD):
                act.wait_ge(side_used, KD + m + 1)
                fn(h_hi[:, 4 + m, :] if m < 4 else z2_hi[:, m - 4, :], x1[:, m, :],
                   ACT.Copy).then_inc(mhi_ready, 1)
            for k in range(KD):
                for b in range(3):
                    act.wait_ge(proj_free[b], use0 + 24 + k + 1)
                if k:
                    act.wait_ge(ms2_ready, k)
                fn(sq_o[:], x1[:, k, :], ACT.Square).then_inc(sq1_ready, 1)
            for b, (a, e, _) in enumerate(PIECES):
                src, free = take_mix(u_out, 0, b)
                fn(rstd[:, a:e], src[:, 0:e - a], ACT.Sqrt, bias=eps[:, 0:1], scale=1.0 / D).then_inc(free, 1)
            for k in range(KD):
                act.wait_ge(h2_32, k + 1)
                fn(h_hi[:, k, :], (y_n, sq_n)[k % 2][:], ACT.Copy).then_inc(h2_hi, 1)

            def up_bank(n):
                return (2 * n + 1) % 4, (2 * n + 1) // 4

            def ffn_step(s, first):
                for n in range(7):
                    if n < 6:
                        p = n % 3
                        a, e, _ = PIECES[p]
                        b = 2 * n % 4
                        act.wait_ge(f_done[b], 3 * s + (2 * n // 4 + 1))
                        if n >= 2 or not first:
                            pb, puse = up_bank((n - 2) % 6)
                            act.wait_ge(f_free[pb], 3 * s + (puse + 1 - (3 if n < 2 else 0)))
                        fn(sil[n % 2][:, 0:e - a], ps[b][:, 0:e - a], ACT.Silu).then_inc(f_free[b], 1)
                    if n >= 1:
                        q = n - 1
                        pb, puse = up_bank(q)
                        act.wait_ge(f_free[pb], 3 * s + (puse + 1))
                        a, e, _ = PIECES[q % 3]
                        if not first:
                            v = KD * (q % 3) + KD - 1
                            act.wait_ge(f_done[4 + v % 4], 6 * s + (v // 4 + 1 - 6))
                        fn(act_hi[:, q // 3, a:e], a32[q % 2][:, 0:e - a], ACT.Copy).then_inc(ahi_ready, 1)

            ffn_step(0, True)
            with act.Fori(1, FFN_STEPS) as s:
                ffn_step(s, False)
            for k in range(KD):
                v = 2 * KD + k
                act.wait_ge(f_free[4 + v % 4], 6 * (FFN_STEPS - 1) + v // 4 + 1)
                if k == 0:
                    act.wait_ge(f_done[7], 6 * FFN_STEPS)
                if k >= 2:
                    act.wait_ge(ms3_ready, k - 1)
                fn((sq_n, y_n)[k % 2][:], x1[:, k, :], ACT.Square).then_inc(sq3_ready, 1)
            act.wait_ge(ms3_ready, KD)
            for b, (a, e, _) in enumerate(PIECES):
                own.add(fn(rstd[:, a:e], ps[b][:, 0:e - a], ACT.Sqrt, bias=eps[:, 0:1], scale=1.0 / D))
            own.settle()
            act.sem_inc(rstd_ready, 1)

        @block.vector
        def _(dve):
            own = Chain(dve, dve_step)
            bf = Butterfly(dve, own)
            tt, ts, stt = nc.vector.tensor_tensor, nc.vector.tensor_scalar, nc.vector.scalar_tensor_tensor

            def take_mix(units, it, j):
                b = units.bank(j)
                dve.wait_ge(mix_done[b], units.nth(it, j) + 1)
                return mix(b), mix_free[b]

            def mix_taken(units, it, j):
                dve.wait_ge(mix_free[units.bank(j)], units.nth(it, j) + 1)

            def proj_taken(use):
                for b in range(3):
                    dve.wait_ge(proj_free[b], use + 1)

            dve.wait_ge(filt_in, 64)
            for j in range(6):
                a, e, _ = PIECES[j % 3]
                src, free = take_mix(u_setup, 0, j)
                if j >= 3:
                    dve.wait_ge(sin_ready, j - 2)
                layer = j // 3
                x, n = arg[:, a:e], turns[:, a:e]
                ts(x, src[0:FILT_HID, 0:e - a], f_vec[:, layer:layer + 1], f_vec[:, 2:3], ALU.add,
                   ALU.mult).then_inc(free, 1)
                dve.wait_ge(free, u_setup.nth(0, j) + 1)
                own(ts(n, x, 1.0 / (2 * math.pi), ROUND, ALU.mult, ALU.add))
                own(ts(n, n, ROUND, None, ALU.subtract))
                for part in TWO_PI:
                    own(stt(x, n, -part, x, ALU.mult, ALU.add))
                ts(x, x, PI_BELOW, -PI_BELOW, ALU.min, ALU.max).then_inc(arg_ready, 1)
            dve.wait_ge(vec_in, 16)
            lam = vec[:, V_LAM:V_LAM + 16]
            w = [sp_w[:, n, :] for n in range(6)]
            own(ts(w[0], lam, -1.0, None, ALU.mult))
            own(tt(w[1], lam, w[0], ALU.min))
            own(ts(w[0], w[0], 0.0, None, ALU.max))
            dve.sem_inc(sp_ready, 1)
            dve.wait_ge(sp_e, 1)
            own(ts(w[3], w[2], 1.0, None, ALU.add))
            dve.sem_inc(sp_ready, 1)
            own(ts(w[5], w[3], 1.0, None, ALU.subtract))
            own(ts(sp_pos[:], w[5], 0.0, None, ALU.is_equal))
            own(tt(w[5], w[5], sp_pos[:], ALU.add))
            own(nc.vector.reciprocal(w[5], w[5]))
            dve.wait_ge(sp_l, 1)
            own(tt(w[4], w[4], sp_pos[:], ALU.add))
            own(tt(w[4], w[4], w[5], ALU.mult))
            own(tt(w[4], w[4], w[2], ALU.mult))
            own(tt(w[4], w[4], w[0], ALU.add))
            own(ts(sp_pos[:], w[4], RG_C, None, ALU.mult))
            own(ts(sp_neg[:], w[4], -RG_C, None, ALU.mult))

            def ada_add(units, it, j, group):
                src, free = take_mix(units, it, j)
                tt(mod[:, bass.ds(2 * group, 2), :], src[:, 0:4].rearrange("p (a b) -> p a b", a=2),
                   vec[:, bass.ds(2 * group + V_BADA, 2)].unsqueeze(2).to_broadcast([P, 2, 2]),
                   ALU.add).then_inc(free, 1)
                dve.wait_ge(free, units.nth(it, j) + 1)
                dve.sem_inc(mod_ready, 1)

            for g in range(ADA_FIRST):
                ada_add(u_setup, 0, 7 + 2 * g, g)

            def norm_scale(gain, scale_chunk):
                for s in range(2):
                    own(stt(norm_a[:, :, s], mod[:, scale_chunk:scale_chunk + KD, s], 1.0,
                            vec[:, gain:gain + KD], ALU.add, ALU.mult))

            def modulated(x, root, tmp, out, shift_chunk, k, rounded, whole_ready):
                own(tt(tmp, x, root, ALU.mult))
                for a, e, s in SEQS:
                    own(ts(out[:, a:e], tmp[:, a:e], norm_a[:, k, s:s + 1],
                           mod[:, shift_chunk + k, s:s + 1], ALU.mult, ALU.add))
                dve.sem_inc(whole_ready, 1)

            def remainder(k, whole, rounded_ready, ready, count=None):
                dve.wait_ge(rounded_ready, k + 1)
                tt(h_lo[:, k, :], whole, h_hi[:, k, :].bitcast(F32), ALU.subtract).then_inc(ready, 1)

            norm_scale(V_N1, KD)
            for b in range(3):
                dve.wait_ge(proj_free[b], 1)
            own(nc.vector.reciprocal(rstd0[:], rstd0[:]))
            for k in range(KD):
                modulated(x_in[:, k, :], rstd0[:], y0[:], x_in[:, k, :], 0, k, None, h32_ready)
                if k:
                    remainder(k - 1, x_in[:, k - 1, :], hi_ready, h_ready)
            remainder(KD - 1, x_in[:, KD - 1, :], hi_ready, h_ready)
            dve.wait_ge(h_ready, KD)
            own.settle()
            for a, e in ((0, PAD_LAT), (PAD_LAT + LAT, PAD_CTX), (PAD_CTX + CTX, PAD_T)):
                own(nc.vector.memset(hin[:, a:e], 0.0))
            dve.sem_inc(hin_zero, 1)
            own.restart()

            def depthwise(out, src, taps_at, bias, count, left, last_sem):
                for a, e, seq in SEQS:
                    at = (PAD_CTX if seq else PAD_LAT) - left
                    own(ts(out[:, a:e], src[:, at:at + e - a], taps_at(0), bias, ALU.mult, ALU.add))
                for k in range(1, count):
                    for a, e, seq in SEQS:
                        at = (PAD_CTX if seq else PAD_LAT) - left + k
                        ins = stt(out[:, a:e], src[:, at:at + e - a], taps_at(k), out[:, a:e],
                                  ALU.mult, ALU.add)
                        own(ins)
                dve.sem_inc(last_sem, 1)

            def hy_conv(tile, use):
                proj_taken(use)
                dve.wait_ge(hy_stored, 16 * tile)
                depthwise(hout, hin, lambda k: vec[:, bass.ds(4 * tile + (V_HY + k), 1)],
                          vec[:, bass.ds(4 * tile + (V_HY + 3), 1)], 3, 1, hy_conved)

            def first_stage(src, dst, tmp, context_at):
                out = spectrum_places(dst)
                real_dft_even(bf, places(src, P), places(tmp, P), out)
                real_dft_odd(bf, places(src, P), places(tmp, P), out)
                real_dft_context(bf, places(src, P, NL), out)

            def take_k(i, j, imag):
                src, free = take_mix(u1, i, (13 if imag else 6) + j)
                base = FH * imag + 4 * j
                v = src[:, :].rearrange("p (a c) -> p a c", a=4)
                cuts = [(0, 4, 0)] if j < 2 else [(0, 1, 0), (1, 4, 1)]
                for n, (a, e, seq) in enumerate(cuts):
                    ins = tt(kstage[:, base + a:base + e, :], v[:, a:e, :],
                             rs_k[:, seq, :].unsqueeze(1).to_broadcast([P, e - a, P]), ALU.mult)
                    if n < len(cuts) - 1:
                        own(ins)
                ins.then_inc(free, 1)

            with dve.Fori(0, 8) as i:
                dve.wait_ge(decay_in, 16 * i + 16)
                for j in range(5):
                    src, free = take_mix(u1, i, j)
                    for s in range(2):
                        tile = 2 * j + s
                        ins = tt(taps[:, tile, :, :], src[:, 256 * s:256 * s + 256].rearrange("p (d c) -> p d c", d=2),
                                 decay[:, tile, :].unsqueeze(1).to_broadcast([P, 2, P]), ALU.mult)
                        if s == 0:
                            own(ins)
                    ins.then_inc(free, 1)
                for j in range(5):
                    mix_taken(u1, i, j)
                own(nc.vector.memset(taps[0:1, 0, 1, :], 0.0))
                own(nc.vector.memset(taps[0:1, NL, 1, :], 0.0))
                dve.sem_inc(taps_ready, 1)
                own(tt(tsum[:, :, :], taps[:, :, 0, :], taps[:, :, 1, :], ALU.add))
                dve.wait_ge(taps_sq, i + 1)
                for seq, (a, e) in enumerate(((0, 2 * NL), (2 * NL, 2 * NT))):
                    own(nc.vector.tensor_reduce(ss_k[:, seq, :], kstage[:, a:e, :].rearrange("p n c -> p c n"),
                                                AX_X, ALU.add))
                dve.sem_inc(ss_ready, 1)
                first_stage(tsum, f_a, f_t, None)
                dve.sem_inc(fa_ready, 1)
                own(tt(tsum[:, :, :], taps[:, :, 0, :], taps[:, :, 1, :], ALU.subtract))
                mix_taken(u1, i, 5)
                own(nc.vector.reciprocal(rs_k[:, :, :], rs_k[:, :, :]))
                hy_conv(2 * i, 2 * i + 1)
                for j in range(3):
                    take_k(i, j, 0)
                for j in range(3):
                    mix_taken(u1, i, 6 + j)
                first_stage(tsum, f_a, f_t, None)
                dve.sem_inc(fa_ready, 1)
                for g in range(2):
                    ada_add(u1, i, 10 + 2 * g, 2 * i + (ADA_FIRST + g))
                for j in range(3):
                    take_k(i, j, 1)
                for j in range(3):
                    mix_taken(u1, i, 13 + j)
                dve.sem_inc(k_ready, 1)
                hy_conv(2 * i + 1, 2 * i + 2)
                own.restart()

            dve.wait_ge(hy_stored, 16 * TILES_L1)
            dve.wait_ge(k_stored, 16 * 8)
            for a, e in ((0, PAD_LAT), (PAD_LAT + LAT, PAD_CTX), (PAD_CTX + CTX, PAD_T)):
                own(nc.vector.memset(rin[:, a:e], 0.0))
            dve.sem_inc(hin_zero, 1)
            own.restart()
            with dve.Fori(0, KD // 2) as m:
                for s in range(2):
                    n = 2 * m + s
                    proj_taken(2 * n + (L2_TILE0 + 1))
                    dve.wait_ge(rpack_in[s], 16 * m + 16)
                    pack = rpack[s]
                    depthwise(xr, rin, lambda k: pack[:, R_CONV + k:R_CONV + k + 1],
                              pack[:, R_CONVB:R_CONVB + 1], 4, 2, xr_ready)
                    for d in range(2):
                        for j in range(3):
                            mix_taken(u2, n, 6 * d + 3 + j)
                        own.add(tt(i_b[d][:], i_b[d][:], xr[:], ALU.mult))
                        dve.wait_ge(a2_ready, 2 * n + (d + 1))
                        stt(r_b[d][:], r_b[d][:], 1.0, t_b[d][:], ALU.add, ALU.mult).then_inc(m2_ready, 1)
                    for d in range(2):
                        dve.wait_ge(root_ready, 2 * n + (d + 1))
                        first = LAT if d == 0 else T - 1
                        own(nc.vector.memset(r_b[d][:, first:first + 1], 1.0))
                        own(tt(i_b[d][:], r_b[d][:], i_b[d][:], ALU.mult))
                        for a, e, seq in SEQS:
                            step = slice(a, e) if d == 0 else (slice(e - 1, a - 1, -1) if a else slice(e - 1, None, -1))
                            start = 0.0 if seq else pack[:, R_ST + d:R_ST + d + 1]
                            own.add(nc.vector.tensor_tensor_scan(t_b[d][:, step], a_b[d][:, step], i_b[d][:, step],
                                                                 start, ALU.mult, ALU.add))
                    own.settle()
                    own.add(nc.vector.tensor_copy(fin[:, bass.ds(n, 1), 0], t_b[0][:, T - 1:T]))
                    own.add(nc.vector.tensor_copy(fin[:, bass.ds(n, 1), 1], t_b[1][:, LAT:LAT + 1]))
                    own(tt(r_b[0][:], t_b[0][:], t_b[1][:], ALU.add))
                    proj_taken(2 * n + (L2_TILE0 + 2))
                    own(tt(r_b[0][:], r_b[0][:], g_ry[:], ALU.mult))
                    dve.sem_inc(zc_ready, 1)
                    own.restart()

            with dve.Fori(0, CH) as c:
                dve.wait_ge(fn_in, 16 * c + 16)
                dve.wait_ge(mix_done[u_fn.bank(4)], u_fn.nth(c, 4))
                out = spectrum_places(fn_a)
                real_dft_even(bf, places(fn_u, P), places(fn_tmp, P), out)
                bf.add(fn_a[:, 9, :], fn_u[:, NL, :], fn_u[:, NL + 1, :])
                bf.sub(fn_a[:, 10, :], fn_u[:, NL, :], fn_u[:, NL + 1, :])
                dve.sem_inc(fna_ready, 1)
                own.restart()

            with dve.Fori(0, CH) as c:
                for order in range(2):
                    j0 = 14 * order
                    for j in range(3):
                        mix_taken(u3, c, j0 + j)
                    first_stage(ztok, hy_a, hy_z, None)
                    dve.sem_inc(hya_ready, 1)
                    for j in range(6):
                        mix_taken(u3, c, j0 + 3 + j)
                    dve.wait_ge(k_in, 32 * c + 16 * (order + 1))
                    re, im = slice(0, FH), slice(FH, 2 * FH)
                    own.add(tt(hy_a[:, re, :], hy_z[:, re, :], hy_k[:, re, :], ALU.mult))
                    own.add(tt(ztok[:, :, :], hy_z[:, im, :], hy_k[:, im, :], ALU.mult))
                    own(tt(hy_a[:, im, :], hy_z[:, re, :], hy_k[:, im, :], ALU.mult))
                    own(tt(hy_a[:, re, :], hy_a[:, re, :], ztok[:, :, :], ALU.subtract))
                    own(tt(ztok[:, :, :], hy_z[:, im, :], hy_k[:, re, :], ALU.mult))
                    own(tt(hy_a[:, im, :], hy_a[:, im, :], ztok[:, :, :], ALU.add))
                    dve.sem_inc(y_ready, 1)
                    for j in range(5):
                        mix_taken(u3, c, j0 + 9 + j)
                    b_at = inverse_places(hy_z)
                    inverse_latent(bf, b_at, places(hy_a, P), places(ztok, P))
                    inverse_context(bf, b_at, places(hy_a, P), places(ztok, P, NL))
                    dve.wait_ge(xg_in, 32 * c + 16 * (order + 1))
                    if order == 0:
                        dve.wait_ge(hbias_in, 16 * c + 16)
                        dve.wait_ge(v_in, 16 * c + 16)
                    y = ztok[:, 0:NT, :].rearrange("p a c -> p (a c)")
                    own(stt(z_b[:], z_b[:], hbias[:, order:order + 1], y, ALU.mult, ALU.add))
                    own(tt(z_b[:], z_b[:], x_b[:], ALU.mult))
                    dve.sem_inc(z_ready, 1)
                own.restart()

            use0 = OUT_TILE0 + 1

            def split_z(n):
                dve.wait_ge(zhi_ready, n + 1)
                if n < 12:
                    hi, lo = (h_hi[:, n, :], h_lo[:, n, :]) if n < 8 else (z2_hi[:, n - 8, :], z2_lo[:, n - 8, :])
                else:
                    hi, lo = h_hi[:, n - 12, :], h_lo[:, n - 12, :]
                tt(lo, zraw[:], hi.bitcast(F32), ALU.subtract).then_inc(z_split, 1)

            def take_branch(job, m):
                dve.wait_ge(side_in[job % 2], 16 * (job // 2 + 1))
                for b, (a, e, _) in enumerate(PIECES):
                    dve.wait_ge(proj_done[b], use0 + job + 1)
                    dst = x1[:, m, a:e] if job < 8 else side[job % 2][:, a:e]
                    tt(dst, ps[b][:, 0:e - a], side[job % 2][:, a:e], ALU.mult).then_inc(proj_free[b], 1)
                if job >= 8:
                    proj_taken(use0 + job)
                    tt(x1[:, m, :], x1[:, m, :], side[job % 2][:], ALU.add).then_inc(side_used, 1)

            def split_merged(m):
                dve.wait_ge(mhi_ready, m + 1)
                hi, lo = ((h_hi[:, 4 + m, :], h_lo[:, 4 + m, :]) if m < 4 else
                          (z2_hi[:, m - 4, :], z2_lo[:, m - 4, :]))
                tt(lo, x1[:, m, :], hi.bitcast(F32), ALU.subtract).then_inc(m_split, 1)

            for n in range(4):
                split_z(n)
            for n in range(4, 12):
                split_z(n)
                take_branch(n - 4, n - 4)
            for n in range(12, 16):
                split_z(n)
            for m in range(KD):
                if m == 0:
                    proj_taken(use0 + 7)
                take_branch(8 + m, m)
            for m in range(KD):
                if m == 0:
                    dve.wait_ge(side_used, KD)
                take_branch(16 + m, m)
                if m:
                    split_merged(m - 1)
            split_merged(KD - 1)
            dve.wait_ge(m_split, KD)
            for m in range(KD):
                job = 24 + m
                dve.wait_ge(side_in[job % 2], 16 * (job // 2 + 1))
                for b, (a, e, seq) in enumerate(PIECES):
                    dve.wait_ge(proj_done[b], use0 + job + 1)
                    stt(x1[:, m, a:e], ps[b][:, 0:e - a], mod[:, 2 * KD + m, seq:seq + 1], side[job % 2][:, a:e],
                        ALU.mult, ALU.add).then_inc(proj_free[b], 1)
            proj_taken(use0 + 31)
            norm_scale(V_N2, 4 * KD)
            for b in range(3):
                mix_taken(u_out, 0, b)
            own(nc.vector.reciprocal(rstd[:], rstd[:]))
            for k in range(KD):
                buf = (y_n, sq_n)[k % 2]
                if k >= 2:
                    dve.wait_ge(h2_ready, k - 1)
                modulated(x1[:, k, :], rstd[:], buf[:], buf, 3 * KD, k, None, h2_32)
                if k:
                    remainder(k - 1, (y_n, sq_n)[(k - 1) % 2][:], h2_hi, h2_ready)
            remainder(KD - 1, (y_n, sq_n)[(KD - 1) % 2][:], h2_hi, h2_ready)
            dve.wait_ge(h2_ready, KD)
            own.restart()

            def gated_unit(s, n):
                a, e, _ = PIECES[n % 3]
                gb, gn = 2 * n % 4, 2 * n // 4
                ub, un = (2 * n + 1) % 4, (2 * n + 1) // 4
                dve.wait_ge(f_free[gb], 3 * s + (gn + 1))
                dve.wait_ge(f_done[ub], 3 * s + (un + 1))
                if n >= 2:
                    dve.wait_ge(act_ready, 6 * s + (n - 1))
                tt(a32[n % 2][:, 0:e - a], sil[n % 2][:, 0:e - a], ps[ub][:, 0:e - a],
                   ALU.mult).then_inc(f_free[ub], 1)

            def gated_remainder(s, n):
                a, e, _ = PIECES[n % 3]
                dve.wait_ge(ahi_ready, 6 * s + (n + 1))
                tt(act_lo[:, n // 3, a:e], a32[n % 2][:, 0:e - a], act_hi[:, n // 3, a:e].bitcast(F32),
                   ALU.subtract).then_inc(act_ready, 1)

            with dve.Fori(0, FFN_STEPS) as s:
                for n in range(7):
                    if n < 6:
                        gated_unit(s, n)
                    if n:
                        gated_remainder(s, n - 1)
                dve.wait_ge(act_ready, 6 * s + 6)
                for p, (a, e, seq) in enumerate(PIECES):
                    for m in range(KD):
                        v = KD * p + m
                        b = 4 + v % 4
                        dve.wait_ge(f_done[b], 6 * s + (v // 4 + 1))
                        stt(x1[:, m, a:e], ps[b][:, 0:e - a], mod[:, 5 * KD + m, seq:seq + 1], x1[:, m, a:e],
                            ALU.mult, ALU.add).then_inc(f_free[b], 1)
            for b in range(4, 8):
                dve.wait_ge(f_free[b], 6 * FFN_STEPS)
            dve.wait_ge(rstd_ready, 1)
            own(nc.vector.reciprocal(rstd[:], rstd[:]))
            for k in range(KD):
                stt(x1[:, k, :], x1[:, k, :], vec[:, V_FG + k:V_FG + k + 1], rstd[:], ALU.mult,
                    ALU.mult).then_inc(y_out, 1)


def dft_constants():
    f64 = np.float64
    p = np.arange(P, dtype=f64)
    fwd = np.zeros((P, FH, 3, P))
    inv = np.zeros((P, FH, 3, P))
    for q in range(FH):
        n, f1 = (2 * LAT, q) if q < 9 else (2 * CTX, q - 9)
        radix = n // P
        angle = 2 * np.pi * np.outer(p, f1 + radix * p) / n
        fwd[:, q] = np.stack([np.cos(angle), np.sin(angle), -np.sin(angle)], axis=1)
        weight = (1.0 if f1 in (0, radix // 2) else 2.0) / n
        back = angle.T
        inv[:, q] = weight * np.stack([-np.sin(back), np.cos(back), np.sin(back)], axis=1)
    angle = 2 * np.pi * np.outer(p, p) / P
    fn_ch = np.stack([np.sin(angle), np.cos(angle), -np.sin(angle), -np.cos(angle)], axis=1)
    fn_t = np.zeros((P, NT, 2, P))
    for m in range(NT):
        length, f1 = (LAT, m) if m < NL else (CTX, m - NL)
        radix = length // P
        angle = 2 * np.pi * np.outer(p, f1 + radix * p) / length
        fn_t[:, m] = np.stack([np.cos(angle), np.sin(angle)], axis=1) / np.sqrt(length * P)
    return [a.astype(np.float32) for a in (fwd, inv, fn_ch, fn_t)]


def filter_constants():
    f32 = np.float32
    feats, windows = [], []
    deltas = np.linspace(-math.log(1e-2) / 1.5, -math.log(1e-2) / 0.3, D_HY).astype(f32)
    for length in (LAT, CTX):
        t = np.arange(length, dtype=f32) / f32(length)
        ang = f32(2.0 * math.pi) * t[:, None] * np.arange(1, 9, dtype=f32)
        feats.append(np.concatenate([t[:, None], np.sin(ang), np.cos(ang)], axis=-1).T)
        window = np.exp(-t[:, None] * deltas)
        windows.append(window.reshape(length // P, P, CH, P).transpose(2, 1, 0, 3))
    decay = np.concatenate(windows, axis=2).astype(f32)
    return np.concatenate(feats, axis=1).astype(f32), np.concatenate([decay, decay], axis=0)


def columns(v):
    return np.ascontiguousarray(v.reshape(-1, P).T)


def tiles(w):
    n = w.shape[1] // P
    return w.reshape(KD, P, n, P).transpose(2, 1, 0, 3).reshape(n, P, D)


def kernel(x_prompt, x_sample, c, state_rglru, c_ctx, norm1_g, norm2_g, w_ada, b_ada, w_in,
           hy_conv_w, hy_conv_b, hy_f_w1, hy_f_b1, hy_f_w2, hy_f_b2, hy_f_w3, hy_f_freq, hy_bias,
           w_a, w_b, rg_conv_w, rg_conv_b, rg_wr, rg_br, rg_wi, rg_bi, rg_lam, w_c, w_o,
           w_gu, w_down, final_g):
    import concourse.bacc as bacc
    from concourse.bass_utils import run_bass_kernel_spmd

    fwd, inv, fn_ch, fn_t = dft_constants()
    feats, decay = filter_constants()

    tokens = np.concatenate([np.asarray(x_sample)[0], np.asarray(x_prompt)[0]], axis=0)
    cond = np.stack([np.asarray(c)[0], np.asarray(c_ctx)])

    t_in = tiles(np.asarray(w_in)[0])
    order = list(range(16)) + [x for n in range(8) for x in (16 + n, 24 + n)] + list(range(32, 56))
    def narrow(w):
        return w.reshape(4, P, 4, 2, P).transpose(2, 1, 3, 0, 4).reshape(4, P, D)
    t_gu, t_down = tiles(np.asarray(w_gu)[0]), np.asarray(w_down)[0].reshape(FF, P, D)
    ffn = [x for s in range(FFN_STEPS) for x in
           (t_gu[2 * s], t_gu[FF + 2 * s], t_gu[2 * s + 1], t_gu[FF + 2 * s + 1], t_down[2 * s], t_down[2 * s + 1])]
    weights = np.concatenate([t_in[order], narrow(np.asarray(w_b)[0]), tiles(np.asarray(w_c)[0]),
                              narrow(np.asarray(w_a)[0]), tiles(np.asarray(w_o)[0]), np.stack(ffn)], axis=0)

    hy = np.concatenate([np.asarray(hy_conv_w)[0], np.asarray(hy_conv_b)], axis=0)
    hy = hy.reshape(4, 12, P).transpose(2, 1, 0)
    plain = np.broadcast_to(np.array([0, 1, 0, 0], np.float32), (P, 4, 4))
    hy = np.concatenate([hy, plain], axis=1).reshape(P, 64)
    lam = np.asarray(rg_lam)[0].reshape(2, KD, P).transpose(2, 1, 0).reshape(P, 16)
    vec = np.concatenate([columns(np.asarray(norm1_g)[0]), columns(np.asarray(norm2_g)[0]),
                          columns(np.asarray(final_g)), columns(np.asarray(b_ada)[0]), hy, lam], axis=1)

    wr, wi = np.asarray(rg_wr)[0], np.asarray(rg_wi)[0]
    mats = np.stack([wr[0], wi[0], wr[1], wi[1]], axis=0).transpose(1, 2, 0, 3).reshape(KD, P, 4 * P)
    per_chunk = [np.asarray(rg_conv_w)[0], np.asarray(rg_conv_b), np.asarray(rg_br)[0], np.asarray(rg_bi)[0],
                 np.asarray(state_rglru)[0, 0]]
    vectors = np.concatenate(per_chunk, axis=0).reshape(-1, KD, P).transpose(1, 2, 0)
    rpack = np.concatenate([mats, vectors], axis=2)

    w3 = np.asarray(hy_f_w3)[0].reshape(FILT_HID, 2, 2, CH, P).transpose(1, 3, 0, 2, 4).reshape(8, FILT_HID, 2 * P)
    arrays = {
        "x": tokens.T.reshape(KD, P, T),
        "cvec": cond.reshape(2, KD, P).transpose(2, 1, 0),
        "w_ada": np.asarray(w_ada)[0].reshape(KD, P, HALF_GROUPS, 256).transpose(2, 1, 0, 3)
                 .reshape(HALF_GROUPS, P, KD * 256),
        "weights": weights,
        "vec": vec,
        "rpack": rpack,
        "f_w1": np.asarray(hy_f_w1)[0],
        "f_w2": np.asarray(hy_f_w2)[0],
        "f_vec": np.stack([np.asarray(hy_f_b1)[0], np.asarray(hy_f_b2)[0], np.asarray(hy_f_freq)[0]], axis=1),
        "w3": w3,
        "hbias": np.asarray(hy_bias)[0].reshape(2, CH, P).transpose(1, 2, 0),
        "feats": feats,
        "decay": decay,
        "ident": np.eye(P, dtype=np.float32),
        "fwd": fwd,
        "inv": inv,
        "fn_ch": fn_ch,
        "fn_t": fn_t,
    }
    arrays = {k: np.ascontiguousarray(v) for k, v in arrays.items()}
    nc = bacc.Bacc("TRN2", target_bir_lowering=False, num_devices=1)
    dr = {k: nc.dram_tensor(f"in_{k}", v.shape, F32, kind="ExternalInput").ap() for k, v in arrays.items()}
    for name, shape in (("y", (KD, P, T)), ("state_out", (P, KD, 2))):
        dr[name] = nc.dram_tensor(f"out_{name}", shape, F32, kind="ExternalOutput").ap()
    for name, shape in SCRATCH:
        dr[name] = nc.dram_tensor(f"scratch_{name}", shape, F32).ap()
    build_program(nc, dr)
    got = run_bass_kernel_spmd(nc, [{f"in_{k}": v for k, v in arrays.items()}], core_ids=[0]).results[0]
    y = got["out_y"].reshape(D, T).T
    state = got["out_state_out"].transpose(2, 1, 0).reshape(1, 1, 2, D)
    return (np.ascontiguousarray(y[LAT:])[None], np.ascontiguousarray(y[:LAT])[None], np.ascontiguousarray(state))
```

```python
import math
from contextlib import ExitStack

import numpy as np

import concourse.bass as bass
from concourse import mybir

F32 = mybir.dt.float32
F32R = mybir.dt.float32r
ALU = mybir.AluOpType
ACT = mybir.ActivationFunctionType
AX_X = mybir.AxisListType.X

P = 128
D = 1024
KD = D // P
LAT, CTX = 1024, 256
T = LAT + CTX
NL, NC = LAT // P, CTX // P
NT = NL + NC
PIECES = [(0, 512, 0), (512, 1024, 0), (1024, 1280, 1)]
SEQS = [(0, LAT, 0), (LAT, T, 1)]
D_HY = 512
CH = D_HY // P
D_FF = 2816
FF = D_FF // P
D_IN = 7168
EPS = 1e-6
RG_C = 8.0
FILT_EMB, FILT_HID = 17, 64
FH = 9 + 3
PAD_LAT, PAD_CTX, PAD_T = 2, 2 + LAT + 2, 2 + LAT + 2 + CTX + 2
HALF_GROUPS = 24
ADA_FIRST = 8
SQUARES_AT = ((0,), (1, 2), (3, 4), (5,), (6,), (7,), (), ())
FIRST_MIX = 3
MIX_BANKS = 5

V_N1, V_N2, V_FG, V_BADA = 0, KD, 2 * KD, 3 * KD
V_HY = V_BADA + 48
V_LAM = V_HY + 64
V_ALL = V_LAM + 2 * KD
R_CONV, R_CONVB, R_BR, R_BI, R_ST = 512, 516, 517, 519, 521
R_ALL = 523

TILES_L1, TILES_L2, TILES_L3 = 16, 16, 24
TILES_A, TILES_C, TILES_O = 4, 8, 8
L2_TILE0 = TILES_L1
L3_TILE0 = L2_TILE0 + TILES_L2
OUT_TILE0 = L3_TILE0 + TILES_L3
MIX_TILES = OUT_TILE0 + 2 * TILES_A + TILES_C + TILES_O
FFN_STEPS = FF // 2
FFN_TILES = 6
N_TILES = MIX_TILES + FFN_STEPS * FFN_TILES

TWO_PI = [6.28125, 0.0019350051879882812, 3.0199e-07]
ROUND = 1.5 * 2.0 ** 23
PI_BELOW = 3.1415925
SCRATCH = [("hy_s", (16, P, T)), ("k_s", (8, P, 2 * FH * P)), ("gate_s", (24, P, T)), ("za_s", (CH, P, T)),
           ("zb_s", (CH, P, T)), ("zc_s", (KD, P, T))]
COS = [math.cos(math.pi * k / 8) for k in range(5)]
SIN = [math.sin(math.pi * k / 8) for k in range(5)]


def real_dft_even(o, z, temp, out):
    e, d = temp(0, 4), temp(4, 8)
    o.add(e, z(0, 4), z(4, 8))
    o.sub(d, z(0, 4), z(4, 8))
    o.sub(out("re4"), temp(0), temp(2))
    o.sub(out("im4"), temp(3), temp(1))
    o.add(temp(8, 10), temp(0, 2), temp(2, 4))
    o.sub(temp(10), temp(5), temp(7))
    o.add(temp(11), temp(5), temp(7))
    o.add(out("re0"), temp(8), temp(9))
    o.sub(out("re8"), temp(8), temp(9))
    o.mul_add(out("re2"), temp(10), COS[2], temp(4))
    o.mul_add(out("re6"), temp(10), -COS[2], temp(4))
    o.mul_add(out("im6"), temp(11), -COS[2], temp(6))
    o.mul_sub(out("im2"), temp(11), -COS[2], temp(6))


def real_dft_odd(o, z, temp, out):
    o.sub(temp(0, 3), z(1, 4), z(7, 4, -1))
    o.add(temp(3, 6), z(1, 4), z(7, 4, -1))
    u = [None, temp(0), temp(1), temp(2)]
    v = [None, temp(3), temp(4), temp(5)]
    o.mul_add(temp(6), u[2], COS[2], z(0))
    o.mul_add(temp(7), u[2], -COS[2], z(0))
    o.mul(temp(8), u[3], COS[3])
    o.mul(temp(9), u[3], -COS[1])
    o.mul_add(temp(8), u[1], COS[1], temp(8))
    o.mul_add(temp(9), u[1], COS[3], temp(9))
    o.add(out("re1"), temp(6), temp(8))
    o.sub(out("re7"), temp(6), temp(8))
    o.add(out("re3"), temp(7), temp(9))
    o.sub(out("re5"), temp(7), temp(9))
    o.mul_add(temp(6), v[2], SIN[2], z(4))
    o.mul_sub(temp(7), v[2], SIN[2], z(4))
    o.mul(temp(8), v[3], -SIN[3])
    o.mul(temp(9), v[3], SIN[1])
    o.mul_add(temp(8), v[1], -SIN[1], temp(8))
    o.mul_add(temp(9), v[1], -SIN[3], temp(9))
    o.sub(out("im1"), temp(8), temp(6))
    o.add(out("im7"), temp(8), temp(6))
    o.sub(out("im3"), temp(9), temp(7))
    o.add(out("im5"), temp(9), temp(7))


def real_dft_context(o, z, out):
    o.add(out("cre0"), z(0), z(1))
    o.sub(out("cre2"), z(0), z(1))
    o.mul(out("cre1"), z(0), 1.0)
    o.mul(out("cim1"), z(1), -1.0)


def inverse_latent(o, b, temp, y):
    rp, rm, ip, im = temp(0, 3), temp(3, 6), temp(6, 9), temp(9, 12)
    low_re, high_re = b("re", 1, 3), b("re", 7, 5)
    low_im, high_im = b("im", 1, 3), b("im", 7, 5)
    o.add(rp, low_re, high_re)
    o.sub(rm, low_re, high_re)
    o.add(ip, low_im, high_im)
    o.sub(im, low_im, high_im)
    o.add(temp(12), b("re0"), b("re8"))
    o.sub(temp(13), b("re0"), b("re8"))
    re4, im4 = b("re4"), b("im4")
    x, w, d = temp(14), temp(15), temp(16)
    o.add(x, temp(12), re4)
    o.add(w, temp(0), temp(2))
    o.sub(y(4), x, temp(1))
    o.sub(d, temp(11), temp(9))
    o.add(x, x, temp(1))
    o.add(y(4), y(4), d)
    o.add(y(0), x, w)
    x = [None] + [temp(17 + 2 * k) for k in range(3)]
    w = [None] + [temp(18 + 2 * k) for k in range(3)]
    sums = []
    for i in (1, 2, 3):
        s = i % 2
        r = [None] + [temp((3 if s else 0) + k) for k in range(3)]
        m = [None] + [temp((6 if s else 9) + k) for k in range(3)]
        terms_w = [(r[3], math.cos(3 * math.pi * i / 8)), (r[1], math.cos(math.pi * i / 8)),
                   (m[2], -math.sin(math.pi * i / 4)), (im4, -math.sin(math.pi * i / 2))]
        terms_x = [(r[2], math.cos(math.pi * i / 4)), (re4, math.cos(math.pi * i / 2)),
                   (m[1], -math.sin(math.pi * i / 8)), (m[3], -math.sin(3 * math.pi * i / 8))]
        for out, terms, first in ((w[i], terms_w, None), (x[i], terms_x, temp(12 + s))):
            sums.append((out, [(a, c) for a, c in terms if abs(c) > 1e-9], first))
    for k in range(4):
        for out, terms, first in sums:
            if k == 0 and first is None:
                o.mul(out, *terms[0])
            elif k < len(terms):
                o.mul_add(out, *terms[k], out if k else first)
    for i in (1, 2, 3):
        o.add(y(i), x[i], w[i])
        o.sub(y(8 - i), x[i], w[i])


def inverse_context(o, b, temp, y):
    o.add(temp(0), b("cre0"), b("cre2"))
    o.sub(temp(1), b("cre0"), b("cre2"))
    o.add(y(0), temp(0), b("cre1"))
    o.sub(y(1), temp(1), b("cim1"))


class Chain:

    def __init__(self, eng, sem):
        self.eng, self.sem, self.n = eng, sem, 0

    def __call__(self, ins):
        ins.then_inc(self.sem, 1)
        self.n += 1
        self.eng.wait_ge(self.sem, self.n)

    def loose(self, ins):
        ins.then_inc(self.sem, 1)
        self.n += 1
        if self.n > 1:
            self.eng.wait_ge(self.sem, self.n - 1)

    def add(self, ins):
        ins.then_inc(self.sem, 1)
        self.n += 1

    def settle(self):
        if self.n:
            self.eng.wait_ge(self.sem, self.n)

    def restart(self):
        self.settle()
        if self.n:
            self.eng.sem_clear(self.sem)
        self.n = 0


class Butterfly:

    def __init__(self, dve, chain):
        self.dve, self.chain = dve, chain

    def add(self, out, a, b):
        self.chain.loose(self.dve.tensor_tensor(out, a, b, ALU.add))

    def sub(self, out, a, b):
        self.chain.loose(self.dve.tensor_tensor(out, a, b, ALU.subtract))

    def mul(self, out, a, c):
        self.chain.loose(self.dve.tensor_scalar(out, a, float(c), None, ALU.mult))

    def mul_add(self, out, a, c, b):
        self.chain.loose(self.dve.scalar_tensor_tensor(out, a, float(c), b, ALU.mult, ALU.add))

    def mul_sub(self, out, a, c, b):
        self.chain.loose(self.dve.scalar_tensor_tensor(out, a, float(c), b, ALU.mult, ALU.subtract))


class MixUnits:

    def __init__(self, base, units):
        self.base, self.units = list(base), units

    def uses(self, b):
        return len([j for j in range(self.units) if j % MIX_BANKS == b])

    def bank(self, j):
        return j % MIX_BANKS

    def nth(self, it, j):
        b = j % MIX_BANKS
        return it * self.uses(b) + (self.base[b] + j // MIX_BANKS)

    def after(self, passes):
        return [self.base[b] + passes * self.uses(b) for b in range(MIX_BANKS)]


def places(buf, width, first=0):
    def at(a, b=None, step=1):
        if b is None:
            return buf[:, first + a, :]
        if step == 1:
            return buf[:, first + a:first + b, :]
        return buf[:, first + a:first + b:-1, :]
    return at


def spectrum_places(buf):
    def at(name):
        if name.startswith("c"):
            return buf[:, 9 + int(name[3:]), :] if name[1:3] == "re" else buf[:, 19, :]
        f = int(name[2:])
        return buf[:, f if name[:2] == "re" else 11 + f, :]
    return at


def inverse_places(buf):
    def at(name, a=None, b=None):
        part = 0 if "re" in name else 1
        if a is not None:
            lo, hi = 2 * (a - 1) + part, 2 * (b - 1) + part
            return buf[:, lo:hi + 1:2, :] if a < b else buf[:, lo:hi - 1:-2, :]
        if name in ("re0", "re8", "cre0", "cre2"):
            return buf[:, 16 + ("re0", "re8", "cre0", "cre2").index(name), :]
        f = 8 if name.startswith("c") else int(name[2:])
        return buf[:, 2 * (f - 1) + part, :]
    return at


HAS_IMAG = [1 <= q <= 7 or q == 10 for q in range(FH)]
IMAG_AT = {q: (19 if q == 10 else 11 + q) for q in range(FH) if HAS_IMAG[q]}
PAIRS = [(1, 2), (3, 4), (5, 6), (7, 10)]
SINGLES = (0, 8, 9, 11)


def build_program(nc, dr):
    ctx = ExitStack()
    with ctx:
        def sem(name):
            return ctx.enter_context(nc.semaphore(name))

        def sb(stack, name, shape, dt=F32):
            return stack.enter_context(nc.sbuf_tensor(name, shape, dt))

        w_raw = [sb(ctx, f"w_raw{s}", [P, D]) for s in range(2)]
        w_hi = [sb(ctx, f"w_hi{s}", [P, D], F32R) for s in range(2)]
        w_lo = [sb(ctx, f"w_lo{s}", [P, D], F32R) for s in range(2)]
        h_hi = sb(ctx, "h_hi", [P, KD, T], F32R)
        h_lo = sb(ctx, "h_lo", [P, KD, T], F32R)
        vec = sb(ctx, "vec", [P, V_ALL])
        mod = sb(ctx, "mod", [P, 48, 2])
        norm_a = sb(ctx, "norm_a", [P, KD, 2])
        fin = sb(ctx, "fin", [P, KD, 2])
        ones = sb(ctx, "ones", [P, P])
        eps = sb(ctx, "eps", [P, 1])
        zero_col = sb(ctx, "zero_col", [P, 1])
        hy_taps = sb(ctx, "hy_taps", [P, 4])
        sp_w = sb(ctx, "sp_w", [P, 6, 2 * KD])
        sp_pos = sb(ctx, "sp_pos", [P, 2 * KD])
        sp_neg = sb(ctx, "sp_neg", [P, 2 * KD])
        cvec = sb(ctx, "cvec", [P, KD, 2])
        csilu = sb(ctx, "csilu", [P, KD, 2])
        ps = [ctx.enter_context(nc.psum_tensor(f"ps{b}", [P, 512], F32)) for b in range(8)]

        fwd_stack = ExitStack()
        fwd = sb(fwd_stack, "fwd", [P, FH, 3, P])
        filt_ada = sb(fwd_stack, "filt_ada", [P, T])
        h2f = filt_ada[0:FILT_HID, :]
        ada_row = filt_ada[FILT_HID:FILT_HID + 2, 0:512]
        ada_w = [sb(fwd_stack, f"ada_w{s}", [P, KD * 256]) for s in range(2)]
        ident = sb(fwd_stack, "ident", [P, P])

        st = ExitStack()
        x_in = sb(st, "x_in", [P, KD, T])
        sq0 = sb(st, "sq0", [P, T])
        y0 = sb(st, "y0", [P, T])
        rstd0 = sb(st, "rstd0", [P, T])
        f_vec = sb(st, "f_vec", [FILT_HID, 3])
        f_w1 = sb(st, "f_w1", [FILT_EMB, FILT_HID])
        f_w2 = sb(st, "f_w2", [FILT_HID, FILT_HID])
        feats = sq0[0:FILT_EMB, :]
        h1f = x_in[0:FILT_HID, 7, :]
        arg = x_in[0:FILT_HID, 6, :]
        turns = x_in[0:FILT_HID, 5, :]
        st.close()

        st = ExitStack()
        hin = sb(st, "hin", [P, PAD_T])
        hout = sb(st, "hout", [P, T])
        decay = sb(st, "decay", [P, NT, P])
        w3 = sb(st, "w3", [FILT_HID, 2 * P])
        taps = sb(st, "taps", [P, NT, 2, P])
        tsum = sb(st, "tsum", [P, NT, P])
        kstage = sb(st, "kstage", [P, 2 * FH, P])
        f_a = sb(st, "f_a", [P, 20, P])
        f_t = sb(st, "f_t", [P, 12, P])
        ss_k = sb(st, "ss_k", [P, 2, P])
        rs_k = sb(st, "rs_k", [P, 2, P])
        hy_part = sb(st, "hy_part", [P, CTX])
        st.close()
        fwd_l1 = fwd

        st = ExitStack()
        r_b, i_b, a_b = ([sb(st, f"{name}0", [P, T])] for name in ("r_b", "i_b", "a_b"))
        rin = sb(st, "rin", [P, PAD_T])
        g_ry = sb(st, "g_ry", [P, T])
        xr = sb(st, "xr", [P, T])
        rpack = [sb(st, f"rpack{s}", [P, R_ALL]) for s in range(2)]
        for buf, name in ((r_b, "r_b"), (i_b, "i_b"), (a_b, "a_b")):
            buf.append(sb(st, f"{name}1", [P, T]))
        t_b = [sb(st, f"t_b{d}", [P, T]) for d in range(2)]
        st.close()
        fwd_stack.close()
        st = ExitStack()
        fn_ch = sb(st, "fn_ch", [P, 4, P])
        fn_t = sb(st, "fn_t", [P, NT, 2, P])
        fn_u = sb(st, "fn_u", [P, NT, P])
        fn_a = sb(st, "fn_a", [P, 20, P])
        fn_c = sb(st, "fn_c", [P, NT, 2, P])
        st.close()
        fn_y = fn_u[:, :, :].rearrange("p n c -> p (n c)")
        fn_tmp = fn_c[:, :, :, :].rearrange("p n d c -> p (n d) c")


        st = ExitStack()
        fwd3 = sb(st, "fwd3", [P, FH, 3, P])
        ident3 = sb(st, "ident3", [P, P])
        inv = sb(st, "inv", [P, FH, 3, P])
        x_b = sb(st, "x_b", [P, T])
        v_b = sb(st, "v_b", [P, T])
        z_b = sb(st, "z_b", [P, T])
        ztok = sb(st, "ztok", [P, FH, P])
        hy_a = sb(st, "hy_a", [P, 2 * FH, P])
        hy_z = sb(st, "hy_z", [P, 2 * FH, P])
        hbias = sb(st, "hbias", [P, 2])
        g_st = sb(st, "g_st", [P, T])
        hy_k = sb(st, "hy_k", [P, 2 * FH, P])
        st.close()

        low_stack = ExitStack()
        z2_hi = sb(low_stack, "z2_hi", [P, 4, T], F32R)
        z2_lo = sb(low_stack, "z2_lo", [P, 4, T], F32R)
        x1 = sb(low_stack, "x1", [P, KD, T])
        st = ExitStack()
        side = [sb(st, f"side{s}", [P, T]) for s in range(2)]
        zraw = [sb(st, f"zraw{s}", [P, T]) for s in range(2)]
        st.close()
        sq_o, sq_sum = zraw

        def norm1_u(k, a, e):
            return x_in[:, k, a:e]

        def norm2_u(k, a, e):
            return side[1][:, k % 2 * 512:k % 2 * 512 + e - a]

        st = ExitStack()
        act_hi = sb(st, "act_hi", [P, 2, T], F32R)
        act_lo = sb(st, "act_lo", [P, 2, T], F32R)
        st.close()
        low_stack.close()
        st = ExitStack()
        wf_hi = list(w_hi) + [sb(st, f"wf_hi{s}", [P, D], F32R) for s in range(2, 6)]
        wf_lo = list(w_lo) + [sb(st, f"wf_lo{s}", [P, D], F32R) for s in range(2, 6)]
        sil = [sb(st, f"sil{s}", [P, 512]) for s in range(2)]
        a32 = [sb(st, f"a32_{s}", [P, 512]) for s in range(2)]
        st.close()
        sq_end = sil
        sq_end_sum = [w_raw[0][:, 0:512], w_raw[0][:, 512:1024], w_raw[1][:, 0:256]]

        vec_in, consts_in, filt_in, cvec_in = sem("vec_in"), sem("consts_in"), sem("filt_in"), sem("cvec_in")
        x_loaded = [sem(f"x_loaded{k}") for k in range(KD)]
        ada_in = [sem(f"ada_in{s}") for s in range(2)]
        raw_in = [sem(f"raw_in{s}") for s in range(2)]
        hpack_in, decay_in, w3_in = sem("hpack_in"), sem("decay_in"), sem("w3_in")
        rpack_in = [sem(f"rpack_in{s}") for s in range(2)]
        fn_const_in, fn_in = sem("fn_const_in"), sem("fn_in")
        hy_const_in, v_in, xg_in, k_in, hbias_in = (sem("hy_const_in"), sem("v_in"), sem("xg_in"), sem("k_in"),
                                                    sem("hbias_in"))
        side_in = [sem(f"side_in{s}") for s in range(2)]
        zraw_in = [sem(f"zraw_in{s}") for s in range(2)]
        hy_stored, k_stored, zc_stored, zb_stored = (sem("hy_stored"), sem("k_stored"), sem("zc_stored"),
                                                     sem("zb_stored"))
        gate_stored, za_stored, fin_stored, y_stored = (sem("gate_stored"), sem("za_stored"), sem("fin_stored"),
                                                        sem("y_stored"))
        split_done = sem("split_done")
        proj_done = [sem(f"proj_done{b}") for b in range(3)]
        proj_free = [sem(f"proj_free{b}") for b in range(3)]
        mix_done = [sem(f"mix_done{b}") for b in range(MIX_BANKS)]
        mix_free = [sem(f"mix_free{b}") for b in range(MIX_BANKS)]
        act_step, dve_step, pool_step, conv_step = (sem("act_step"), sem("dve_step"), sem("pool_step"),
                                                    sem("conv_step"))
        consts_set, csilu_set, arg_ready, sin_ready = (sem("consts_set"), sem("csilu_set"), sem("arg_ready"),
                                                       sem("sin_ready"))
        ada_row_ready, mod_ready = sem("ada_row_ready"), sem("mod_ready")
        sq_ready, ms_ready, u_ready, hi_ready, h_ready = (
            sem("sq_ready"), sem("ms_ready"), sem("u_ready"), sem("hi_ready"), sem("h_ready"))
        hin_zero, hin_ready, hy_conved = sem("hin_zero"), sem("hin_ready"), sem("hy_conved")
        taps_ready, taps_sq, ss_ready, norm_root, fa_ready, k_ready = (
            sem("taps_ready"), sem("taps_sq"), sem("ss_ready"), sem("norm_root"), sem("fa_ready"), sem("k_ready"))
        rin_ready, xr_ready, sp_ready, ri_ready, a2_ready, m2_ready, root_ready, zc_ready = (
            sem("rin_ready"), sem("xr_ready"), sem("sp_ready"), sem("ri_ready"), sem("a2_ready"),
            sem("m2_ready"), sem("root_ready"), sem("zc_ready"))
        sp_e, sp_l = sem("sp_e"), sem("sp_l")
        g_ready, rg_done = sem("g_ready"), sem("rg_done")
        fna_ready, fnc_ready, fny_ready = sem("fna_ready"), sem("fnc_ready"), sem("fny_ready")
        ztok_ready, hya_ready, z_ready, y_ready, b_ready, za_ready, gate_ready, x_used, k_used = (
            sem("ztok_ready"), sem("hya_ready"), sem("z_ready"), sem("y_ready"), sem("b_ready"), sem("za_ready"),
            sem("gate_ready"), sem("x_used"), sem("k_used"))
        zhi_ready, z_split, side_used, merged_done, mhi_ready, m_split, x1_ready, sq1_ready = (
            sem("zhi_ready"), sem("z_split"), sem("side_used"), sem("merged_done"), sem("mhi_ready"),
            sem("m_split"), sem("x1_ready"), sem("sq1_ready"))
        sq_summed, u2_ready, h2_hi, h2_ready = sem("sq_summed"), sem("u2_ready"), sem("h2_hi"), sem("h2_ready")
        f_done = [sem(f"f_done{b}") for b in range(8)]
        f_free = [sem(f"f_free{b}") for b in range(8)]
        sil_ready, a32_ready, ahi_ready, act_ready = sem("sil_ready"), sem("a32_ready"), sem("ahi_ready"), sem("act_ready")
        sq3_ready, sq3_summed, ms3_ready, root3_ready, y_out = (
            sem("sq3_ready"), sem("sq3_summed"), sem("ms3_ready"), sem("root3_ready"), sem("y_out"))

        u_setup = MixUnits([0] * MIX_BANKS, 6 + 2 * ADA_FIRST)
        u_taps = MixUnits(u_setup.after(1), 5)
        u1 = MixUnits(u_taps.after(1), 1 + 1 + 3 + 5 + 3 + 1)
        u1_last = MixUnits(u1.after(7), 1 + 1 + 3 + 3 + 1)
        u2 = MixUnits(u1_last.after(1), 12 + 5 + 3 + 12)
        RG_UNIT, FN1_UNIT, FN2_UNIT = (0, 12 + 5 + 3), 12, 12 + 5
        u3 = MixUnits(u2.after(KD // 2), 2 * (3 + 6 + 5))
        out_base = u3.after(CH)
        NORM_BANKS = (1, 2, 3)

        def mix(b):
            return ps[FIRST_MIX + b]

        block = ctx.enter_context(nc.Block())
        stream = dr["weights"]

        @block.sync
        def _(sp):
            def load_tile(t, slot):
                sp.dma_start(w_raw[slot][:], stream[t]).then_inc(raw_in[slot], 16)

            def load_ahead(t, slot):
                sp.wait_ge(split_done, t + 1)
                load_tile(t + 2, slot)

            sp.dma_start(cvec[:], dr["cvec"]).then_inc(cvec_in, 16)
            sp.dma_start(feats, dr["feats"]).then_inc(filt_in, 16)
            sp.dma_start(f_w1[:], dr["f_w1"]).then_inc(filt_in, 16)
            sp.dma_start(f_w2[:], dr["f_w2"]).then_inc(filt_in, 16)
            sp.dma_start(f_vec[:], dr["f_vec"]).then_inc(filt_in, 16)
            sp.dma_start(ident[:], dr["ident"]).then_inc(consts_in, 16)
            sp.dma_start(vec[:], dr["vec"]).then_inc(vec_in, 16)
            for g in range(2):
                sp.dma_start(ada_w[g][:], dr["w_ada"][g]).then_inc(ada_in[g], 16)
            for k in range(5):
                sp.dma_start(x_in[:, k, :], dr["x"][k]).then_inc(x_loaded[k], 16)
            for g in range(2, ADA_FIRST + 2):
                sp.wait_ge(ada_row_ready, g - 1)
                sp.dma_start(ada_w[g % 2][:], dr["w_ada"][g]).then_inc(ada_in[g % 2], 16)
                if g == 3:
                    sp.wait_ge(sin_ready, 6)
                if 3 <= g < 6:
                    sp.dma_start(x_in[:, g + 2, :], dr["x"][g + 2]).then_inc(x_loaded[g + 2], 16)
            sp.dma_start(fwd[:], dr["fwd"]).then_inc(consts_in, 16)
            load_tile(0, 0)
            load_tile(1, 1)
            sp.wait_ge(h_ready, 3 * KD)

            def load_taps(i):
                sp.dma_start(w3[:], dr["w3"][i]).then_inc(w3_in, 16)
                sp.dma_start(decay[:], dr["decay"][i]).then_inc(decay_in, 16)

            def l1_pass(i, last):
                load_ahead(2 * i, 0)
                if not last:
                    sp.wait_ge(taps_ready, i + 1)
                    load_taps(i + 1)
                load_ahead(2 * i + 1, 1)
                if not last:
                    sp.wait_ge(ada_row_ready, i + (ADA_FIRST + 1))
                    for g in range(2):
                        sp.dma_start(ada_w[g][:], dr["w_ada"][2 * i + (ADA_FIRST + 2 + g)]).then_inc(ada_in[g], 16)
                sp.wait_ge(hy_conved, 2 * i + 1)
                sp.dma_start(dr["hy_s"][2 * i], hout[:]).then_inc(hy_stored, 16)
                sp.wait_ge(k_ready, i + 1)
                sp.dma_start(dr["k_s"][i], kstage[:]).then_inc(k_stored, 16)
                if not last:
                    sp.wait_ge(hy_conved, 2 * i + 2)
                    sp.dma_start(dr["hy_s"][2 * i + 1], hout[:]).then_inc(hy_stored, 16)

            load_taps(0)
            with sp.Fori(0, 7) as i:
                l1_pass(i, False)
            l1_pass(7, True)

            sp.wait_ge(mod_ready, ADA_FIRST + 8)
            sp.wait_ge(k_stored, 16 * 8)
            sp.dma_start(rpack[0][:], dr["rpack"][0]).then_inc(rpack_in[0], 16)
            sp.dma_start(fn_ch[:], dr["fn_ch"]).then_inc(fn_const_in, 16)
            sp.dma_start(fn_t[:], dr["fn_t"]).then_inc(fn_const_in, 16)

            def l2_pair(m, last):
                sp.wait_ge(zb_stored, 16 * m)
                sp.dma_start(fn_u[:], dr["hy_s"][m + 12]).then_inc(fn_in, 16)
                for s in range(2):
                    n = 2 * m + s
                    if not (last and s):
                        sp.wait_ge(zc_ready, n)
                        sp.dma_start(rpack[1 - s][:], dr["rpack"][n + 1]).then_inc(rpack_in[1 - s], 16)
                    load_ahead(2 * n + L2_TILE0, 0)
                    load_ahead(2 * n + (L2_TILE0 + 1), 1)
                    if s == 1:
                        sp.wait_ge(mix_free[u2.bank(FN2_UNIT + 2)], u2.nth(m, FN2_UNIT + 2) + 1)
                        sp.dma_start(dr["zb_s"][m], fn_y).then_inc(zb_stored, 16)
                    if last and s:
                        sp.wait_ge(zb_stored, 16 * CH)
                        sp.dma_start(ident3[:], dr["ident"]).then_inc(hy_const_in, 16)
                        sp.dma_start(fwd3[:], dr["fwd"]).then_inc(hy_const_in, 16)
                        sp.dma_start(inv[:], dr["inv"]).then_inc(hy_const_in, 16)
                    sp.wait_ge(zc_ready, n + 1)
                    sp.dma_start(dr["zc_s"][n], r_b[0][:]).then_inc(zc_stored, 16)

            sp.wait_ge(hy_conved, TILES_L1)
            sp.dma_start(dr["hy_s"][TILES_L1 - 1], hout[:]).then_inc(hy_stored, 16)
            sp.wait_ge(hy_stored, 16 * TILES_L1)
            with sp.Fori(0, KD // 2 - 1) as m:
                l2_pair(m, False)
            l2_pair(KD // 2 - 1, True)

            sp.dma_start(v_b[:], dr["hy_s"][0]).then_inc(v_in, 16)
            sp.dma_start(dr["state_out"], fin[:]).then_inc(fin_stored, 16)
            sp.wait_ge(zc_stored, 16 * KD)

            def load_z(n, src):
                if n >= 2:
                    sp.wait_ge(z_split, n - 1)
                sp.dma_start(zraw[n % 2][:], src).then_inc(zraw_in[n % 2], 16)

            def l3_pass(c, last):
                t = 6 * c + L3_TILE0
                sp.dma_start(hbias[:], dr["hbias"][c]).then_inc(hbias_in, 16)
                for order in range(2):
                    sp.wait_ge(z_ready, 2 * c + order)
                    sp.dma_start(x_b[:], dr["hy_s"][c + (4 + 4 * order)]).then_inc(xg_in, 16)
                    sp.dma_start(hy_k[:], dr["k_s"][c + 4 * order]).then_inc(k_in, 16)
                    if order == 1 and not last:
                        sp.dma_start(v_b[:], dr["hy_s"][c + 1]).then_inc(v_in, 16)
                    for g in range(3):
                        j = 3 * order + g
                        load_ahead(t + j, j % 2)
                        for b in range(3):
                            sp.wait_ge(proj_free[b], t + (j + 2))
                        sp.dma_start(dr["gate_s"][6 * c + j], g_st[:]).then_inc(gate_stored, 16)
                        if last and order == 1 and g == 1:
                            sp.wait_ge(y_ready, 2 * CH)
                            for n in range(2):
                                load_z(n, dr["zb_s"][n])
                sp.wait_ge(z_ready, 2 * c + 2)
                sp.dma_start(dr["za_s"][c], z_b[:]).then_inc(za_stored, 16)

            with sp.Fori(0, CH - 1) as c:
                l3_pass(c, False)
            l3_pass(CH - 1, True)
            for n in range(2, 4):
                load_z(n, dr["zb_s"][n])
            sp.wait_ge(za_stored, 16 * CH)
            sp.wait_ge(gate_stored, 16 * TILES_L3)

            def load_side(n, src):
                if 2 <= n < 10 or n >= 26:
                    for b in range(3):
                        sp.wait_ge(proj_free[b], OUT_TILE0 + n)
                elif n >= 10:
                    sp.wait_ge(side_used, n - 9)
                sp.dma_start(side[n % 2][:], src).then_inc(side_in[n % 2], 16)

            z_src = [dr["zb_s"][c] for c in range(4)] + [dr["zc_s"][n] for n in range(8)] + \
                    [dr["za_s"][c] for c in range(4)]
            gate_src = [dr["gate_s"][8 + m] for m in range(8)] + [dr["gate_s"][16 + m] for m in range(8)] + \
                       [dr["gate_s"][m] for m in range(8)] + [dr["x"][m] for m in range(8)]
            for n in range(4, 12):
                load_z(n, z_src[n])
                load_side(n - 4, gate_src[n - 4])
                if n % 2:
                    load_ahead(OUT_TILE0 + (n - 5) // 2, (n - 5) // 2 % 2)
            for n in range(12, 16):
                load_z(n, z_src[n])
            for n in range(8):
                load_side(8 + n, gate_src[8 + n])
                load_ahead(OUT_TILE0 + 4 + n, n % 2)
            for n in range(8):
                load_side(16 + n, gate_src[16 + n])
                if n % 2:
                    load_ahead(OUT_TILE0 + 12 + n // 2, n // 2 % 2)
            for n in range(8):
                load_side(24 + n, gate_src[24 + n])
                load_ahead(OUT_TILE0 + 16 + n, n % 2)
            with sp.Fori(0, FFN_STEPS * FFN_TILES // 2 - 1) as m:
                load_ahead(2 * m + MIX_TILES, 0)
                load_ahead(2 * m + (MIX_TILES + 1), 1)
            for p, (a, e, _) in enumerate(PIECES):
                sp.wait_ge(y_out, KD * (p + 1))
                sp.dma_start(dr["y"][:, :, a:e], x1[:, :, a:e]).then_inc(y_stored, 16)
            sp.wait_ge(fin_stored, 16)
            sp.wait_ge(y_stored, 16 * 3)

        @block.gpsimd
        def _(pool):
            nc.gpsimd.memset(ones[:], 1.0).then_inc(consts_set, 1)
            nc.gpsimd.memset(eps[:], EPS).then_inc(consts_set, 1)
            nc.gpsimd.memset(zero_col[:], 0.0).then_inc(consts_set, 1)
            pool.wait_ge(consts_set, 3)

            def split(t, slot, hi, lo):
                pool.wait_ge(raw_in[slot % 2], t * 8 + (16 - 8 * (slot % 2)))
                nc.gpsimd.tensor_tensor(hi[:], w_raw[slot % 2][:], zero_col[:].to_broadcast([P, D]),
                                        ALU.add).then_inc(pool_step, 1)
                pool.wait_ge(pool_step, t + 1)
                nc.gpsimd.tensor_tensor(lo[:], w_raw[slot % 2][:], hi[:].bitcast(F32),
                                        ALU.subtract).then_inc(split_done, 1)

            own = Chain(pool, conv_step)

            def hy_conv(tile, use):
                for b in range(3):
                    pool.wait_ge(proj_free[b], use + 1)
                pool.wait_ge(hy_stored, 16 * tile)
                own(nc.gpsimd.tensor_copy(hy_taps[:], vec[:, bass.ds(4 * tile + V_HY, 4)]))
                for a, e, seq in SEQS:
                    at = (PAD_CTX if seq else PAD_LAT) - 1
                    own.add(nc.gpsimd.tensor_scalar(hout[:, a:e], hin[:, at:at + e - a], hy_taps[:, 0:1],
                                                    hy_taps[:, 3:4], ALU.mult, ALU.add))
                own.settle()
                for k in (1, 2):
                    for a in range(0, T, CTX):
                        at = (PAD_LAT + a if a < LAT else PAD_CTX) - 1 + k
                        own(nc.gpsimd.tensor_scalar(hy_part[:], hin[:, at:at + CTX], hy_taps[:, k:k + 1], None,
                                                    ALU.mult))
                        own(nc.gpsimd.tensor_tensor(hout[:, a:a + CTX], hout[:, a:a + CTX], hy_part[:], ALU.add))
                pool.sem_inc(hy_conved, 1)

            split(0, 0, w_hi[0], w_lo[0])
            split(1, 1, w_hi[1], w_lo[1])
            pool.wait_ge(vec_in, 16)
            with pool.Fori(0, 8) as i:
                for s in range(2):
                    pool.wait_ge(proj_done[2], 2 * i + (2 + s))
                    split(2 * i + (2 + s), s, w_hi[s], w_lo[s])
                    if s == 0:
                        hy_conv(2 * i, 2 * i + 1)
                own.restart()
            with pool.Fori(TILES_L1 // 2 + 1, OUT_TILE0 // 2 + 1) as m:
                for s in range(2):
                    pool.wait_ge(proj_done[2], 2 * m + s)
                    split(2 * m + s, s, w_hi[s], w_lo[s])
            chunks = [2] * TILES_A + [1] * TILES_C + [2] * TILES_A + [1] * TILES_O
            for n in range(2, len(chunks)):
                t = OUT_TILE0 + n
                pool.wait_ge(proj_done[2], OUT_TILE0 + 1 + sum(chunks[:n - 1]))
                split(t, n % 2, w_hi[n % 2], w_lo[n % 2])
            for q in range(FFN_TILES):
                if q < 2:
                    pool.wait_ge(proj_done[2], OUT_TILE0 + 1 + 31 + q)
                split(MIX_TILES + q, q, wf_hi[q], wf_lo[q])
            with pool.Fori(1, FFN_STEPS) as s:
                frees = [(f_done[0], 3 * s - 1), (f_done[1], 3 * s - 1), (f_done[2], 3 * s), (f_done[3], 3 * s),
                         (f_done[7], 6 * s), (f_done[7], 6 * s)]
                for q in range(FFN_TILES):
                    pool.wait_ge(*frees[q])
                    split(FFN_TILES * s + (MIX_TILES + q), q, wf_hi[q], wf_lo[q])

        @block.tensor
        def _(pe):
            mm = nc.tensor.matmul

            def split_product(out, w_pair, x_pair, first, last):
                mm(out, w_pair[0], x_pair[0], start=first, stop=False)
                mm(out, w_pair[0], x_pair[1], start=False, stop=False)
                return mm(out, w_pair[1], x_pair[0], start=False, stop=last)

            def projection(use, ws, xs, cols, made=None, pieces=(0, 1, 2)):
                for b in pieces:
                    a, e, _ = PIECES[b]
                    if made:
                        pe.wait_ge(made, len(xs) * (b + 1))
                    pe.wait_ge(proj_free[b], use)
                    for k, (w, x) in enumerate(zip(ws, xs)):
                        ins = split_product(ps[b][:, 0:e - a], [w[0][:, cols[k]], w[1][:, cols[k]]],
                                            [x[0][:, a:e], x[1][:, a:e]], k == 0, k == len(ws) - 1)
                    ins.then_inc(proj_done[b], 1)

            h_pairs = [(h_hi[:, k, :], h_lo[:, k, :]) for k in range(KD)]

            def projection_tile(t, slot, made=None, pieces=(0, 1, 2)):
                pe.wait_ge(split_done, t + 1)
                projection(t + 1, [(w_hi[slot], w_lo[slot])] * KD, h_pairs,
                           [slice(k * P, k * P + P) for k in range(KD)], made, pieces)

            def mix_unit(units, it, j):
                b = units.bank(j)
                pe.wait_ge(mix_free[b], units.nth(it, j))
                return mix(b), mix_done[b]

            def ada_row_unit(units, it, j, slots, loads):
                out, done = mix_unit(units, it, j)
                for n, slot in enumerate(slots):
                    pe.wait_ge(ada_in[slot], loads)
                    for k in range(KD):
                        ins = mm(out[0:2, n * 256:(n + 1) * 256], csilu[:, k, :],
                                 ada_w[slot][:, k * 256:(k + 1) * 256], start=k == 0, stop=k == KD - 1)
                ins.then_inc(done, 1)

            def ada_turn_unit(units, it, j, rows, at, width):
                out, done = mix_unit(units, it, j)
                pe.wait_ge(ada_row_ready, rows)
                for q in range(width // P):
                    ins = mm(out[:, 2 * q:2 * q + 2], ada_row[0:2, at + q * P:at + (q + 1) * P],
                             ident[FILT_HID:FILT_HID + 2, FILT_HID:FILT_HID + 2],
                             start=True, stop=True)
                ins.then_inc(done, 1)

            pe.wait_ge(filt_in, 64)
            for j, (a, e, _) in enumerate(PIECES):
                out, done = mix_unit(u_setup, 0, j)
                mm(out[0:FILT_HID, 0:e - a], f_w1[:, :], feats[:, a:e], start=True, stop=True).then_inc(done, 1)
            for j, (a, e, _) in enumerate(PIECES):
                out, done = mix_unit(u_setup, 0, 3 + j)
                pe.wait_ge(sin_ready, j + 1)
                mm(out[0:FILT_HID, 0:e - a], f_w2[:, :], h1f[:, a:e], start=True, stop=True).then_inc(done, 1)
            pe.wait_ge(csilu_set, 1)
            pe.wait_ge(consts_in, 16)
            pe.wait_ge(consts_set, 3)
            for g in range(ADA_FIRST):
                ada_row_unit(u_setup, 0, 6 + 2 * g, [g % 2], 16 * (g // 2 + 1))
                ada_turn_unit(u_setup, 0, 7 + 2 * g, g + 1, g % 2 * 256, 256)
                for k in SQUARES_AT[g]:
                    pe.wait_ge(sq_ready, k + 1)
                    for b, (a, e, _) in enumerate(PIECES):
                        ins = mm(ps[b][:, 0:e - a], ones[:], (sq0, y0)[k % 2][:, a:e], start=k == 0,
                                 stop=k == KD - 1, skip_group_check=True)
                        if k == KD - 1:
                            ins.then_inc(proj_done[b], 1)
                    if k < KD - 1:
                        ins.then_inc(ms_ready, 1)
            def fwd_unit(units, it, j, block_j, imag, a_buf, mats):
                out, done = mix_unit(units, it, j)
                for s in range(4):
                    q = 4 * block_j + s
                    o = out[:, s * P:(s + 1) * P]
                    re, im = a_buf[:, q, :], a_buf[:, IMAG_AT[q], :] if HAS_IMAG[q] else None
                    terms = [(0, re), (1, im)] if not imag else [(2, re), (0, im)]
                    terms = [x for x in terms if x[1] is not None]
                    for n, (m, part) in enumerate(terms):
                        ins = mm(o, mats[:, q, m, :], part, start=n == 0, stop=n == len(terms) - 1)
                ins.then_inc(done, 1)

            pe.wait_ge(consts_in, 32)

            def taps_units(units, it, j0, loads):
                pe.wait_ge(w3_in, loads)
                for j in range(5):
                    out, done = mix_unit(units, it, j0 + j)
                    for s in range(2):
                        tile = 2 * j + s
                        ins = mm(out[:, s * 256:(s + 1) * 256], h2f[:, tile * P:(tile + 1) * P], w3[:, :],
                                 start=True, stop=True)
                    ins.then_inc(done, 1)

            def l1_pass(i, units, it, last):
                ada_row_unit(units, it, 0, range(2), 16 * i + 16 * (ADA_FIRST // 2 + 1))
                out, done = mix_unit(units, it, 1)
                pe.wait_ge(ss_ready, i + 1)
                mm(out[:, 0:2 * P], ones[:], ss_k[:, :, :], start=True, stop=True).then_inc(done, 1)
                pe.wait_ge(fa_ready, 2 * i + 1)
                for j in range(3):
                    fwd_unit(units, it, 2 + j, j, False, f_a, fwd_l1)
                if not last:
                    taps_units(units, it, 5, 16 * i + 32)
                projection_tile(2 * i + 1, 1)
                pe.wait_ge(fa_ready, 2 * i + 2)
                j0 = 5 if last else 10
                for j in range(3):
                    fwd_unit(units, it, j0 + j, j, True, f_a, fwd_l1)
                ada_turn_unit(units, it, j0 + 3, i + (ADA_FIRST + 1), 0, 512)
                if not last:
                    projection_tile(2 * i + 2, 0)

            projection_tile(0, 0, h_ready)
            taps_units(u_taps, 0, 0, 16)
            with pe.Fori(0, 7) as i:
                l1_pass(i, u1, i, False)
            l1_pass(7, u1_last, 0, True)

            def fnet_channels(c):
                pe.wait_ge(fn_const_in, 32)
                pe.wait_ge(fna_ready, c + 1)
                for j in range(5):
                    out, done = mix_unit(u2, c, FN1_UNIT + j)
                    for s in range(2):
                        f = 2 * j + s
                        o = out[:, s * 256:(s + 1) * 256]
                        if f >= NL:
                            terms = [(9 + f - NL, 1)]
                        else:
                            g = f if f <= 4 else 8 - f
                            terms = [(2 * g, 1)]
                            if 1 <= g <= 3:
                                terms.append((11 + 2 * g, 0 if f <= 4 else 2))
                        for n, (place, m) in enumerate(terms):
                            ins = mm(o, fn_a[:, place, :], fn_ch[:, m:m + 2, :], start=n == 0,
                                     stop=n == len(terms) - 1)
                    ins.then_inc(done, 1)

            def fnet_tokens(c):
                for j in range(5):
                    pe.wait_ge(mix_free[u2.bank(FN1_UNIT + j)], u2.nth(c, FN1_UNIT + j) + 1)
                for j in range(3):
                    out, done = mix_unit(u2, c, FN2_UNIT + j)
                    for f in range(4 * j, min(4 * j + 4, NT)):
                        for part in range(2):
                            ins = mm(out[:, (f % 4) * P:(f % 4 + 1) * P], fn_c[:, f, part, :],
                                     fn_t[:, f, part, :], start=part == 0, stop=part == 1)
                    ins.then_inc(done, 1)

            with pe.Fori(0, KD // 2) as m:
                for s in range(2):
                    n = 2 * m + s
                    projection_tile(2 * n + L2_TILE0, 0)
                    if s == 1:
                        fnet_tokens(m)
                    projection_tile(2 * n + (L2_TILE0 + 1), 1)
                    pe.wait_ge(xr_ready, n + 1)
                    pe.wait_ge(rpack_in[s], 16 * m + 16)
                    for j in range(12):
                        out, done = mix_unit(u2, m, RG_UNIT[s] + j)
                        a, e, _ = PIECES[j % 3]
                        mm(out[:, 0:e - a], rpack[s][:, (j // 3) * P:(j // 3 + 1) * P], xr[:, a:e],
                           start=True, stop=True).then_inc(done, 1)
                    if s == 0:
                        fnet_channels(m)

            pe.wait_ge(hy_const_in, 48)
            with pe.Fori(0, CH) as c:
                for order in range(2):
                    j0 = 14 * order
                    t = 6 * c + (L3_TILE0 + 3 * order)
                    slot = 3 * order % 2
                    if order == 0:
                        pe.wait_ge(v_in, 16 * c + 16)
                    else:
                        pe.wait_ge(z_ready, 2 * c + 1)
                    for j in range(3):
                        out, done = mix_unit(u3, c, j0 + j)
                        for tile in range(4 * j, min(4 * j + 4, NT)):
                            ins = nc.tensor.transpose(out[:, (tile % 4) * P:(tile % 4 + 1) * P],
                                                      (v_b, z_b)[order][:, tile * P:(tile + 1) * P], ident3[:, :])
                        ins.then_inc(done, 1)
                    projection_tile(t, slot)
                    pe.wait_ge(hya_ready, 2 * c + (order + 1))
                    for j in range(6):
                        fwd_unit(u3, c, j0 + 3 + j, j % 3, j >= 3, hy_a, fwd3)
                    projection_tile(t + 1, 1 - slot, pieces=(0, 1))
                    pe.wait_ge(y_ready, 2 * c + (order + 1))
                    for j in range(5):
                        out, done = mix_unit(u3, c, j0 + 9 + j)
                        if j < 4:
                            for s, q in enumerate(PAIRS[j]):
                                o = out[:, s * 256:(s + 1) * 256]
                                mm(o, hy_a[:, q, :], inv[:, q, 1:3, :], start=True, stop=False)
                                ins = mm(o, hy_a[:, FH + q, :], inv[:, q, 0:2, :], start=False, stop=True)
                        else:
                            for s, q in enumerate(SINGLES):
                                o = out[:, s * P:(s + 1) * P]
                                mm(o, hy_a[:, q, :], inv[:, q, 1, :], start=True, stop=False)
                                ins = mm(o, hy_a[:, FH + q, :], inv[:, q, 0, :], start=False, stop=True)
                        ins.then_inc(done, 1)
                    projection_tile(t + 1, 1 - slot, pieces=(2,))
                    projection_tile(t + 2, slot)

            z2_pairs = [(z2_hi[:, k, :], z2_lo[:, k, :]) for k in range(4)]
            use0 = OUT_TILE0 + 1

            def narrow_tiles(first_tile, first_use):
                with pe.Fori(0, 2) as m:
                    for s in range(2):
                        pe.wait_ge(split_done, 2 * m + (first_tile + s + 1))
                        for q in range(2):
                            projection(4 * m + (first_use + 2 * s + q), [(w_hi[s], w_lo[s])] * 4, z2_pairs,
                                       [slice((4 * q + k) * P, (4 * q + k + 1) * P) for k in range(4)])

            def wide_tile(t, use, slot):
                pe.wait_ge(split_done, t + 1)
                projection(use, [(w_hi[slot], w_lo[slot])] * KD, h_pairs,
                           [slice(k * P, k * P + P) for k in range(KD)])

            pe.wait_ge(z_split, 4)
            narrow_tiles(OUT_TILE0, use0)
            pe.wait_ge(z_split, 12)
            with pe.Fori(0, 4) as m:
                for s in range(2):
                    wide_tile(2 * m + (OUT_TILE0 + 4 + s), 2 * m + (use0 + 8 + s), s)
            pe.wait_ge(z_split, 16)
            narrow_tiles(OUT_TILE0 + 12, use0 + 16)
            pe.wait_ge(m_split, KD)

            for m in range(KD):
                wide_tile(OUT_TILE0 + 16 + m, use0 + 24 + m, m % 2)
            for p, (a, e, _) in enumerate(PIECES):
                b = NORM_BANKS[p]
                pe.wait_ge(mix_free[b], out_base[b])
                pe.wait_ge(sq_summed, 3 * (KD - 2) + p + 1)
                mm(mix(b)[:, 0:e - a], ones[:], sq_sum[:, a:e], start=True, stop=True).then_inc(mix_done[b], 1)

            for b in range(3):
                pe.wait_ge(proj_free[b], use0 + 32)
            for b in (0, 4):
                pe.wait_ge(mix_free[b], out_base[b])
            with pe.Fori(0, FFN_STEPS) as s:
                for j in range(2):
                    for p, (a, e, _) in enumerate(PIECES):
                        for up in range(2):
                            q = 2 * j + up
                            if p == 0:
                                pe.wait_ge(split_done, FFN_TILES * s + (MIX_TILES + q + 1))
                            if j == 0 and up == 0:
                                pe.wait_ge(h2_ready, KD * (p + 1))
                            n = 2 * (3 * j + p) + up
                            pe.wait_ge(f_free[n % 4], 3 * s + n // 4)
                            for k in range(KD):
                                ins = split_product(ps[n % 4][:, 0:e - a],
                                                    [wf_hi[q][:, k * P:(k + 1) * P], wf_lo[q][:, k * P:(k + 1) * P]],
                                                    [h_hi[:, k, a:e], h_lo[:, k, a:e]], k == 0, k == KD - 1)
                            ins.then_inc(f_done[n % 4], 1)
                pe.wait_ge(split_done, FFN_TILES * s + (MIX_TILES + FFN_TILES))
                for p, (a, e, _) in enumerate(PIECES):
                    pe.wait_ge(act_ready, 6 * s + (3 + p + 1))
                    for m in range(KD):
                        v = KD * p + m
                        b = 4 + v % 4
                        pe.wait_ge(f_free[b], 6 * s + v // 4)
                        for j in range(2):
                            ins = split_product(ps[b][:, 0:e - a],
                                                [wf_hi[4 + j][:, m * P:(m + 1) * P], wf_lo[4 + j][:, m * P:(m + 1) * P]],
                                                [act_hi[:, j, a:e], act_lo[:, j, a:e]], j == 0, j == 1)
                        ins.then_inc(f_done[b], 1)
            for p, (a, e, _) in enumerate(PIECES):
                pe.wait_ge(f_free[p], 3 * FFN_STEPS)
                pe.wait_ge(sq3_summed, (KD - 1) * (p + 1))
                mm(ps[p][:, 0:e - a], ones[:], sq_end_sum[p], start=True, stop=True).then_inc(ms3_ready, 1)

        @block.scalar
        def _(act):
            own = Chain(act, act_step)
            fn = nc.scalar.activation

            def take_mix(units, it, j):
                b = units.bank(j)
                act.wait_ge(mix_done[b], units.nth(it, j) + 1)
                return mix(b), mix_free[b]

            def mix_taken(units, it, j):
                act.wait_ge(mix_free[units.bank(j)], units.nth(it, j) + 1)

            def take_proj(use, b):
                act.wait_ge(proj_done[b], use + 1)
                return ps[b], proj_free[b]

            act.wait_ge(cvec_in, 16)
            fn(csilu[:], cvec[:], ACT.Silu).then_inc(csilu_set, 1)
            for j in range(6):
                a, e, _ = PIECES[j % 3]
                act.wait_ge(arg_ready, j + 1)
                fn((h1f if j < 3 else h2f[:, :])[:, a:e], arg[:, a:e], ACT.Sin).then_inc(sin_ready, 1)
            act.wait_ge(sp_ready, 1)
            fn(sp_w[:, 2, :], sp_w[:, 1, :], ACT.Exp).then_inc(sp_e, 1)
            act.wait_ge(sp_ready, 2)
            fn(sp_w[:, 4, :], sp_w[:, 3, :], ACT.Ln).then_inc(sp_l, 1)
            for g in range(ADA_FIRST):
                src, free = take_mix(u_setup, 0, 6 + 2 * g)
                if g > 1:
                    act.wait_ge(mod_ready, g - 1)
                fn(ada_row[0:2, g % 2 * 256:g % 2 * 256 + 256], src[0:2, 0:256], ACT.Copy).then_inc(own.sem, 1)
                own.n += 1
                own.settle()
                act.sem_inc(free, 1)
                act.sem_inc(ada_row_ready, 1)
                for k in SQUARES_AT[g]:
                    act.wait_ge(x_loaded[k], 16)
                    if k >= 2:
                        act.wait_ge(ms_ready, k - 1)
                    fn((sq0, y0)[k % 2][:], x_in[:, k, :], ACT.Square).then_inc(sq_ready, 1)
                if g == ADA_FIRST - 2:
                    act.wait_ge(consts_set, 3)
                    for b, (a, e, _) in enumerate(PIECES):
                        src, free = take_proj(0, b)
                        fn(rstd0[:, a:e], src[:, 0:e - a], ACT.Sqrt, bias=eps[:, 0:1],
                           scale=1.0 / D).then_inc(free, 1)

            def round_normed(u_at, shift_chunk, made, rounded):
                for p, (a, e, seq) in enumerate(PIECES):
                    for k in range(KD):
                        act.wait_ge(made, KD * p + k + 1)
                        fn(h_hi[:, k, a:e], u_at(k, a, e), ACT.Identity,
                           bias=mod[:, shift_chunk + k, seq:seq + 1]).then_inc(rounded, 1)

            round_normed(norm1_u, 0, u_ready, hi_ready)
            own.restart()

            act.wait_ge(hin_zero, 1)

            def into_padded(use, dst):
                for b, (a, e, seq) in enumerate(PIECES):
                    src, free = take_proj(use, b)
                    at = PAD_CTX if seq else PAD_LAT + a
                    fn(dst[:, at:at + e - a], src[:, 0:e - a], ACT.Copy).then_inc(free, 1)

            def taps_squares(i):
                act.wait_ge(taps_ready, i + 1)
                fn(f_a[:, 0:2 * NT, :], taps[:, :, :, :].rearrange("p n d c -> p (n d) c"),
                   ACT.Square).then_inc(taps_sq, 1)

            def l1_pass(i, units, it, last):
                src, free = take_mix(units, it, 0)
                act.wait_ge(mod_ready, i + ADA_FIRST)
                own(fn(ada_row[0:2, :], src[0:2, :], ACT.Copy))
                act.sem_inc(free, 1)
                act.sem_inc(ada_row_ready, 1)
                src, free = take_mix(units, it, 1)
                fn(rs_k[:, :, :], src[:, 0:2 * P].rearrange("p (s c) -> p s c", s=2), ACT.Sqrt,
                   bias=eps[:, 0:1]).then_inc(free, 1)
                act.wait_ge(hy_conved, 2 * i)
                into_padded(2 * i + 1, hin)
                act.wait_ge(hy_conved, 2 * i + 1)
                into_padded(2 * i + 2, hin)
                if not last:
                    act.wait_ge(mix_done[units.bank(12)], units.nth(it, 12) + 1)
                    taps_squares(i + 1)
                own.restart()

            taps_squares(0)
            with act.Fori(0, 7) as i:
                l1_pass(i, u1, i, False)
            l1_pass(7, u1_last, 0, True)

            act.wait_ge(hin_zero, 2)
            act.wait_ge(k_stored, 16 * 8)

            def take_fnet_channels(c):
                for j in range(5):
                    src, free = take_mix(u2, c, FN1_UNIT + j)
                    fn(fn_c[:, 2 * j:2 * j + 2, :, :].rearrange("p a b c -> p (a b c)"), src[:, 0:512],
                       ACT.Copy).then_inc(free, 1)

            def take_fnet_tokens(c):
                for j in range(3):
                    src, free = take_mix(u2, c, FN2_UNIT + j)
                    if j < 2:
                        dst = fn_y[:, 0:LAT].rearrange("p (f k) -> p k f", k=NL)[:, 4 * j:4 * j + 4, :]
                        src = src[:, 0:512].rearrange("p (k f) -> p k f", k=4)
                    else:
                        for q in range(2):
                            mix_taken(u2, c, FN2_UNIT + q)
                        dst = fn_y[:, LAT:T].rearrange("p (f k) -> p k f", k=NC)
                        src = src[:, 0:256].rearrange("p (k f) -> p k f", k=2)
                    fn(dst, src, ACT.Copy).then_inc(free, 1)

            with act.Fori(0, KD // 2) as m:
                for s in range(2):
                    n = 2 * m + s
                    act.wait_ge(xr_ready, n)
                    into_padded(2 * n + (L2_TILE0 + 1), rin)
                    if s == 1:
                        take_fnet_tokens(m)
                    act.wait_ge(zc_ready, n)
                    for b, (a, e, _) in enumerate(PIECES):
                        src, free = take_proj(2 * n + (L2_TILE0 + 2), b)
                        fn(g_ry[:, a:e], src[:, 0:e - a], ACT.Gelu_apprx_tanh).then_inc(free, 1)
                    act.wait_ge(zc_stored, 16 * n)
                    act.wait_ge(hy_stored, 16 * TILES_L1)
                    for j in range(12):
                        d, which = j // 6, j // 3 % 2
                        a, e, _ = PIECES[j % 3]
                        src, free = take_mix(u2, m, RG_UNIT[s] + j)
                        bias = (R_BR, R_BI)[which] + d
                        fn((r_b, i_b)[which][d][:, a:e], src[:, 0:e - a], ACT.Sigmoid,
                           bias=rpack[s][:, bias:bias + 1]).then_inc(free, 1)
                    for d in range(2):
                        for j in range(3):
                            mix_taken(u2, m, RG_UNIT[s] + 6 * d + j)
                        own.add(fn(a_b[d][:], r_b[d][:], ACT.Exp, scale=sp_neg[:, bass.ds(2 * n + d, 1)]))
                        own.add(fn(t_b[d][:], r_b[d][:], ACT.Tanh, scale=sp_pos[:, bass.ds(2 * n + d, 1)]))
                        own.settle()
                        fn(r_b[d][:], a_b[d][:], ACT.Square).then_inc(a2_ready, 1)
                    for d in range(2):
                        act.wait_ge(m2_ready, 2 * n + (d + 1))
                        fn(r_b[d][:], r_b[d][:], ACT.Sqrt).then_inc(root_ready, 1)
                    if s == 0:
                        take_fnet_channels(m)
                    own.restart()

            with act.Fori(0, CH) as c:
                for order in range(2):
                    j0 = 14 * order

                    def gate(g, pieces=(0, 1, 2)):
                        n = 3 * order + g
                        act.wait_ge(gate_stored, 96 * c + 16 * n)
                        for b in pieces:
                            a, e, _ = PIECES[b]
                            src, free = take_proj(6 * c + (L3_TILE0 + 1 + n), b)
                            fn(g_st[:, a:e], src[:, 0:e - a], ACT.Sigmoid).then_inc(free, 1)

                    act.wait_ge(z_ready, 2 * c + order)
                    for j in range(3):
                        src, free = take_mix(u3, c, j0 + j)
                        w = min(4, NT - 4 * j)
                        fn(ztok[:, 4 * j:4 * j + w, :].rearrange("p a c -> p (a c)"), src[:, 0:w * P],
                           ACT.Copy).then_inc(free, 1)
                    gate(0)
                    for j in range(6):
                        src, free = take_mix(u3, c, j0 + 3 + j)
                        fn(hy_z[:, 4 * j:4 * j + 4, :].rearrange("p a c -> p (a c)"), src[:],
                           ACT.Copy).then_inc(free, 1)
                    gate(1, (0, 1))
                    for j in range(5):
                        src, free = take_mix(u3, c, j0 + 9 + j)
                        fn(hy_z[:, 4 * j:4 * j + 4, :].rearrange("p a c -> p (a c)"), src[:],
                           ACT.Copy).then_inc(free, 1)
                    gate(1, (2,))
                    gate(2)

            use0 = OUT_TILE0 + 1
            for n in range(16):
                act.wait_ge(zraw_in[n % 2], 16 * (n // 2 + 1))
                if n == 12:
                    for b in range(3):
                        act.wait_ge(proj_done[b], use0 + 8)
                dst = h_hi[:, n - 4, :] if 4 <= n < 12 else z2_hi[:, n % 12, :]
                fn(dst, zraw[n % 2][:], ACT.Copy).then_inc(zhi_ready, 1)
            for b in range(3):
                act.wait_ge(proj_done[b], use0 + 16)
            for m in range(KD):
                act.wait_ge(side_used, KD + m + 1)
                fn(h_hi[:, m, :], x1[:, m, :], ACT.Copy).then_inc(mhi_ready, 1)
            for k in range(KD):
                for b, (a, e, _) in enumerate(PIECES):
                    act.wait_ge(proj_free[b], use0 + 24 + k + 1)
                    if k >= 2:
                        act.wait_ge(sq_summed, 3 * (k - 2) + b + 1)
                    fn((sq_o if k else sq_sum)[:, a:e], x1[:, k, a:e], ACT.Square).then_inc(sq1_ready, 1)
            for p, (a, e, _) in enumerate(PIECES):
                b = NORM_BANKS[p]
                act.wait_ge(mix_done[b], out_base[b] + 1)
                fn(mix(b)[:, 0:e - a], mix(b)[:, 0:e - a], ACT.Sqrt, bias=eps[:, 0:1],
                   scale=1.0 / D).then_inc(mix_free[b], 1)
            round_normed(norm2_u, 3 * KD, u2_ready, h2_hi)

            def up_bank(n):
                return (2 * n + 1) % 4, (2 * n + 1) // 4

            def ffn_step(s, first):
                for n in range(7):
                    if n < 6:
                        p = n % 3
                        a, e, _ = PIECES[p]
                        b = 2 * n % 4
                        act.wait_ge(f_done[b], 3 * s + (2 * n // 4 + 1))
                        if n >= 2 or not first:
                            pb, puse = up_bank((n - 2) % 6)
                            act.wait_ge(f_free[pb], 3 * s + (puse + 1 - (3 if n < 2 else 0)))
                        fn(sil[n % 2][:, 0:e - a], ps[b][:, 0:e - a], ACT.Silu).then_inc(f_free[b], 1)
                    if n >= 1:
                        q = n - 1
                        pb, puse = up_bank(q)
                        act.wait_ge(f_free[pb], 3 * s + (puse + 1))
                        a, e, _ = PIECES[q % 3]
                        if not first:
                            v = KD * (q % 3) + KD - 1
                            act.wait_ge(f_done[4 + v % 4], 6 * s + (v // 4 + 1 - 6))
                        fn(act_hi[:, q // 3, a:e], a32[q % 2][:, 0:e - a], ACT.Copy).then_inc(ahi_ready, 1)

            ffn_step(0, True)
            with act.Fori(1, FFN_STEPS) as s:
                ffn_step(s, False)
            act.wait_ge(split_done, N_TILES)
            for p, (a, e, _) in enumerate(PIECES):
                for k in range(KD):
                    v = KD * p + k
                    act.wait_ge(f_free[4 + v % 4], 6 * (FFN_STEPS - 1) + v // 4 + 1)
                    if k >= 3:
                        act.wait_ge(sq3_summed, (KD - 1) * p + k - 2)
                    elif k:
                        act.wait_ge(sq3_summed, (KD - 1) * p)
                    dst = sq_end[k % 2][:, 0:e - a] if k else sq_end_sum[p]
                    fn(dst, x1[:, k, a:e], ACT.Square).then_inc(sq3_ready, 1)
            for p, (a, e, _) in enumerate(PIECES):
                act.wait_ge(ms3_ready, p + 1)
                fn(ps[p][:, 0:e - a], ps[p][:, 0:e - a], ACT.Sqrt, bias=eps[:, 0:1],
                   scale=1.0 / D).then_inc(root3_ready, 1)

        @block.vector
        def _(dve):
            own = Chain(dve, dve_step)
            bf = Butterfly(dve, own)
            tt, ts, stt = nc.vector.tensor_tensor, nc.vector.tensor_scalar, nc.vector.scalar_tensor_tensor

            def take_mix(units, it, j):
                b = units.bank(j)
                dve.wait_ge(mix_done[b], units.nth(it, j) + 1)
                return mix(b), mix_free[b]

            def mix_taken(units, it, j):
                dve.wait_ge(mix_free[units.bank(j)], units.nth(it, j) + 1)

            def proj_taken(use):
                for b in range(3):
                    dve.wait_ge(proj_free[b], use + 1)

            dve.wait_ge(filt_in, 64)
            for j in range(6):
                a, e, _ = PIECES[j % 3]
                src, free = take_mix(u_setup, 0, j)
                if j >= 3:
                    dve.wait_ge(sin_ready, j - 2)
                layer = j // 3
                x, n = arg[:, a:e], turns[:, a:e]
                ts(x, src[0:FILT_HID, 0:e - a], f_vec[:, layer:layer + 1], f_vec[:, 2:3], ALU.add,
                   ALU.mult).then_inc(free, 1)
                dve.wait_ge(free, u_setup.nth(0, j) + 1)
                own(ts(n, x, 1.0 / (2 * math.pi), ROUND, ALU.mult, ALU.add))
                own(ts(n, n, ROUND, None, ALU.subtract))
                for part in TWO_PI:
                    own(stt(x, n, -part, x, ALU.mult, ALU.add))
                ts(x, x, PI_BELOW, -PI_BELOW, ALU.min, ALU.max).then_inc(arg_ready, 1)
            dve.wait_ge(vec_in, 16)
            lam = vec[:, V_LAM:V_LAM + 16]
            w = [sp_w[:, n, :] for n in range(6)]
            own(ts(w[0], lam, -1.0, None, ALU.mult))
            own(tt(w[1], lam, w[0], ALU.min))
            own(ts(w[0], w[0], 0.0, None, ALU.max))
            dve.sem_inc(sp_ready, 1)
            dve.wait_ge(sp_e, 1)
            own(ts(w[3], w[2], 1.0, None, ALU.add))
            dve.sem_inc(sp_ready, 1)
            own(ts(w[5], w[3], 1.0, None, ALU.subtract))
            own(ts(sp_pos[:], w[5], 0.0, None, ALU.is_equal))
            own(tt(w[5], w[5], sp_pos[:], ALU.add))
            own(nc.vector.reciprocal(w[5], w[5]))
            dve.wait_ge(sp_l, 1)
            own(tt(w[4], w[4], sp_pos[:], ALU.add))
            own(tt(w[4], w[4], w[5], ALU.mult))
            own(tt(w[4], w[4], w[2], ALU.mult))
            own(tt(w[4], w[4], w[0], ALU.add))
            own(ts(sp_pos[:], w[4], RG_C, None, ALU.mult))
            own(ts(sp_neg[:], w[4], -RG_C, None, ALU.mult))

            def ada_add(units, it, j, group, n):
                src, free = take_mix(units, it, j)
                tt(mod[:, bass.ds(2 * group, n), :], src[:, 0:2 * n].rearrange("p (a b) -> p a b", a=n),
                   vec[:, bass.ds(2 * group + V_BADA, n)].unsqueeze(2).to_broadcast([P, n, 2]),
                   ALU.add).then_inc(free, 1)
                dve.wait_ge(free, units.nth(it, j) + 1)
                dve.sem_inc(mod_ready, 1)

            for g in range(ADA_FIRST):
                ada_add(u_setup, 0, 7 + 2 * g, g, 2)
                if g == ADA_FIRST - 2:
                    for p, (a, e, _) in enumerate(PIECES):
                        dve.wait_ge(proj_free[p], 1)
                        own(nc.vector.reciprocal(rstd0[:, a:e], rstd0[:, a:e]))

            def norm_scale(gain, scale_chunk):
                for s in range(2):
                    own(stt(norm_a[:, :, s], mod[:, scale_chunk:scale_chunk + KD, s], 1.0,
                            vec[:, gain:gain + KD], ALU.add, ALU.mult))

            def norm_piece(p, x, root, u_at, shift_chunk, made, rounded, ready):
                a, e, seq = PIECES[p]
                for k in range(KD + 1):
                    if k < KD:
                        if KD * p + k >= 2:
                            dve.wait_ge(ready, KD * p + k - 1)
                        stt(u_at(k, a, e), x[:, k, a:e], norm_a[:, k, seq:seq + 1], root, ALU.mult,
                            ALU.mult).then_inc(made, 1)
                    if k:
                        dve.wait_ge(rounded, KD * p + k)
                        stt(h_lo[:, k - 1, a:e], u_at(k - 1, a, e), mod[:, shift_chunk + k - 1, seq:seq + 1],
                            h_hi[:, k - 1, a:e].bitcast(F32), ALU.add, ALU.subtract).then_inc(ready, 1)

            norm_scale(V_N1, KD)
            for p, (a, e, _) in enumerate(PIECES):
                norm_piece(p, x_in, rstd0[:, a:e], norm1_u, 0, u_ready, hi_ready, h_ready)
            dve.wait_ge(h_ready, 3 * KD)
            own.settle()
            for a, e in ((0, PAD_LAT), (PAD_LAT + LAT, PAD_CTX), (PAD_CTX + CTX, PAD_T)):
                own(nc.vector.memset(hin[:, a:e], 0.0))
            dve.sem_inc(hin_zero, 1)
            own.restart()

            def depthwise(out, src, taps_at, bias, count, left, last_sem):
                for a, e, seq in SEQS:
                    at = (PAD_CTX if seq else PAD_LAT) - left
                    own.add(ts(out[:, a:e], src[:, at:at + e - a], taps_at(0), bias, ALU.mult, ALU.add))
                own.settle()
                for k in range(1, count):
                    for a, e, seq in SEQS:
                        at = (PAD_CTX if seq else PAD_LAT) - left + k
                        own.add(stt(out[:, a:e], src[:, at:at + e - a], taps_at(k), out[:, a:e],
                                    ALU.mult, ALU.add))
                    own.settle()
                dve.sem_inc(last_sem, 1)

            def first_stage(src, dst, tmp):
                out = spectrum_places(dst)
                real_dft_even(bf, places(src, P), places(tmp, P), out)
                real_dft_odd(bf, places(src, P), places(tmp, P), out)
                real_dft_context(bf, places(src, P, NL), out)
                own.settle()

            def take_k(i, units, it, unit, j, imag):
                if not imag and j == 0:
                    dve.wait_ge(k_stored, 16 * i)
                src, free = take_mix(units, it, unit)
                base = FH * imag + 4 * j
                v = src[:, :].rearrange("p (a c) -> p a c", a=4)
                cuts = [(0, 4, 0)] if j < 2 else [(0, 1, 0), (1, 4, 1)]
                for n, (a, e, seq) in enumerate(cuts):
                    ins = tt(kstage[:, base + a:base + e, :], v[:, a:e, :],
                             rs_k[:, seq, :].unsqueeze(1).to_broadcast([P, e - a, P]), ALU.mult)
                    if n < len(cuts) - 1:
                        own(ins)
                ins.then_inc(free, 1)

            def make_taps(units, it, j0, loads):
                dve.wait_ge(decay_in, loads)
                for j in range(5):
                    src, free = take_mix(units, it, j0 + j)
                    for s in range(2):
                        tile = 2 * j + s
                        ins = tt(taps[:, tile, :, :], src[:, 256 * s:256 * s + 256].rearrange("p (d c) -> p d c", d=2),
                                 decay[:, tile, :].unsqueeze(1).to_broadcast([P, 2, P]), ALU.mult)
                        if s == 0:
                            own(ins)
                    ins.then_inc(free, 1)
                for j in range(5):
                    mix_taken(units, it, j0 + j)
                own(nc.vector.memset(taps[0:1, 0, 1, :], 0.0))
                own(nc.vector.memset(taps[0:1, NL, 1, :], 0.0))
                dve.sem_inc(taps_ready, 1)

            def l1_pass(i, units, it, last):
                own(tt(tsum[:, :, :], taps[:, :, 0, :], taps[:, :, 1, :], ALU.add))
                dve.wait_ge(taps_sq, i + 1)
                for seq, (a, e) in enumerate(((0, 2 * NL), (2 * NL, 2 * NT))):
                    own(nc.vector.tensor_reduce(ss_k[:, seq, :], f_a[:, a:e, :].rearrange("p n c -> p c n"),
                                                AX_X, ALU.add))
                dve.sem_inc(ss_ready, 1)
                first_stage(tsum, f_a, f_t)
                dve.sem_inc(fa_ready, 1)
                own(tt(tsum[:, :, :], taps[:, :, 0, :], taps[:, :, 1, :], ALU.subtract))
                mix_taken(units, it, 1)
                own(nc.vector.reciprocal(rs_k[:, :, :], rs_k[:, :, :]))
                for j in range(3):
                    take_k(i, units, it, 2 + j, j, 0)
                for j in range(3):
                    mix_taken(units, it, 2 + j)
                first_stage(tsum, f_a, f_t)
                dve.sem_inc(fa_ready, 1)
                j0 = 5 if last else 10
                if not last:
                    make_taps(units, it, 5, 16 * i + 32)
                for j in range(3):
                    take_k(i, units, it, j0 + j, j, 1)
                ada_add(units, it, j0 + 3, 2 * i + ADA_FIRST, 4)
                for j in range(3):
                    mix_taken(units, it, j0 + j)
                dve.sem_inc(k_ready, 1)
                tile = 2 * i + 1
                proj_taken(tile + 1)
                dve.wait_ge(hy_stored, 16 * tile)
                depthwise(hout, hin, lambda k: vec[:, bass.ds(4 * tile + (V_HY + k), 1)],
                          vec[:, bass.ds(4 * tile + (V_HY + 3), 1)], 3, 1, hy_conved)
                own.restart()

            make_taps(u_taps, 0, 0, 16)
            own.restart()
            with dve.Fori(0, 7) as i:
                l1_pass(i, u1, i, False)
            l1_pass(7, u1_last, 0, True)

            for a, e in ((0, PAD_LAT), (PAD_LAT + LAT, PAD_CTX), (PAD_CTX + CTX, PAD_T)):
                own(nc.vector.memset(rin[:, a:e], 0.0))
            dve.sem_inc(hin_zero, 1)
            own.restart()

            def fnet_first_stage(c):
                dve.wait_ge(fn_in, 16 * c + 16)
                out = spectrum_places(fn_a)
                real_dft_even(bf, places(fn_u, P), places(fn_tmp, P), out)
                bf.add(fn_a[:, 9, :], fn_u[:, NL, :], fn_u[:, NL + 1, :])
                bf.sub(fn_a[:, 10, :], fn_u[:, NL, :], fn_u[:, NL + 1, :])
                own.settle()
                dve.sem_inc(fna_ready, 1)

            with dve.Fori(0, KD // 2) as m:
                for s in range(2):
                    n = 2 * m + s
                    proj_taken(2 * n + (L2_TILE0 + 1))
                    dve.wait_ge(rpack_in[s], 16 * m + 16)
                    pack = rpack[s]
                    depthwise(xr, rin, lambda k: pack[:, R_CONV + k:R_CONV + k + 1],
                              pack[:, R_CONVB:R_CONVB + 1], 4, 2, xr_ready)
                    if s == 0:
                        fnet_first_stage(m)
                    for d in range(2):
                        for j in range(3):
                            mix_taken(u2, m, RG_UNIT[s] + 6 * d + 3 + j)
                        own.add(tt(i_b[d][:], i_b[d][:], xr[:], ALU.mult))
                        dve.wait_ge(a2_ready, 2 * n + (d + 1))
                        stt(r_b[d][:], r_b[d][:], 1.0, t_b[d][:], ALU.add, ALU.mult).then_inc(m2_ready, 1)
                    for d in range(2):
                        dve.wait_ge(root_ready, 2 * n + (d + 1))
                        first = LAT if d == 0 else T - 1
                        own(nc.vector.memset(r_b[d][:, first:first + 1], 1.0))
                        own(tt(i_b[d][:], r_b[d][:], i_b[d][:], ALU.mult))
                        for a, e, seq in SEQS:
                            step = slice(a, e) if d == 0 else (slice(e - 1, a - 1, -1) if a else slice(e - 1, None, -1))
                            start = 0.0 if seq else pack[:, R_ST + d:R_ST + d + 1]
                            own.add(nc.vector.tensor_tensor_scan(t_b[d][:, step], a_b[d][:, step], i_b[d][:, step],
                                                                 start, ALU.mult, ALU.add))
                    own.settle()
                    own.add(nc.vector.tensor_copy(fin[:, bass.ds(n, 1), 0], t_b[0][:, T - 1:T]))
                    own.add(nc.vector.tensor_copy(fin[:, bass.ds(n, 1), 1], t_b[1][:, LAT:LAT + 1]))
                    own(tt(r_b[0][:], t_b[0][:], t_b[1][:], ALU.add))
                    proj_taken(2 * n + (L2_TILE0 + 2))
                    own(tt(r_b[0][:], r_b[0][:], g_ry[:], ALU.mult))
                    dve.sem_inc(zc_ready, 1)
                    own.restart()

            with dve.Fori(0, CH) as c:
                for order in range(2):
                    j0 = 14 * order
                    for j in range(3):
                        mix_taken(u3, c, j0 + j)
                    first_stage(ztok, hy_a, hy_z)
                    dve.sem_inc(hya_ready, 1)
                    for j in range(6):
                        mix_taken(u3, c, j0 + 3 + j)
                    dve.wait_ge(k_in, 32 * c + 16 * (order + 1))
                    re, im = slice(0, FH), slice(FH, 2 * FH)
                    own.add(tt(hy_a[:, re, :], hy_z[:, re, :], hy_k[:, re, :], ALU.mult))
                    own.add(tt(ztok[:, :, :], hy_z[:, im, :], hy_k[:, im, :], ALU.mult))
                    own(tt(hy_a[:, im, :], hy_z[:, re, :], hy_k[:, im, :], ALU.mult))
                    own(tt(hy_a[:, re, :], hy_a[:, re, :], ztok[:, :, :], ALU.subtract))
                    own(tt(ztok[:, :, :], hy_z[:, im, :], hy_k[:, re, :], ALU.mult))
                    own(tt(hy_a[:, im, :], hy_a[:, im, :], ztok[:, :, :], ALU.add))
                    dve.sem_inc(y_ready, 1)
                    for j in range(5):
                        mix_taken(u3, c, j0 + 9 + j)
                    b_at = inverse_places(hy_z)
                    inverse_latent(bf, b_at, places(hy_a, P), places(ztok, P))
                    inverse_context(bf, b_at, places(hy_a, P), places(ztok, P, NL))
                    own.settle()
                    dve.wait_ge(xg_in, 32 * c + 16 * (order + 1))
                    if order == 0:
                        dve.wait_ge(hbias_in, 16 * c + 16)
                        dve.wait_ge(v_in, 16 * c + 16)
                        dve.wait_ge(za_stored, 16 * c)
                    y = ztok[:, 0:NT, :].rearrange("p a c -> p (a c)")
                    own(stt(z_b[:], (v_b, z_b)[order][:], hbias[:, order:order + 1], y, ALU.mult, ALU.add))
                    own(tt(z_b[:], z_b[:], x_b[:], ALU.mult))
                    dve.sem_inc(z_ready, 1)
                own.restart()

            use0 = OUT_TILE0 + 1

            def split_z(n):
                dve.wait_ge(zhi_ready, n + 1)
                if 4 <= n < 12:
                    hi, lo = h_hi[:, n - 4, :], h_lo[:, n - 4, :]
                else:
                    hi, lo = z2_hi[:, n % 12, :], z2_lo[:, n % 12, :]
                tt(lo, zraw[n % 2][:], hi.bitcast(F32), ALU.subtract).then_inc(z_split, 1)

            def take_branch(job, m):
                dve.wait_ge(side_in[job % 2], 16 * (job // 2 + 1))
                for b, (a, e, _) in enumerate(PIECES):
                    dve.wait_ge(proj_done[b], use0 + job + 1)
                    dst = x1[:, m, a:e] if job < 8 else side[job % 2][:, a:e]
                    tt(dst, ps[b][:, 0:e - a], side[job % 2][:, a:e], ALU.mult).then_inc(proj_free[b], 1)
                if job >= 8:
                    proj_taken(use0 + job)
                    tt(x1[:, m, :], x1[:, m, :], side[job % 2][:], ALU.add).then_inc(side_used, 1)

            def split_merged(m):
                dve.wait_ge(mhi_ready, m + 1)
                tt(h_lo[:, m, :], x1[:, m, :], h_hi[:, m, :].bitcast(F32), ALU.subtract).then_inc(m_split, 1)

            for n in range(4):
                split_z(n)
            for n in range(4, 12):
                split_z(n)
                take_branch(n - 4, n - 4)
            for n in range(12, 16):
                split_z(n)
            for m in range(KD):
                if m == 0:
                    proj_taken(use0 + 7)
                take_branch(8 + m, m)
            for m in range(KD):
                if m == 0:
                    dve.wait_ge(side_used, KD)
                take_branch(16 + m, m)
                if m:
                    split_merged(m - 1)
            split_merged(KD - 1)
            dve.wait_ge(m_split, KD)

            def add_square(k, b):
                a, e, _ = PIECES[b]
                dve.wait_ge(sq1_ready, 3 * k + b + 1)
                if k >= 2:
                    dve.wait_ge(sq_summed, 3 * (k - 2) + b + 1)
                tt(sq_sum[:, a:e], sq_sum[:, a:e], sq_o[:, a:e], ALU.add).then_inc(sq_summed, 1)

            for m in range(KD):
                job = 24 + m
                dve.wait_ge(side_in[job % 2], 16 * (job // 2 + 1))
                for b, (a, e, seq) in enumerate(PIECES):
                    dve.wait_ge(proj_done[b], use0 + job + 1)
                    stt(x1[:, m, a:e], ps[b][:, 0:e - a], mod[:, 2 * KD + m, seq:seq + 1], side[job % 2][:, a:e],
                        ALU.mult, ALU.add).then_inc(proj_free[b], 1)
                    if m >= 2:
                        add_square(m - 1, b)
            for b in range(3):
                add_square(KD - 1, b)
            norm_scale(V_N2, 4 * KD)
            for p, (a, e, _) in enumerate(PIECES):
                b = NORM_BANKS[p]
                dve.wait_ge(mix_free[b], out_base[b] + 1)
                own(nc.vector.reciprocal(mix(b)[:, 0:e - a], mix(b)[:, 0:e - a]))
                norm_piece(p, x1, mix(b)[:, 0:e - a], norm2_u, 3 * KD, u2_ready, h2_hi, h2_ready)
            own.restart()

            def gated_unit(s, n):
                a, e, _ = PIECES[n % 3]
                gb, gn = 2 * n % 4, 2 * n // 4
                ub, un = (2 * n + 1) % 4, (2 * n + 1) // 4
                dve.wait_ge(f_free[gb], 3 * s + (gn + 1))
                dve.wait_ge(f_done[ub], 3 * s + (un + 1))
                if n >= 2:
                    dve.wait_ge(act_ready, 6 * s + (n - 1))
                tt(a32[n % 2][:, 0:e - a], sil[n % 2][:, 0:e - a], ps[ub][:, 0:e - a],
                   ALU.mult).then_inc(f_free[ub], 1)

            def gated_remainder(s, n):
                a, e, _ = PIECES[n % 3]
                dve.wait_ge(ahi_ready, 6 * s + (n + 1))
                tt(act_lo[:, n // 3, a:e], a32[n % 2][:, 0:e - a], act_hi[:, n // 3, a:e].bitcast(F32),
                   ALU.subtract).then_inc(act_ready, 1)

            def add_square_end(p, k):
                dve.wait_ge(sq3_ready, KD * p + k + 1)
                if k >= 2:
                    dve.wait_ge(sq3_summed, (KD - 1) * p + k - 1)
                a, e, _ = PIECES[p]
                tt(sq_end_sum[p], sq_end_sum[p], sq_end[k % 2][:, 0:e - a], ALU.add).then_inc(sq3_summed, 1)

            def ffn_step(s, last):
                for n in range(7):
                    if n < 6:
                        gated_unit(s, n)
                    if n:
                        gated_remainder(s, n - 1)
                dve.wait_ge(act_ready, 6 * s + 6)
                for p, (a, e, seq) in enumerate(PIECES):
                    for m in range(KD):
                        v = KD * p + m
                        b = 4 + v % 4
                        dve.wait_ge(f_done[b], 6 * s + (v // 4 + 1))
                        stt(x1[:, m, a:e], ps[b][:, 0:e - a], mod[:, 5 * KD + m, seq:seq + 1], x1[:, m, a:e],
                            ALU.mult, ALU.add).then_inc(f_free[b], 1)
                        if last and m >= 2:
                            add_square_end(p, m - 1)
                    if last:
                        add_square_end(p, KD - 1)

            with dve.Fori(0, FFN_STEPS - 1) as s:
                ffn_step(s, False)
            ffn_step(FFN_STEPS - 1, True)
            for p, (a, e, _) in enumerate(PIECES):
                dve.wait_ge(root3_ready, p + 1)
                root = ps[p][:, 0:e - a]
                own(nc.vector.reciprocal(root, root))
                for k in range(KD):
                    stt(x1[:, k, a:e], x1[:, k, a:e], vec[:, V_FG + k:V_FG + k + 1], root, ALU.mult,
                        ALU.mult).then_inc(y_out, 1)


def dft_constants():
    f64 = np.float64
    p = np.arange(P, dtype=f64)
    fwd = np.zeros((P, FH, 3, P))
    inv = np.zeros((P, FH, 3, P))
    for q in range(FH):
        n, f1 = (2 * LAT, q) if q < 9 else (2 * CTX, q - 9)
        radix = n // P
        angle = 2 * np.pi * np.outer(p, f1 + radix * p) / n
        fwd[:, q] = np.stack([np.cos(angle), np.sin(angle), -np.sin(angle)], axis=1)
        weight = (1.0 if f1 in (0, radix // 2) else 2.0) / n
        back = angle.T
        inv[:, q] = weight * np.stack([-np.sin(back), np.cos(back), np.sin(back)], axis=1)
    angle = 2 * np.pi * np.outer(p, p) / P
    fn_ch = np.stack([np.sin(angle), np.cos(angle), -np.sin(angle), -np.cos(angle)], axis=1)
    fn_t = np.zeros((P, NT, 2, P))
    for m in range(NT):
        length, f1 = (LAT, m) if m < NL else (CTX, m - NL)
        radix = length // P
        angle = 2 * np.pi * np.outer(p, f1 + radix * p) / length
        fn_t[:, m] = np.stack([np.cos(angle), np.sin(angle)], axis=1) / np.sqrt(length * P)
    return [a.astype(np.float32) for a in (fwd, inv, fn_ch, fn_t)]


def filter_constants():
    f32 = np.float32
    feats, windows = [], []
    deltas = np.linspace(-math.log(1e-2) / 1.5, -math.log(1e-2) / 0.3, D_HY).astype(f32)
    for length in (LAT, CTX):
        t = np.arange(length, dtype=f32) / f32(length)
        ang = f32(2.0 * math.pi) * t[:, None] * np.arange(1, 9, dtype=f32)
        feats.append(np.concatenate([t[:, None], np.sin(ang), np.cos(ang)], axis=-1).T)
        window = np.exp(-t[:, None] * deltas)
        windows.append(window.reshape(length // P, P, CH, P).transpose(2, 1, 0, 3))
    decay = np.concatenate(windows, axis=2).astype(f32)
    return np.concatenate(feats, axis=1).astype(f32), np.concatenate([decay, decay], axis=0)


def columns(v):
    return np.ascontiguousarray(v.reshape(-1, P).T)


def tiles(w):
    n = w.shape[1] // P
    return w.reshape(KD, P, n, P).transpose(2, 1, 0, 3).reshape(n, P, D)


def kernel(x_prompt, x_sample, c, state_rglru, c_ctx, norm1_g, norm2_g, w_ada, b_ada, w_in,
           hy_conv_w, hy_conv_b, hy_f_w1, hy_f_b1, hy_f_w2, hy_f_b2, hy_f_w3, hy_f_freq, hy_bias,
           w_a, w_b, rg_conv_w, rg_conv_b, rg_wr, rg_br, rg_wi, rg_bi, rg_lam, w_c, w_o,
           w_gu, w_down, final_g):
    import concourse.bacc as bacc
    from concourse.bass_utils import run_bass_kernel_spmd

    fwd, inv, fn_ch, fn_t = dft_constants()
    feats, decay = filter_constants()

    tokens = np.concatenate([np.asarray(x_sample)[0], np.asarray(x_prompt)[0]], axis=0)
    cond = np.stack([np.asarray(c)[0], np.asarray(c_ctx)])

    t_in = tiles(np.asarray(w_in)[0])
    order = list(range(16)) + [x for n in range(8) for x in (16 + n, 24 + n)] + list(range(32, 56))
    def narrow(w):
        return w.reshape(4, P, 4, 2, P).transpose(2, 1, 3, 0, 4).reshape(4, P, D)
    t_gu, t_down = tiles(np.asarray(w_gu)[0]), np.asarray(w_down)[0].reshape(FF, P, D)
    ffn = [x for s in range(FFN_STEPS) for x in
           (t_gu[2 * s], t_gu[FF + 2 * s], t_gu[2 * s + 1], t_gu[FF + 2 * s + 1], t_down[2 * s], t_down[2 * s + 1])]
    weights = np.concatenate([t_in[order], narrow(np.asarray(w_b)[0]), tiles(np.asarray(w_c)[0]),
                              narrow(np.asarray(w_a)[0]), tiles(np.asarray(w_o)[0]), np.stack(ffn)], axis=0)

    hy = np.concatenate([np.asarray(hy_conv_w)[0], np.asarray(hy_conv_b)], axis=0)
    hy = hy.reshape(4, 12, P).transpose(2, 1, 0)
    plain = np.broadcast_to(np.array([0, 1, 0, 0], np.float32), (P, 4, 4))
    hy = np.concatenate([hy, plain], axis=1).reshape(P, 64)
    lam = np.asarray(rg_lam)[0].reshape(2, KD, P).transpose(2, 1, 0).reshape(P, 16)
    vec = np.concatenate([columns(np.asarray(norm1_g)[0]), columns(np.asarray(norm2_g)[0]),
                          columns(np.asarray(final_g)), columns(np.asarray(b_ada)[0]), hy, lam], axis=1)

    wr, wi = np.asarray(rg_wr)[0], np.asarray(rg_wi)[0]
    mats = np.stack([wr[0], wi[0], wr[1], wi[1]], axis=0).transpose(1, 2, 0, 3).reshape(KD, P, 4 * P)
    per_chunk = [np.asarray(rg_conv_w)[0], np.asarray(rg_conv_b), np.asarray(rg_br)[0], np.asarray(rg_bi)[0],
                 np.asarray(state_rglru)[0, 0]]
    vectors = np.concatenate(per_chunk, axis=0).reshape(-1, KD, P).transpose(1, 2, 0)
    rpack = np.concatenate([mats, vectors], axis=2)

    w3 = np.asarray(hy_f_w3)[0].reshape(FILT_HID, 2, 2, CH, P).transpose(1, 3, 0, 2, 4).reshape(8, FILT_HID, 2 * P)
    arrays = {
        "x": tokens.T.reshape(KD, P, T),
        "cvec": cond.reshape(2, KD, P).transpose(2, 1, 0),
        "w_ada": np.asarray(w_ada)[0].reshape(KD, P, HALF_GROUPS, 256).transpose(2, 1, 0, 3)
                 .reshape(HALF_GROUPS, P, KD * 256),
        "weights": weights,
        "vec": vec,
        "rpack": rpack,
        "f_w1": np.asarray(hy_f_w1)[0],
        "f_w2": np.asarray(hy_f_w2)[0],
        "f_vec": np.stack([np.asarray(hy_f_b1)[0], np.asarray(hy_f_b2)[0], np.asarray(hy_f_freq)[0]], axis=1),
        "w3": w3,
        "hbias": np.asarray(hy_bias)[0].reshape(2, CH, P).transpose(1, 2, 0),
        "feats": feats,
        "decay": decay,
        "ident": np.eye(P, dtype=np.float32),
        "fwd": fwd,
        "inv": inv,
        "fn_ch": fn_ch,
        "fn_t": fn_t,
    }
    arrays = {k: np.ascontiguousarray(v) for k, v in arrays.items()}
    nc = bacc.Bacc("TRN2", target_bir_lowering=False, num_devices=1)
    dr = {k: nc.dram_tensor(f"in_{k}", v.shape, F32, kind="ExternalInput").ap() for k, v in arrays.items()}
    for name, shape in (("y", (P, KD, T)), ("state_out", (P, KD, 2))):
        dr[name] = nc.dram_tensor(f"out_{name}", shape, F32, kind="ExternalOutput").ap()
    for name, shape in SCRATCH:
        dr[name] = nc.dram_tensor(f"scratch_{name}", shape, F32).ap()
    build_program(nc, dr)
    got = run_bass_kernel_spmd(nc, [{f"in_{k}": v for k, v in arrays.items()}], core_ids=[0]).results[0]
    y = got["out_y"].transpose(1, 0, 2).reshape(D, T).T
    state = got["out_state_out"].transpose(2, 1, 0).reshape(1, 1, 2, D)
    return (np.ascontiguousarray(y[LAT:])[None], np.ascontiguousarray(y[:LAT])[None], np.ascontiguousarray(state))
```

```python
import math
from contextlib import ExitStack

import numpy as np

import concourse.bass as bass
from concourse import mybir

F32 = mybir.dt.float32
F32R = mybir.dt.float32r
ALU = mybir.AluOpType
ACT = mybir.ActivationFunctionType
AX_X = mybir.AxisListType.X

P = 128
D = 1024
KD = D // P
LAT, CTX = 1024, 256
T = LAT + CTX
NL, NC = LAT // P, CTX // P
NT = NL + NC
PIECES = [(0, 512, 0), (512, 1024, 0), (1024, 1280, 1)]
SEQS = [(0, LAT, 0), (LAT, T, 1)]
D_HY = 512
CH = D_HY // P
D_FF = 2816
FF = D_FF // P
EPS = 1e-6
RG_C = 8.0
FILT_EMB, FILT_HID = 17, 64
FH = 9 + 3
PAD_LAT, PAD_CTX, PAD_T = 2, 2 + LAT + 2, 2 + LAT + 2 + CTX + 2
HALF_GROUPS = 24
ADA_FIRST = 8
SQUARES_AT = ((0,), (1, 2), (3, 4), (5,), (6,), (7,), (), ())
FIRST_MIX = 3
MIX_BANKS = 5

V_N1, V_N2, V_FG, V_BADA = 0, KD, 2 * KD, 3 * KD
V_HY = V_BADA + 48
V_LAM = V_HY + 64
V_ALL = V_LAM + 2 * KD
R_CONV, R_CONVB, R_BR, R_BI, R_ST = 512, 516, 517, 519, 521
R_ALL = 523

TILES_L1, TILES_L2, TILES_L3 = 16, 16, 24
TILES_A, TILES_C, TILES_O = 4, 8, 8
L2_TILE0 = TILES_L1
L3_TILE0 = L2_TILE0 + TILES_L2
OUT_TILE0 = L3_TILE0 + TILES_L3
MIX_TILES = OUT_TILE0 + 2 * TILES_A + TILES_C + TILES_O
FFN_STEPS = FF // 2
FFN_TILES = 6
N_TILES = MIX_TILES + FFN_STEPS * FFN_TILES

TWO_PI = [6.28125, 0.0019350051879882812, 3.0199e-07]
ROUND = 1.5 * 2.0 ** 23
PI_BELOW = 3.1415925
SCRATCH = [("hy_s", (16, P, T)), ("k_s", (8, P, 2 * FH * P)), ("gate_s", (24, P, T)), ("za_s", (CH, P, T)),
           ("zb_s", (CH, P, T)), ("zc_s", (KD, P, T))]
COS = [math.cos(math.pi * k / 8) for k in range(5)]
SIN = [math.sin(math.pi * k / 8) for k in range(5)]


def real_dft_even(o, z, temp, out):
    e, d = temp(0, 4), temp(4, 8)
    o.add(e, z(0, 4), z(4, 8))
    o.sub(d, z(0, 4), z(4, 8))
    o.sub(out("re4"), temp(0), temp(2))
    o.sub(out("im4"), temp(3), temp(1))
    o.add(temp(8, 10), temp(0, 2), temp(2, 4))
    o.sub(temp(10), temp(5), temp(7))
    o.add(temp(11), temp(5), temp(7))
    o.add(out("re0"), temp(8), temp(9))
    o.sub(out("re8"), temp(8), temp(9))
    o.mul_add(out("re2"), temp(10), COS[2], temp(4))
    o.mul_add(out("re6"), temp(10), -COS[2], temp(4))
    o.mul_add(out("im6"), temp(11), -COS[2], temp(6))
    o.mul_sub(out("im2"), temp(11), -COS[2], temp(6))


def real_dft_odd(o, z, temp, out):
    o.sub(temp(0, 3), z(1, 4), z(7, 4, -1))
    o.add(temp(3, 6), z(1, 4), z(7, 4, -1))
    u = [None, temp(0), temp(1), temp(2)]
    v = [None, temp(3), temp(4), temp(5)]
    o.mul_add(temp(6), u[2], COS[2], z(0))
    o.mul_add(temp(7), u[2], -COS[2], z(0))
    o.mul(temp(8), u[3], COS[3])
    o.mul(temp(9), u[3], -COS[1])
    o.mul_add(temp(8), u[1], COS[1], temp(8))
    o.mul_add(temp(9), u[1], COS[3], temp(9))
    o.add(out("re1"), temp(6), temp(8))
    o.sub(out("re7"), temp(6), temp(8))
    o.add(out("re3"), temp(7), temp(9))
    o.sub(out("re5"), temp(7), temp(9))
    o.mul_add(temp(6), v[2], SIN[2], z(4))
    o.mul_sub(temp(7), v[2], SIN[2], z(4))
    o.mul(temp(8), v[3], -SIN[3])
    o.mul(temp(9), v[3], SIN[1])
    o.mul_add(temp(8), v[1], -SIN[1], temp(8))
    o.mul_add(temp(9), v[1], -SIN[3], temp(9))
    o.sub(out("im1"), temp(8), temp(6))
    o.add(out("im7"), temp(8), temp(6))
    o.sub(out("im3"), temp(9), temp(7))
    o.add(out("im5"), temp(9), temp(7))


def real_dft_context(o, z, out):
    o.add(out("cre0"), z(0), z(1))
    o.sub(out("cre2"), z(0), z(1))
    o.mul(out("cre1"), z(0), 1.0)
    o.mul(out("cim1"), z(1), -1.0)


def inverse_latent(o, b, temp, y):
    rp, rm, ip, im = temp(0, 3), temp(3, 6), temp(6, 9), temp(9, 12)
    low_re, high_re = b("re", 1, 3), b("re", 7, 5)
    low_im, high_im = b("im", 1, 3), b("im", 7, 5)
    o.add(rp, low_re, high_re)
    o.sub(rm, low_re, high_re)
    o.add(ip, low_im, high_im)
    o.sub(im, low_im, high_im)
    o.add(temp(12), b("re0"), b("re8"))
    o.sub(temp(13), b("re0"), b("re8"))
    re4, im4 = b("re4"), b("im4")
    x, w, d = temp(14), temp(15), temp(16)
    o.add(x, temp(12), re4)
    o.add(w, temp(0), temp(2))
    o.sub(y(4), x, temp(1))
    o.sub(d, temp(11), temp(9))
    o.add(x, x, temp(1))
    o.add(y(4), y(4), d)
    o.add(y(0), x, w)
    x = [None] + [temp(17 + 2 * k) for k in range(3)]
    w = [None] + [temp(18 + 2 * k) for k in range(3)]
    sums = []
    for i in (1, 2, 3):
        s = i % 2
        r = [None] + [temp((3 if s else 0) + k) for k in range(3)]
        m = [None] + [temp((6 if s else 9) + k) for k in range(3)]
        terms_w = [(r[3], math.cos(3 * math.pi * i / 8)), (r[1], math.cos(math.pi * i / 8)),
                   (m[2], -math.sin(math.pi * i / 4)), (im4, -math.sin(math.pi * i / 2))]
        terms_x = [(r[2], math.cos(math.pi * i / 4)), (re4, math.cos(math.pi * i / 2)),
                   (m[1], -math.sin(math.pi * i / 8)), (m[3], -math.sin(3 * math.pi * i / 8))]
        for out, terms, first in ((w[i], terms_w, None), (x[i], terms_x, temp(12 + s))):
            sums.append((out, [(a, c) for a, c in terms if abs(c) > 1e-9], first))
    for k in range(4):
        for out, terms, first in sums:
            if k == 0 and first is None:
                o.mul(out, *terms[0])
            elif k < len(terms):
                o.mul_add(out, *terms[k], out if k else first)
    for i in (1, 2, 3):
        o.add(y(i), x[i], w[i])
        o.sub(y(8 - i), x[i], w[i])


def inverse_context(o, b, temp, y):
    o.add(temp(0), b("cre0"), b("cre2"))
    o.sub(temp(1), b("cre0"), b("cre2"))
    o.add(y(0), temp(0), b("cre1"))
    o.sub(y(1), temp(1), b("cim1"))


class Chain:

    def __init__(self, eng, sem):
        self.eng, self.sem, self.n = eng, sem, 0

    def __call__(self, ins):
        ins.then_inc(self.sem, 1)
        self.n += 1
        self.eng.wait_ge(self.sem, self.n)

    def loose(self, ins):
        ins.then_inc(self.sem, 1)
        self.n += 1
        if self.n > 1:
            self.eng.wait_ge(self.sem, self.n - 1)

    def add(self, ins):
        ins.then_inc(self.sem, 1)
        self.n += 1

    def settle(self):
        if self.n:
            self.eng.wait_ge(self.sem, self.n)

    def restart(self):
        self.settle()
        if self.n:
            self.eng.sem_clear(self.sem)
        self.n = 0


class Butterfly:

    def __init__(self, dve, chain):
        self.dve, self.chain = dve, chain

    def add(self, out, a, b):
        self.chain.loose(self.dve.tensor_tensor(out, a, b, ALU.add))

    def sub(self, out, a, b):
        self.chain.loose(self.dve.tensor_tensor(out, a, b, ALU.subtract))

    def mul(self, out, a, c):
        self.chain.loose(self.dve.tensor_scalar(out, a, float(c), None, ALU.mult))

    def mul_add(self, out, a, c, b):
        self.chain.loose(self.dve.scalar_tensor_tensor(out, a, float(c), b, ALU.mult, ALU.add))

    def mul_sub(self, out, a, c, b):
        self.chain.loose(self.dve.scalar_tensor_tensor(out, a, float(c), b, ALU.mult, ALU.subtract))


class MixUnits:

    def __init__(self, base, units):
        self.base, self.units = list(base), units

    def uses(self, b):
        return len([j for j in range(self.units) if j % MIX_BANKS == b])

    def bank(self, j):
        return j % MIX_BANKS

    def nth(self, it, j):
        b = j % MIX_BANKS
        return it * self.uses(b) + (self.base[b] + j // MIX_BANKS)

    def after(self, passes):
        return [self.base[b] + passes * self.uses(b) for b in range(MIX_BANKS)]


def places(buf, width, first=0):
    def at(a, b=None, step=1):
        if b is None:
            return buf[:, first + a, :]
        if step == 1:
            return buf[:, first + a:first + b, :]
        return buf[:, first + a:first + b:-1, :]
    return at


def spectrum_places(buf):
    def at(name):
        if name.startswith("c"):
            return buf[:, 9 + int(name[3:]), :] if name[1:3] == "re" else buf[:, 19, :]
        f = int(name[2:])
        return buf[:, f if name[:2] == "re" else 11 + f, :]
    return at


def inverse_places(buf):
    def at(name, a=None, b=None):
        part = 0 if "re" in name else 1
        if a is not None:
            lo, hi = 2 * (a - 1) + part, 2 * (b - 1) + part
            return buf[:, lo:hi + 1:2, :] if a < b else buf[:, lo:hi - 1:-2, :]
        if name in ("re0", "re8", "cre0", "cre2"):
            return buf[:, 16 + ("re0", "re8", "cre0", "cre2").index(name), :]
        f = 8 if name.startswith("c") else int(name[2:])
        return buf[:, 2 * (f - 1) + part, :]
    return at


HAS_IMAG = [1 <= q <= 7 or q == 10 for q in range(FH)]
IMAG_AT = {q: (19 if q == 10 else 11 + q) for q in range(FH) if HAS_IMAG[q]}
PAIRS = [(1, 2), (3, 4), (5, 6), (7, 10)]
SINGLES = (0, 8, 9, 11)


def build_program(nc, dr):
    ctx = ExitStack()
    with ctx:
        def sem(name):
            return ctx.enter_context(nc.semaphore(name))

        def sb(stack, name, shape, dt=F32):
            return stack.enter_context(nc.sbuf_tensor(name, shape, dt))

        w_raw = [sb(ctx, f"w_raw{s}", [P, D]) for s in range(2)]
        w_hi = [sb(ctx, f"w_hi{s}", [P, D], F32R) for s in range(2)]
        w_lo = [sb(ctx, f"w_lo{s}", [P, D], F32R) for s in range(2)]
        h_hi = sb(ctx, "h_hi", [P, KD, T], F32R)
        h_lo = sb(ctx, "h_lo", [P, KD, T], F32R)
        vec = sb(ctx, "vec", [P, V_ALL])
        mod = sb(ctx, "mod", [P, 48, 2])
        norm_a = sb(ctx, "norm_a", [P, KD, 2])
        fin = sb(ctx, "fin", [P, KD, 2])
        ones = sb(ctx, "ones", [P, P])
        eps = sb(ctx, "eps", [P, 1])
        zero_col = sb(ctx, "zero_col", [P, 1])
        hy_taps = sb(ctx, "hy_taps", [P, 4])
        sp_w = sb(ctx, "sp_w", [P, 6, 2 * KD])
        sp_pos = sb(ctx, "sp_pos", [P, 2 * KD])
        sp_neg = sb(ctx, "sp_neg", [P, 2 * KD])
        cvec = sb(ctx, "cvec", [P, KD, 2])
        csilu = sb(ctx, "csilu", [P, KD, 2])
        ps = [ctx.enter_context(nc.psum_tensor(f"ps{b}", [P, 512], F32)) for b in range(8)]

        fwd_stack = ExitStack()
        fwd = sb(fwd_stack, "fwd", [P, FH, 3, P])
        filt_ada = sb(fwd_stack, "filt_ada", [P, T])
        h2f = filt_ada[0:FILT_HID, :]
        ada_row = filt_ada[FILT_HID:FILT_HID + 2, 0:512]
        ada_w = [sb(fwd_stack, f"ada_w{s}", [P, KD * 256]) for s in range(2)]
        ident = sb(fwd_stack, "ident", [P, P])
        fwd_flat = fwd[:, :, :, :].rearrange("p q m f -> p (q m f)")
        ada_w += [fwd_flat[:, s * KD * 256:(s + 1) * KD * 256] for s in range(2)]

        st = ExitStack()
        x_in = sb(st, "x_in", [P, KD, T])
        x_sq_sum = sb(st, "x_sq_sum", [P, T])
        x_sq = sb(st, "x_sq", [P, T])
        rstd0 = sb(st, "rstd0", [P, T])
        f_vec = sb(st, "f_vec", [FILT_HID, 3])
        f_w1 = sb(st, "f_w1", [FILT_EMB, FILT_HID])
        f_w2 = sb(st, "f_w2", [FILT_HID, FILT_HID])
        feats = x_sq_sum[0:FILT_EMB, :]
        h1f = x_in[0:FILT_HID, 7, :]
        arg = x_in[0:FILT_HID, 6, :]
        turns = x_in[0:FILT_HID, 5, :]
        st.close()

        st = ExitStack()
        hin = sb(st, "hin", [P, PAD_T])
        hout = sb(st, "hout", [P, T])
        decay = sb(st, "decay", [P, NT, P])
        w3 = sb(st, "w3", [FILT_HID, 2 * P])
        taps = sb(st, "taps", [P, NT, 2, P])
        tsum = sb(st, "tsum", [P, NT, P])
        kstage = sb(st, "kstage", [P, 2 * FH, P])
        f_a = sb(st, "f_a", [P, 20, P])
        f_t = sb(st, "f_t", [P, 12, P])
        ss_k = sb(st, "ss_k", [P, 2, P])
        rs_k = sb(st, "rs_k", [P, 2, P])
        hy_part = sb(st, "hy_part", [P, CTX])
        st.close()

        st = ExitStack()
        r_b, i_b, a_b = ([sb(st, f"{name}0", [P, T])] for name in ("r_b", "i_b", "a_b"))
        rin = sb(st, "rin", [P, PAD_T])
        g_ry = sb(st, "g_ry", [P, T])
        xr = sb(st, "xr", [P, T])
        rpack = [sb(st, f"rpack{s}", [P, R_ALL]) for s in range(2)]
        for buf, name in ((r_b, "r_b"), (i_b, "i_b"), (a_b, "a_b")):
            buf.append(sb(st, f"{name}1", [P, T]))
        t_b = [sb(st, f"t_b{d}", [P, T]) for d in range(2)]
        st.close()
        fwd_stack.close()
        st = ExitStack()
        fn_ch = sb(st, "fn_ch", [P, 4, P])
        fn_t = sb(st, "fn_t", [P, NT, 2, P])
        fn_u = sb(st, "fn_u", [P, NT, P])
        fn_a = sb(st, "fn_a", [P, 20, P])
        fn_c = sb(st, "fn_c", [P, NT, 2, P])
        st.close()
        fn_y = fn_u[:, :, :].rearrange("p n c -> p (n c)")
        fn_tmp = fn_c[:, :, :, :].rearrange("p n d c -> p (n d) c")


        st = ExitStack()
        fwd3 = sb(st, "fwd3", [P, FH, 3, P])
        ident3 = sb(st, "ident3", [P, P])
        inv = sb(st, "inv", [P, FH, 3, P])
        x_b = sb(st, "x_b", [P, T])
        v_b = sb(st, "v_b", [P, T])
        z_b = sb(st, "z_b", [P, T])
        ztok = sb(st, "ztok", [P, FH, P])
        hy_a = sb(st, "hy_a", [P, 2 * FH, P])
        hy_z = sb(st, "hy_z", [P, 2 * FH, P])
        hbias = sb(st, "hbias", [P, 2])
        g_st = sb(st, "g_st", [P, T])
        hy_k = sb(st, "hy_k", [P, 2 * FH, P])
        st.close()

        low_stack = ExitStack()
        z2_hi = sb(low_stack, "z2_hi", [P, 4, T], F32R)
        z2_lo = sb(low_stack, "z2_lo", [P, 4, T], F32R)
        x1 = sb(low_stack, "x1", [P, KD, T])
        st = ExitStack()
        side = [sb(st, f"side{s}", [P, T]) for s in range(2)]
        zraw = [sb(st, f"zraw{s}", [P, T]) for s in range(2)]
        st.close()
        sq_o, sq_sum = zraw

        def norm1_u(k, a, e):
            return x_in[:, k, a:e]

        def norm2_u(k, a, e):
            return side[k % 2][:, a:e]

        st = ExitStack()
        act_hi = sb(st, "act_hi", [P, 2, T], F32R)
        act_lo = sb(st, "act_lo", [P, 2, T], F32R)
        st.close()
        low_stack.close()
        st = ExitStack()
        wf_hi = list(w_hi) + [sb(st, f"wf_hi{s}", [P, D], F32R) for s in range(2, 6)]
        wf_lo = list(w_lo) + [sb(st, f"wf_lo{s}", [P, D], F32R) for s in range(2, 6)]
        sil = [sb(st, f"sil{s}", [P, 512]) for s in range(2)]
        a32 = [sb(st, f"a32_{s}", [P, 512]) for s in range(2)]
        st.close()
        sq_end = sil
        sq_end_sum = [w_raw[0][:, 0:512], w_raw[0][:, 512:1024], w_raw[1][:, 0:256]]

        vec_in, consts_in, cvec_in = sem("vec_in"), sem("consts_in"), sem("cvec_in")
        filt1_in, filt_in = sem("filt1_in"), sem("filt_in")
        x_loaded = [sem(f"x_loaded{k}") for k in range(KD)]
        ada_in = [sem(f"ada_in{s}") for s in range(4)]
        raw_in = [sem(f"raw_in{s}") for s in range(2)]
        decay_in, w3_in = sem("decay_in"), sem("w3_in")
        rpack_in = [sem(f"rpack_in{s}") for s in range(2)]
        fn_const_in, fn_in, hy_const_in = sem("fn_const_in"), sem("fn_in"), sem("hy_const_in")
        v_in, xg_in, k_in, hbias_in = sem("v_in"), sem("xg_in"), sem("k_in"), sem("hbias_in")
        side_in = [sem(f"side_in{s}") for s in range(2)]
        zraw_in = [sem(f"zraw_in{s}") for s in range(2)]
        hy_stored, k_stored, zc_stored = sem("hy_stored"), sem("k_stored"), sem("zc_stored")
        zb_stored, za_stored, gate_stored = sem("zb_stored"), sem("za_stored"), sem("gate_stored")
        fin_stored, y_stored = sem("fin_stored"), sem("y_stored")
        split_done = sem("split_done")
        proj_done = [sem(f"proj_done{b}") for b in range(3)]
        proj_free = [sem(f"proj_free{b}") for b in range(3)]
        mix_done = [sem(f"mix_done{b}") for b in range(MIX_BANKS)]
        mix_free = [sem(f"mix_free{b}") for b in range(MIX_BANKS)]
        act_step, dve_step = sem("act_step"), sem("dve_step")
        pool_step, conv_step = sem("pool_step"), sem("conv_step")
        consts_set = sem("consts_set")
        csilu_set = sem("csilu_set")
        arg_ready = sem("arg_ready")
        sin_ready = sem("sin_ready")
        ada_row_ready = sem("ada_row_ready")
        mod_ready = sem("mod_ready")
        sp_ready = sem("sp_ready")
        sp_e, sp_l = sem("sp_e"), sem("sp_l")
        sq_ready = sem("sq_ready")
        x_sq_summed = sem("x_sq_summed")
        u_ready, hi_ready, h_ready = sem("u_ready"), sem("hi_ready"), sem("h_ready")
        hin_zero = sem("hin_zero")
        hy_conved = sem("hy_conved")
        taps_ready, taps_sq = sem("taps_ready"), sem("taps_sq")
        ss_ready = sem("ss_ready")
        fa_ready = sem("fa_ready")
        k_ready = sem("k_ready")
        xr_ready = sem("xr_ready")
        a2_ready = sem("a2_ready")
        m2_ready, root_ready = sem("m2_ready"), sem("root_ready")
        zc_ready = sem("zc_ready")
        fna_ready = sem("fna_ready")
        hya_ready = sem("hya_ready")
        y_ready = sem("y_ready")
        z_ready = sem("z_ready")
        zhi_ready, z_split = sem("zhi_ready"), sem("z_split")
        side_used = sem("side_used")
        mhi_ready, m_split = sem("mhi_ready"), sem("m_split")
        sq1_ready, sq_summed = sem("sq1_ready"), sem("sq_summed")
        u2_ready, h2_hi, h2_ready = sem("u2_ready"), sem("h2_hi"), sem("h2_ready")
        f_done = [sem(f"f_done{b}") for b in range(8)]
        f_free = [sem(f"f_free{b}") for b in range(8)]
        ahi_ready, act_ready = sem("ahi_ready"), sem("act_ready")
        sq3_ready, sq3_summed = sem("sq3_ready"), sem("sq3_summed")
        ms3_ready, root3_ready = sem("ms3_ready"), sem("root3_ready")
        y_out = sem("y_out")

        FILT_UNIT = (0, 1, 2, 4, 5, 7)
        ROW_UNIT = (3, 6) + tuple(range(9, 20, 2))
        TURN_UNIT = tuple(range(8, 21, 2)) + (21,)
        u_setup = MixUnits([0] * MIX_BANKS, 6 + 2 * ADA_FIRST)
        u_taps = MixUnits(u_setup.after(1), 5)
        u1 = MixUnits(u_taps.after(1), 1 + 1 + 3 + 5 + 3 + 1)
        u1_last = MixUnits(u1.after(7), 1 + 1 + 3 + 3 + 1)
        u2 = MixUnits(u1_last.after(1), 12 + 5 + 3 + 12)
        RG_UNIT, FN1_UNIT, FN2_UNIT = (0, 12 + 5 + 3), 12, 12 + 5
        u3 = MixUnits(u2.after(KD // 2), 2 * (3 + 6 + 5))
        out_base = u3.after(CH)
        NORM_BANKS = (1, 2, 3)

        def mix(b):
            return ps[FIRST_MIX + b]

        def raw_z(n):
            if n == 2:
                return v_b, v_in, 16 * (CH + 1), 0
            if n < 2:
                return zraw[n], zraw_in[n], 16, 0
            slot = (n - 3) % 2
            return zraw[slot], zraw_in[slot], 16 * ((n - 3) // 2 + 2), n - 2 if n < 5 else n - 1

        block = ctx.enter_context(nc.Block())
        stream = dr["weights"]

        @block.sync
        def _(sp):
            def load_tile(t, slot):
                sp.dma_start(w_raw[slot][:], stream[t]).then_inc(raw_in[slot], 16)

            def load_ahead(t, slot):
                sp.wait_ge(split_done, t + 1)
                load_tile(t + 2, slot)

            sp.dma_start(feats, dr["feats"]).then_inc(filt1_in, 16)
            sp.dma_start(f_w1[:], dr["f_w1"]).then_inc(filt1_in, 16)
            sp.dma_start(f_vec[:], dr["f_vec"]).then_inc(filt_in, 16)
            sp.dma_start(f_w2[:], dr["f_w2"]).then_inc(filt_in, 16)
            sp.dma_start(cvec[:], dr["cvec"]).then_inc(cvec_in, 16)
            sp.dma_start(ident[:], dr["ident"]).then_inc(consts_in, 16)
            sp.dma_start(vec[:], dr["vec"]).then_inc(vec_in, 16)
            def load_x(chunks):
                for k in chunks:
                    sp.dma_start(x_in[:, k, :], dr["x"][k]).then_inc(x_loaded[k], 16)

            for g in range(4):
                sp.dma_start(ada_w[g][:], dr["w_ada"][g]).then_inc(ada_in[g], 16)
                load_x(((0,), (1,), (2,), (3, 4))[g])
            for g in range(4, ADA_FIRST + 2):
                sp.wait_ge(ada_row_ready, g - 3)
                sp.dma_start(ada_w[g % 4][:], dr["w_ada"][g]).then_inc(ada_in[g % 4], 16)
                if g == 4:
                    sp.wait_ge(sin_ready, 6)
                    load_x((5,))
                if g == 5:
                    load_x((6, 7))
            for stored in (k_stored, za_stored, zb_stored, zc_stored, gate_stored):
                sp.sem_inc(stored, 16)
            sp.wait_ge(ada_row_ready, ADA_FIRST)
            sp.dma_start(fwd[:], dr["fwd"]).then_inc(consts_in, 16)
            load_tile(0, 0)
            load_tile(1, 1)
            sp.wait_ge(h_ready, 3 * KD)

            def load_taps(i):
                sp.dma_start(w3[:], dr["w3"][i]).then_inc(w3_in, 16)
                sp.dma_start(decay[:], dr["decay"][i]).then_inc(decay_in, 16)

            def l1_pass(i, last):
                load_ahead(2 * i, 0)
                if not last:
                    sp.wait_ge(taps_ready, i + 1)
                    load_taps(i + 1)
                load_ahead(2 * i + 1, 1)
                if not last:
                    sp.wait_ge(ada_row_ready, i + (ADA_FIRST + 1))
                    for g in range(2):
                        sp.dma_start(ada_w[g][:], dr["w_ada"][2 * i + (ADA_FIRST + 2 + g)]).then_inc(ada_in[g], 16)
                sp.wait_ge(hy_conved, 2 * i + 2)
                sp.dma_start(dr["hy_s"][2 * i], hout[:]).then_inc(hy_stored, 16)
                sp.wait_ge(k_ready, i + 1)
                sp.dma_start(dr["k_s"][i], kstage[:]).then_inc(k_stored, 16)
                if not last:
                    sp.wait_ge(hy_conved, 2 * i + 3)
                    sp.dma_start(dr["hy_s"][2 * i + 1], hout[:]).then_inc(hy_stored, 16)

            load_taps(0)
            with sp.Fori(0, 7) as i:
                l1_pass(i, False)
            l1_pass(7, True)

            sp.wait_ge(mod_ready, ADA_FIRST + 8)
            sp.wait_ge(k_stored, 16 * 9)
            sp.dma_start(rpack[0][:], dr["rpack"][0]).then_inc(rpack_in[0], 16)
            sp.dma_start(fn_ch[:], dr["fn_ch"]).then_inc(fn_const_in, 16)
            sp.dma_start(fn_t[:], dr["fn_t"]).then_inc(fn_const_in, 16)

            def l2_pair(m, last):
                sp.wait_ge(zb_stored, 16 * m + 16)
                sp.dma_start(fn_u[:], dr["hy_s"][m + 12]).then_inc(fn_in, 16)
                for s in range(2):
                    n = 2 * m + s
                    if not (last and s):
                        sp.wait_ge(zc_ready, n + 1)
                        sp.dma_start(rpack[1 - s][:], dr["rpack"][n + 1]).then_inc(rpack_in[1 - s], 16)
                    load_ahead(2 * n + L2_TILE0, 0)
                    load_ahead(2 * n + (L2_TILE0 + 1), 1)
                    if s == 1:
                        sp.wait_ge(mix_free[u2.bank(FN2_UNIT + 2)], u2.nth(m, FN2_UNIT + 2) + 1)
                        sp.dma_start(dr["zb_s"][m], fn_y).then_inc(zb_stored, 16)
                    if last and s:
                        sp.wait_ge(zb_stored, 16 * (1 + CH))
                        sp.dma_start(ident3[:], dr["ident"]).then_inc(hy_const_in, 16)
                        sp.dma_start(fwd3[:], dr["fwd"]).then_inc(hy_const_in, 16)
                        sp.dma_start(inv[:], dr["inv"]).then_inc(hy_const_in, 16)
                    sp.wait_ge(zc_ready, n + 2)
                    sp.dma_start(dr["zc_s"][n], r_b[0][:]).then_inc(zc_stored, 16)

            sp.wait_ge(hy_conved, 1 + TILES_L1)
            sp.dma_start(dr["hy_s"][TILES_L1 - 1], hout[:]).then_inc(hy_stored, 16)
            sp.wait_ge(hy_stored, 16 * TILES_L1)
            with sp.Fori(0, KD // 2 - 1) as m:
                l2_pair(m, False)
            l2_pair(KD // 2 - 1, True)

            sp.dma_start(v_b[:], dr["hy_s"][0]).then_inc(v_in, 16)
            sp.dma_start(dr["state_out"], fin[:]).then_inc(fin_stored, 16)
            sp.wait_ge(zc_stored, 16 * (1 + KD))

            def load_z(n, src):
                buf, loaded, _, splits = raw_z(n)
                if splits:
                    sp.wait_ge(z_split, splits)
                sp.dma_start(buf[:], src).then_inc(loaded, 16)

            def l3_pass(c, last):
                t = 6 * c + L3_TILE0
                sp.dma_start(hbias[:], dr["hbias"][c]).then_inc(hbias_in, 16)
                for order in range(2):
                    load_ahead(t + 3 * order, 3 * order % 2)
                    sp.wait_ge(z_ready, 2 * c + (order + 1))
                    sp.dma_start(x_b[:], dr["hy_s"][c + (4 + 4 * order)]).then_inc(xg_in, 16)
                    sp.dma_start(hy_k[:], dr["k_s"][c + 4 * order]).then_inc(k_in, 16)
                    if order == 1 and not last:
                        sp.dma_start(v_b[:], dr["hy_s"][c + 1]).then_inc(v_in, 16)
                    for g in range(3):
                        j = 3 * order + g
                        if g:
                            load_ahead(t + j, j % 2)
                        for b in range(3):
                            sp.wait_ge(proj_free[b], t + (j + 2))
                        sp.dma_start(dr["gate_s"][6 * c + j], g_st[:]).then_inc(gate_stored, 16)
                        if last and order == 1 and g == 1:
                            sp.wait_ge(y_ready, 2 * CH)
                            for n in range(3):
                                load_z(n, dr["zb_s"][n])
                sp.wait_ge(z_ready, 2 * c + 3)
                sp.dma_start(dr["za_s"][c], z_b[:]).then_inc(za_stored, 16)

            with sp.Fori(0, CH - 1) as c:
                l3_pass(c, False)
            l3_pass(CH - 1, True)
            load_z(3, dr["zb_s"][3])
            sp.wait_ge(za_stored, 16 * (1 + CH))
            sp.wait_ge(gate_stored, 16 * (1 + TILES_L3))

            def load_side(n, src):
                if 2 <= n < 10 or n >= 26:
                    for b in range(3):
                        sp.wait_ge(proj_free[b], OUT_TILE0 + n)
                elif n >= 10:
                    sp.wait_ge(side_used, n - 9)
                sp.dma_start(side[n % 2][:], src).then_inc(side_in[n % 2], 16)

            z_src = [dr["zb_s"][c] for c in range(4)] + [dr["zc_s"][n] for n in range(8)] + \
                    [dr["za_s"][c] for c in range(4)]
            gate_src = [dr["gate_s"][8 + m] for m in range(8)] + [dr["gate_s"][16 + m] for m in range(8)] + \
                       [dr["gate_s"][m] for m in range(8)] + [dr["x"][m] for m in range(8)]
            for n in range(4, 12):
                load_z(n, z_src[n])
                load_side(n - 4, gate_src[n - 4])
                if n % 2:
                    load_ahead(OUT_TILE0 + (n - 5) // 2, (n - 5) // 2 % 2)
            for n in range(12, 16):
                load_z(n, z_src[n])
            for n in range(8):
                load_side(8 + n, gate_src[8 + n])
                load_ahead(OUT_TILE0 + 4 + n, n % 2)
            for n in range(8):
                load_side(16 + n, gate_src[16 + n])
                if n % 2:
                    load_ahead(OUT_TILE0 + 12 + n // 2, n // 2 % 2)
            for n in range(8):
                load_side(24 + n, gate_src[24 + n])
                load_ahead(OUT_TILE0 + 16 + n, n % 2)
            with sp.Fori(0, FFN_STEPS * FFN_TILES // 2 - 1) as m:
                load_ahead(2 * m + MIX_TILES, 0)
                load_ahead(2 * m + (MIX_TILES + 1), 1)
            for p, (a, e, _) in enumerate(PIECES):
                sp.wait_ge(y_out, KD * (p + 1))
                sp.dma_start(dr["y"][:, :, a:e], x1[:, :, a:e]).then_inc(y_stored, 16)
            sp.wait_ge(fin_stored, 16)
            sp.wait_ge(y_stored, 16 * 3)

        @block.gpsimd
        def _(pool):
            nc.gpsimd.memset(ones[:], 1.0).then_inc(consts_set, 1)
            nc.gpsimd.memset(eps[:], EPS).then_inc(consts_set, 1)
            nc.gpsimd.memset(zero_col[:], 0.0).then_inc(consts_set, 1)
            for ready in [hy_conved, xr_ready, zc_ready, z_ready] + f_free:
                pool.sem_inc(ready, 1)
            pool.wait_ge(consts_set, 3)

            def split(t, slot, hi, lo):
                pool.wait_ge(raw_in[slot % 2], t * 8 + (16 - 8 * (slot % 2)))
                nc.gpsimd.tensor_tensor(hi[:], w_raw[slot % 2][:], zero_col[:].to_broadcast([P, D]),
                                        ALU.add).then_inc(pool_step, 1)
                pool.wait_ge(pool_step, t + 1)
                nc.gpsimd.tensor_tensor(lo[:], w_raw[slot % 2][:], hi[:].bitcast(F32),
                                        ALU.subtract).then_inc(split_done, 1)

            own = Chain(pool, conv_step)

            def hy_conv(tile, use):
                for b in range(3):
                    pool.wait_ge(proj_free[b], use + 1)
                pool.wait_ge(hy_stored, 16 * tile)
                own(nc.gpsimd.tensor_copy(hy_taps[:], vec[:, bass.ds(4 * tile + V_HY, 4)]))
                for a, e, seq in SEQS:
                    at = (PAD_CTX if seq else PAD_LAT) - 1
                    own.add(nc.gpsimd.tensor_scalar(hout[:, a:e], hin[:, at:at + e - a], hy_taps[:, 0:1],
                                                    hy_taps[:, 3:4], ALU.mult, ALU.add))
                own.settle()
                for k in (1, 2):
                    for a in range(0, T, CTX):
                        at = (PAD_LAT + a if a < LAT else PAD_CTX) - 1 + k
                        own(nc.gpsimd.tensor_scalar(hy_part[:], hin[:, at:at + CTX], hy_taps[:, k:k + 1], None,
                                                    ALU.mult))
                        own(nc.gpsimd.tensor_tensor(hout[:, a:a + CTX], hout[:, a:a + CTX], hy_part[:], ALU.add))
                pool.sem_inc(hy_conved, 1)

            split(0, 0, w_hi[0], w_lo[0])
            split(1, 1, w_hi[1], w_lo[1])
            pool.wait_ge(vec_in, 16)
            with pool.Fori(0, 8) as i:
                for s in range(2):
                    pool.wait_ge(proj_done[2], 2 * i + (2 + s))
                    split(2 * i + (2 + s), s, w_hi[s], w_lo[s])
                    if s == 0:
                        hy_conv(2 * i, 2 * i + 1)
                own.restart()
            with pool.Fori(TILES_L1 // 2 + 1, OUT_TILE0 // 2 + 1) as m:
                for s in range(2):
                    pool.wait_ge(proj_done[2], 2 * m + s)
                    split(2 * m + s, s, w_hi[s], w_lo[s])
            chunks = [2] * TILES_A + [1] * TILES_C + [2] * TILES_A + [1] * TILES_O
            for n in range(2, len(chunks)):
                t = OUT_TILE0 + n
                pool.wait_ge(proj_done[2], OUT_TILE0 + 1 + sum(chunks[:n - 1]))
                split(t, n % 2, w_hi[n % 2], w_lo[n % 2])
            for q in range(FFN_TILES):
                if q < 2:
                    pool.wait_ge(proj_done[2], OUT_TILE0 + 1 + 31 + q)
                split(MIX_TILES + q, q, wf_hi[q], wf_lo[q])
            with pool.Fori(1, FFN_STEPS) as s:
                frees = [(f_done[0], 3 * s), (f_done[1], 3 * s), (f_done[2], 3 * s), (f_done[3], 3 * s),
                         (f_done[7], 6 * s), (f_done[7], 6 * s)]
                for q in range(FFN_TILES):
                    pool.wait_ge(*frees[q])
                    split(FFN_TILES * s + (MIX_TILES + q), q, wf_hi[q], wf_lo[q])

        @block.tensor
        def _(pe):
            mm = nc.tensor.matmul

            def split_product(out, w_pair, x_pair, first, last):
                mm(out, w_pair[0], x_pair[0], start=first, stop=False)
                mm(out, w_pair[0], x_pair[1], start=False, stop=False)
                return mm(out, w_pair[1], x_pair[0], start=False, stop=last)

            def projection(use, ws, xs, cols, made=None, pieces=(0, 1, 2)):
                for b in pieces:
                    a, e, _ = PIECES[b]
                    pe.wait_ge(proj_free[b], use)
                    for k, (w, x) in enumerate(zip(ws, xs)):
                        if made:
                            pe.wait_ge(made, len(xs) * b + k + 1)
                        ins = split_product(ps[b][:, 0:e - a], [w[0][:, cols[k]], w[1][:, cols[k]]],
                                            [x[0][:, a:e], x[1][:, a:e]], k == 0, k == len(ws) - 1)
                    ins.then_inc(proj_done[b], 1)

            h_pairs = [(h_hi[:, k, :], h_lo[:, k, :]) for k in range(KD)]

            def projection_tile(t, slot, made=None, pieces=(0, 1, 2)):
                pe.wait_ge(split_done, t + 1)
                projection(t + 1, [(w_hi[slot], w_lo[slot])] * KD, h_pairs,
                           [slice(k * P, k * P + P) for k in range(KD)], made, pieces)

            def mix_unit(units, it, j):
                b = units.bank(j)
                pe.wait_ge(mix_free[b], units.nth(it, j))
                return mix(b), mix_done[b]

            def ada_row_unit(units, it, j, slots, loads):
                out, done = mix_unit(units, it, j)
                for n, slot in enumerate(slots):
                    pe.wait_ge(ada_in[slot], loads)
                    for k in range(KD):
                        ins = mm(out[0:2, n * 256:(n + 1) * 256], csilu[:, k, :],
                                 ada_w[slot][:, k * 256:(k + 1) * 256], start=k == 0, stop=k == KD - 1)
                ins.then_inc(done, 1)

            def ada_turn_unit(units, it, j, rows, at, width):
                out, done = mix_unit(units, it, j)
                pe.wait_ge(ada_row_ready, rows)
                for q in range(width // P):
                    ins = mm(out[:, 2 * q:2 * q + 2], ada_row[0:2, at + q * P:at + (q + 1) * P],
                             ident[FILT_HID:FILT_HID + 2, FILT_HID:FILT_HID + 2],
                             start=True, stop=True)
                ins.then_inc(done, 1)

            def first_rows(g):
                ada_row_unit(u_setup, 0, ROW_UNIT[g], [g % 4], 16 * (g // 4 + 1))

            pe.wait_ge(filt1_in, 32)
            for j, (a, e, _) in enumerate(PIECES):
                out, done = mix_unit(u_setup, 0, FILT_UNIT[j])
                mm(out[0:FILT_HID, 0:e - a], f_w1[:, :], feats[:, a:e], start=True, stop=True).then_inc(done, 1)
            pe.wait_ge(csilu_set, 1)
            first_rows(0)
            pe.wait_ge(filt_in, 32)
            for j, (a, e, _) in enumerate(PIECES):
                out, done = mix_unit(u_setup, 0, FILT_UNIT[3 + j])
                pe.wait_ge(sin_ready, j + 1)
                mm(out[0:FILT_HID, 0:e - a], f_w2[:, :], h1f[:, a:e], start=True, stop=True).then_inc(done, 1)
                if j == 1:
                    first_rows(1)
            pe.wait_ge(consts_in, 16)
            pe.wait_ge(consts_set, 3)
            for g in range(ADA_FIRST):
                if 2 <= g + 1 < ADA_FIRST:
                    first_rows(g + 1)
                ada_turn_unit(u_setup, 0, TURN_UNIT[g], g + 1, g % 2 * 256, 256)
                if g == ADA_FIRST - 3:
                    pe.wait_ge(x_sq_summed, KD - 1)
                    for b, (a, e, _) in enumerate(PIECES):
                        mm(ps[b][:, 0:e - a], ones[:], x_sq_sum[:, a:e],
                           start=True, stop=True).then_inc(proj_done[b], 1)

            def fwd_unit(units, it, j, block_j, imag, a_buf, mats):
                out, done = mix_unit(units, it, j)
                for s in range(4):
                    q = 4 * block_j + s
                    o = out[:, s * P:(s + 1) * P]
                    re, im = a_buf[:, q, :], a_buf[:, IMAG_AT[q], :] if HAS_IMAG[q] else None
                    terms = [(0, re), (1, im)] if not imag else [(2, re), (0, im)]
                    terms = [x for x in terms if x[1] is not None]
                    for n, (m, part) in enumerate(terms):
                        ins = mm(o, mats[:, q, m, :], part, start=n == 0, stop=n == len(terms) - 1)
                ins.then_inc(done, 1)

            pe.wait_ge(consts_in, 32)

            def taps_units(units, it, j0, loads):
                pe.wait_ge(w3_in, loads)
                for j in range(5):
                    out, done = mix_unit(units, it, j0 + j)
                    for s in range(2):
                        tile = 2 * j + s
                        ins = mm(out[:, s * 256:(s + 1) * 256], h2f[:, tile * P:(tile + 1) * P], w3[:, :],
                                 start=True, stop=True)
                    ins.then_inc(done, 1)

            def l1_pass(i, units, it, last):
                ada_row_unit(units, it, 0, range(2), 16 * i + 16 * (ADA_FIRST // 4 + 1))
                out, done = mix_unit(units, it, 1)
                pe.wait_ge(ss_ready, i + 1)
                mm(out[:, 0:2 * P], ones[:], ss_k[:, :, :], start=True, stop=True).then_inc(done, 1)
                pe.wait_ge(fa_ready, 2 * i + 1)
                for j in range(3):
                    fwd_unit(units, it, 2 + j, j, False, f_a, fwd)
                if not last:
                    taps_units(units, it, 5, 16 * i + 32)
                projection_tile(2 * i + 1, 1)
                pe.wait_ge(fa_ready, 2 * i + 2)
                j0 = 5 if last else 10
                for j in range(3):
                    fwd_unit(units, it, j0 + j, j, True, f_a, fwd)
                ada_turn_unit(units, it, j0 + 3, i + (ADA_FIRST + 1), 0, 512)
                if not last:
                    projection_tile(2 * i + 2, 0)

            projection_tile(0, 0, h_ready)
            taps_units(u_taps, 0, 0, 16)
            with pe.Fori(0, 7) as i:
                l1_pass(i, u1, i, False)
            l1_pass(7, u1_last, 0, True)

            def fnet_channels(c):
                pe.wait_ge(fn_const_in, 32)
                pe.wait_ge(fna_ready, c + 1)
                for j in range(5):
                    out, done = mix_unit(u2, c, FN1_UNIT + j)
                    for s in range(2):
                        f = 2 * j + s
                        o = out[:, s * 256:(s + 1) * 256]
                        if f >= NL:
                            terms = [(9 + f - NL, 1)]
                        else:
                            g = f if f <= 4 else 8 - f
                            terms = [(2 * g, 1)]
                            if 1 <= g <= 3:
                                terms.append((11 + 2 * g, 0 if f <= 4 else 2))
                        for n, (place, m) in enumerate(terms):
                            ins = mm(o, fn_a[:, place, :], fn_ch[:, m:m + 2, :], start=n == 0,
                                     stop=n == len(terms) - 1)
                    ins.then_inc(done, 1)

            def fnet_tokens(c):
                for j in range(5):
                    pe.wait_ge(mix_free[u2.bank(FN1_UNIT + j)], u2.nth(c, FN1_UNIT + j) + 1)
                for j in range(3):
                    out, done = mix_unit(u2, c, FN2_UNIT + j)
                    for f in range(4 * j, min(4 * j + 4, NT)):
                        for part in range(2):
                            ins = mm(out[:, (f % 4) * P:(f % 4 + 1) * P], fn_c[:, f, part, :],
                                     fn_t[:, f, part, :], start=part == 0, stop=part == 1)
                    ins.then_inc(done, 1)

            with pe.Fori(0, KD // 2) as m:
                for s in range(2):
                    n = 2 * m + s
                    projection_tile(2 * n + L2_TILE0, 0)
                    if s == 1:
                        fnet_tokens(m)
                    projection_tile(2 * n + (L2_TILE0 + 1), 1)
                    pe.wait_ge(xr_ready, n + 2)
                    pe.wait_ge(rpack_in[s], 16 * m + 16)
                    for j in range(12):
                        out, done = mix_unit(u2, m, RG_UNIT[s] + j)
                        a, e, _ = PIECES[j % 3]
                        mm(out[:, 0:e - a], rpack[s][:, (j // 3) * P:(j // 3 + 1) * P], xr[:, a:e],
                           start=True, stop=True).then_inc(done, 1)
                    if s == 0:
                        fnet_channels(m)

            with pe.Fori(0, CH) as c:
                for order in range(2):
                    j0 = 14 * order
                    t = 6 * c + (L3_TILE0 + 3 * order)
                    slot = 3 * order % 2
                    projection_tile(t, slot)
                    if order == 0:
                        pe.wait_ge(hy_const_in, 48)
                        pe.wait_ge(v_in, 16 * c + 16)
                    else:
                        pe.wait_ge(z_ready, 2 * c + 2)
                    for j in range(3):
                        out, done = mix_unit(u3, c, j0 + j)
                        for tile in range(4 * j, min(4 * j + 4, NT)):
                            ins = nc.tensor.transpose(out[:, (tile % 4) * P:(tile % 4 + 1) * P],
                                                      (v_b, z_b)[order][:, tile * P:(tile + 1) * P], ident3[:, :])
                        ins.then_inc(done, 1)
                    projection_tile(t + 1, 1 - slot, pieces=(0, 1))
                    pe.wait_ge(hya_ready, 2 * c + (order + 1))
                    for j in range(6):
                        fwd_unit(u3, c, j0 + 3 + j, j % 3, j >= 3, hy_a, fwd3)
                    projection_tile(t + 1, 1 - slot, pieces=(2,))
                    projection_tile(t + 2, slot, pieces=(0, 1))
                    pe.wait_ge(y_ready, 2 * c + (order + 1))
                    for j in range(5):
                        out, done = mix_unit(u3, c, j0 + 9 + j)
                        if j < 4:
                            for s, q in enumerate(PAIRS[j]):
                                o = out[:, s * 256:(s + 1) * 256]
                                mm(o, hy_a[:, q, :], inv[:, q, 1:3, :], start=True, stop=False)
                                ins = mm(o, hy_a[:, FH + q, :], inv[:, q, 0:2, :], start=False, stop=True)
                        else:
                            for s, q in enumerate(SINGLES):
                                o = out[:, s * P:(s + 1) * P]
                                mm(o, hy_a[:, q, :], inv[:, q, 1, :], start=True, stop=False)
                                ins = mm(o, hy_a[:, FH + q, :], inv[:, q, 0, :], start=False, stop=True)
                        ins.then_inc(done, 1)
                    projection_tile(t + 2, slot, pieces=(2,))

            z2_pairs = [(z2_hi[:, k, :], z2_lo[:, k, :]) for k in range(4)]
            use0 = OUT_TILE0 + 1

            def narrow_tiles(first_tile, first_use):
                with pe.Fori(0, 2) as m:
                    for s in range(2):
                        pe.wait_ge(split_done, 2 * m + (first_tile + s + 1))
                        for q in range(2):
                            projection(4 * m + (first_use + 2 * s + q), [(w_hi[s], w_lo[s])] * 4, z2_pairs,
                                       [slice((4 * q + k) * P, (4 * q + k + 1) * P) for k in range(4)])

            def wide_tile(t, use, slot):
                pe.wait_ge(split_done, t + 1)
                projection(use, [(w_hi[slot], w_lo[slot])] * KD, h_pairs,
                           [slice(k * P, k * P + P) for k in range(KD)])

            pe.wait_ge(z_split, 4)
            narrow_tiles(OUT_TILE0, use0)
            pe.wait_ge(z_split, 12)
            with pe.Fori(0, 4) as m:
                for s in range(2):
                    wide_tile(2 * m + (OUT_TILE0 + 4 + s), 2 * m + (use0 + 8 + s), s)
            pe.wait_ge(z_split, 16)
            narrow_tiles(OUT_TILE0 + 12, use0 + 16)
            pe.wait_ge(m_split, KD)

            for m in range(KD):
                wide_tile(OUT_TILE0 + 16 + m, use0 + 24 + m, m % 2)
            for p, (a, e, _) in enumerate(PIECES):
                b = NORM_BANKS[p]
                pe.wait_ge(mix_free[b], out_base[b])
                pe.wait_ge(sq_summed, 3 * (KD - 2) + p + 1)
                mm(mix(b)[:, 0:e - a], ones[:], sq_sum[:, a:e], start=True, stop=True).then_inc(mix_done[b], 1)

            for b in range(3):
                pe.wait_ge(proj_free[b], use0 + 32)
            for b in (0, 4):
                pe.wait_ge(mix_free[b], out_base[b])
            with pe.Fori(0, FFN_STEPS) as s:
                for p, (a, e, _) in enumerate(PIECES):
                    for j in range(2):
                        for up in range(2):
                            q = 2 * j + up
                            if p == 0:
                                pe.wait_ge(split_done, FFN_TILES * s + (MIX_TILES + q + 1))
                            n = 2 * (2 * p + j) + up
                            pe.wait_ge(f_free[n % 4], 3 * s + (n // 4 + 1))
                            for k in range(KD):
                                if j == 0 and up == 0:
                                    pe.wait_ge(h2_ready, KD * p + k + 1)
                                ins = split_product(ps[n % 4][:, 0:e - a],
                                                    [wf_hi[q][:, k * P:(k + 1) * P], wf_lo[q][:, k * P:(k + 1) * P]],
                                                    [h_hi[:, k, a:e], h_lo[:, k, a:e]], k == 0, k == KD - 1)
                            ins.then_inc(f_done[n % 4], 1)
                pe.wait_ge(split_done, FFN_TILES * s + (MIX_TILES + FFN_TILES))
                for p, (a, e, _) in enumerate(PIECES):
                    pe.wait_ge(act_ready, 6 * s + (2 * p + 2))
                    for m in range(KD):
                        v = KD * p + m
                        b = 4 + v % 4
                        pe.wait_ge(f_free[b], 6 * s + (v // 4 + 1))
                        for j in range(2):
                            ins = split_product(ps[b][:, 0:e - a],
                                                [w[4 + j][:, m * P:(m + 1) * P] for w in (wf_hi, wf_lo)],
                                                [act_hi[:, j, a:e], act_lo[:, j, a:e]], j == 0, j == 1)
                        ins.then_inc(f_done[b], 1)
            for p, (a, e, _) in enumerate(PIECES):
                pe.wait_ge(f_free[p], 1 + 3 * FFN_STEPS)
                pe.wait_ge(sq3_summed, (KD - 1) * (p + 1))
                mm(ps[p][:, 0:e - a], ones[:], sq_end_sum[p], start=True, stop=True).then_inc(ms3_ready, 1)

        @block.scalar
        def _(act):
            own = Chain(act, act_step)
            fn = nc.scalar.activation

            def take_mix(units, it, j):
                b = units.bank(j)
                act.wait_ge(mix_done[b], units.nth(it, j) + 1)
                return mix(b), mix_free[b]

            def mix_taken(units, it, j):
                act.wait_ge(mix_free[units.bank(j)], units.nth(it, j) + 1)

            def take_proj(use, b):
                act.wait_ge(proj_done[b], use + 1)
                return ps[b], proj_free[b]

            act.wait_ge(cvec_in, 16)
            fn(csilu[:], cvec[:], ACT.Silu).then_inc(csilu_set, 1)

            def take_row(g):
                src, free = take_mix(u_setup, 0, ROW_UNIT[g])
                if g > 1:
                    act.wait_ge(mod_ready, g - 1)
                own(fn(ada_row[0:2, g % 2 * 256:g % 2 * 256 + 256], src[0:2, 0:256], ACT.Copy))
                act.sem_inc(free, 1)
                act.sem_inc(ada_row_ready, 1)

            for j in range(6):
                a, e, _ = PIECES[j % 3]
                act.wait_ge(arg_ready, j + 1)
                fn((h1f if j < 3 else h2f[:, :])[:, a:e], arg[:, a:e], ACT.Sin).then_inc(sin_ready, 1)
                if j in (1, 3):
                    take_row(j // 2)
            for g in range(ADA_FIRST):
                for k in SQUARES_AT[g]:
                    act.wait_ge(x_loaded[k], 16)
                    if k >= 2:
                        act.wait_ge(x_sq_summed, k - 1)
                    fn((x_sq if k else x_sq_sum)[:], x_in[:, k, :], ACT.Square).then_inc(sq_ready, 1)
                if g == 3:
                    act.wait_ge(sp_ready, 1)
                    fn(sp_w[:, 2, :], sp_w[:, 1, :], ACT.Exp).then_inc(sp_e, 1)
                    act.wait_ge(sp_ready, 2)
                    fn(sp_w[:, 4, :], sp_w[:, 3, :], ACT.Ln).then_inc(sp_l, 1)
                if g == ADA_FIRST - 2:
                    act.wait_ge(consts_set, 3)
                    for b, (a, e, _) in enumerate(PIECES):
                        src, free = take_proj(0, b)
                        fn(rstd0[:, a:e], src[:, 0:e - a], ACT.Sqrt, bias=eps[:, 0:1],
                           scale=1.0 / D).then_inc(free, 1)
                if 2 <= g + 1 < ADA_FIRST:
                    take_row(g + 1)

            def round_normed(p, u_at, shift_chunk, made, rounded):
                a, e, seq = PIECES[p]
                for k in range(KD):
                    act.wait_ge(made, KD * p + k + 1)
                    fn(h_hi[:, k, a:e], u_at(k, a, e), ACT.Identity,
                       bias=mod[:, shift_chunk + k, seq:seq + 1]).then_inc(rounded, 1)

            for p in range(3):
                round_normed(p, norm1_u, 0, u_ready, hi_ready)
            own.restart()

            act.wait_ge(hin_zero, 1)

            def into_padded(use, dst):
                for b, (a, e, seq) in enumerate(PIECES):
                    src, free = take_proj(use, b)
                    at = PAD_CTX if seq else PAD_LAT + a
                    fn(dst[:, at:at + e - a], src[:, 0:e - a], ACT.Copy).then_inc(free, 1)

            def taps_squares(i):
                act.wait_ge(taps_ready, i + 1)
                fn(f_a[:, 0:2 * NT, :], taps[:, :, :, :].rearrange("p n d c -> p (n d) c"),
                   ACT.Square).then_inc(taps_sq, 1)

            def l1_pass(i, units, it, last):
                src, free = take_mix(units, it, 0)
                act.wait_ge(mod_ready, i + ADA_FIRST)
                own(fn(ada_row[0:2, :], src[0:2, :], ACT.Copy))
                act.sem_inc(free, 1)
                act.sem_inc(ada_row_ready, 1)
                src, free = take_mix(units, it, 1)
                fn(rs_k[:, :, :], src[:, 0:2 * P].rearrange("p (s c) -> p s c", s=2), ACT.Sqrt,
                   bias=eps[:, 0:1]).then_inc(free, 1)
                act.wait_ge(hy_conved, 2 * i + 1)
                into_padded(2 * i + 1, hin)
                act.wait_ge(hy_conved, 2 * i + 2)
                into_padded(2 * i + 2, hin)
                if not last:
                    act.wait_ge(mix_done[units.bank(12)], units.nth(it, 12) + 1)
                    taps_squares(i + 1)
                own.restart()

            taps_squares(0)
            with act.Fori(0, 7) as i:
                l1_pass(i, u1, i, False)
            l1_pass(7, u1_last, 0, True)

            act.wait_ge(hin_zero, 2)
            act.wait_ge(k_stored, 16 * 9)

            def take_fnet_channels(c):
                for j in range(5):
                    src, free = take_mix(u2, c, FN1_UNIT + j)
                    fn(fn_c[:, 2 * j:2 * j + 2, :, :].rearrange("p a b c -> p (a b c)"), src[:, 0:512],
                       ACT.Copy).then_inc(free, 1)

            def take_fnet_tokens(c):
                for j in range(3):
                    src, free = take_mix(u2, c, FN2_UNIT + j)
                    if j < 2:
                        dst = fn_y[:, 0:LAT].rearrange("p (f k) -> p k f", k=NL)[:, 4 * j:4 * j + 4, :]
                        src = src[:, 0:512].rearrange("p (k f) -> p k f", k=4)
                    else:
                        for q in range(2):
                            mix_taken(u2, c, FN2_UNIT + q)
                        dst = fn_y[:, LAT:T].rearrange("p (f k) -> p k f", k=NC)
                        src = src[:, 0:256].rearrange("p (k f) -> p k f", k=2)
                    fn(dst, src, ACT.Copy).then_inc(free, 1)

            with act.Fori(0, KD // 2) as m:
                for s in range(2):
                    n = 2 * m + s
                    act.wait_ge(xr_ready, n + 1)
                    into_padded(2 * n + (L2_TILE0 + 1), rin)
                    if s == 1:
                        take_fnet_tokens(m)
                    act.wait_ge(zc_ready, n + 1)
                    for b, (a, e, _) in enumerate(PIECES):
                        src, free = take_proj(2 * n + (L2_TILE0 + 2), b)
                        fn(g_ry[:, a:e], src[:, 0:e - a], ACT.Gelu_apprx_tanh).then_inc(free, 1)
                    act.wait_ge(zc_stored, 16 * n + 16)
                    act.wait_ge(hy_stored, 16 * TILES_L1)
                    for j in range(12):
                        d, which = j // 6, j // 3 % 2
                        a, e, _ = PIECES[j % 3]
                        src, free = take_mix(u2, m, RG_UNIT[s] + j)
                        bias = (R_BR, R_BI)[which] + d
                        fn((r_b, i_b)[which][d][:, a:e], src[:, 0:e - a], ACT.Sigmoid,
                           bias=rpack[s][:, bias:bias + 1]).then_inc(free, 1)
                    for d in range(2):
                        for j in range(3):
                            mix_taken(u2, m, RG_UNIT[s] + 6 * d + j)
                        own.add(fn(a_b[d][:], r_b[d][:], ACT.Exp, scale=sp_neg[:, bass.ds(2 * n + d, 1)]))
                        own.add(fn(t_b[d][:], r_b[d][:], ACT.Tanh, scale=sp_pos[:, bass.ds(2 * n + d, 1)]))
                        own.settle()
                        fn(r_b[d][:], a_b[d][:], ACT.Square).then_inc(a2_ready, 1)
                    for d in range(2):
                        act.wait_ge(m2_ready, 2 * n + (d + 1))
                        fn(r_b[d][:], r_b[d][:], ACT.Sqrt).then_inc(root_ready, 1)
                    if s == 0:
                        take_fnet_channels(m)
                    own.restart()

            with act.Fori(0, CH) as c:
                for order in range(2):
                    j0 = 14 * order

                    def gate(g, pieces=(0, 1, 2)):
                        n = 3 * order + g
                        act.wait_ge(gate_stored, 96 * c + 16 * (n + 1))
                        for b in pieces:
                            a, e, _ = PIECES[b]
                            src, free = take_proj(6 * c + (L3_TILE0 + 1 + n), b)
                            fn(g_st[:, a:e], src[:, 0:e - a], ACT.Sigmoid).then_inc(free, 1)

                    if order == 0:
                        act.wait_ge(zc_ready, 1 + KD)
                    gate(0)
                    act.wait_ge(z_ready, 2 * c + (order + 1))
                    for j in range(3):
                        src, free = take_mix(u3, c, j0 + j)
                        w = min(4, NT - 4 * j)
                        fn(ztok[:, 4 * j:4 * j + w, :].rearrange("p a c -> p (a c)"), src[:, 0:w * P],
                           ACT.Copy).then_inc(free, 1)
                    gate(1, (0, 1))
                    for j in range(6):
                        src, free = take_mix(u3, c, j0 + 3 + j)
                        fn(hy_z[:, 4 * j:4 * j + 4, :].rearrange("p a c -> p (a c)"), src[:],
                           ACT.Copy).then_inc(free, 1)
                    gate(1, (2,))
                    gate(2, (0, 1))
                    for j in range(5):
                        src, free = take_mix(u3, c, j0 + 9 + j)
                        fn(hy_z[:, 4 * j:4 * j + 4, :].rearrange("p a c -> p (a c)"), src[:],
                           ACT.Copy).then_inc(free, 1)
                    gate(2, (2,))

            use0 = OUT_TILE0 + 1
            for n in range(16):
                raw, loaded, count, _ = raw_z(n)
                act.wait_ge(loaded, count)
                if n == 12:
                    for b in range(3):
                        act.wait_ge(proj_done[b], use0 + 8)
                dst = h_hi[:, n - 4, :] if 4 <= n < 12 else z2_hi[:, n % 12, :]
                fn(dst, raw[:], ACT.Copy).then_inc(zhi_ready, 1)
            for b in range(3):
                act.wait_ge(proj_done[b], use0 + 16)
            for m in range(KD):
                act.wait_ge(side_used, KD + m + 1)
                fn(h_hi[:, m, :], x1[:, m, :], ACT.Copy).then_inc(mhi_ready, 1)
            for k in range(KD):
                for b, (a, e, _) in enumerate(PIECES):
                    act.wait_ge(proj_free[b], use0 + 24 + k + 1)
                    if k >= 2:
                        act.wait_ge(sq_summed, 3 * (k - 2) + b + 1)
                    fn((sq_o if k else sq_sum)[:, a:e], x1[:, k, a:e], ACT.Square).then_inc(sq1_ready, 1)
            for p, (a, e, _) in enumerate(PIECES):
                b = NORM_BANKS[p]
                act.wait_ge(mix_done[b], out_base[b] + 1)
                fn(mix(b)[:, 0:e - a], mix(b)[:, 0:e - a], ACT.Sqrt, bias=eps[:, 0:1],
                   scale=1.0 / D).then_inc(mix_free[b], 1)
            for p in range(2):
                round_normed(p, norm2_u, 3 * KD, u2_ready, h2_hi)

            def up_bank(n):
                return (2 * n + 1) % 4, (2 * n + 1) // 4

            def ffn_step(s, first):
                for n in range(7):
                    if first and n == 2:
                        round_normed(2, norm2_u, 3 * KD, u2_ready, h2_hi)
                    if n < 6:
                        a, e, _ = PIECES[n // 2]
                        b = 2 * n % 4
                        act.wait_ge(f_done[b], 3 * s + (2 * n // 4 + 1))
                        if n >= 2 or not first:
                            pb, puse = up_bank((n - 2) % 6)
                            act.wait_ge(f_free[pb], 3 * s + (puse + 2 - (3 if n < 2 else 0)))
                        fn(sil[n % 2][:, 0:e - a], ps[b][:, 0:e - a], ACT.Silu).then_inc(f_free[b], 1)
                    if n >= 1:
                        q = n - 1
                        pb, puse = up_bank(q)
                        act.wait_ge(f_free[pb], 3 * s + (puse + 2))
                        a, e, _ = PIECES[q // 2]
                        if not first:
                            v = KD * (q // 2) + KD - 1
                            act.wait_ge(f_done[4 + v % 4], 6 * s + (v // 4 + 1 - 6))
                        fn(act_hi[:, q % 2, a:e], a32[q % 2][:, 0:e - a], ACT.Copy).then_inc(ahi_ready, 1)

            ffn_step(0, True)
            with act.Fori(1, FFN_STEPS) as s:
                ffn_step(s, False)
            act.wait_ge(split_done, N_TILES)
            for p, (a, e, _) in enumerate(PIECES):
                for k in range(KD):
                    v = KD * p + k
                    act.wait_ge(f_free[4 + v % 4], 6 * (FFN_STEPS - 1) + v // 4 + 2)
                    if k >= 3:
                        act.wait_ge(sq3_summed, (KD - 1) * p + k - 2)
                    elif k:
                        act.wait_ge(sq3_summed, (KD - 1) * p)
                    dst = sq_end[k % 2][:, 0:e - a] if k else sq_end_sum[p]
                    fn(dst, x1[:, k, a:e], ACT.Square).then_inc(sq3_ready, 1)
            for p, (a, e, _) in enumerate(PIECES):
                act.wait_ge(ms3_ready, p + 1)
                fn(ps[p][:, 0:e - a], ps[p][:, 0:e - a], ACT.Sqrt, bias=eps[:, 0:1],
                   scale=1.0 / D).then_inc(root3_ready, 1)

        @block.vector
        def _(dve):
            own = Chain(dve, dve_step)
            bf = Butterfly(dve, own)
            tt, ts, stt = nc.vector.tensor_tensor, nc.vector.tensor_scalar, nc.vector.scalar_tensor_tensor

            def take_mix(units, it, j):
                b = units.bank(j)
                dve.wait_ge(mix_done[b], units.nth(it, j) + 1)
                return mix(b), mix_free[b]

            def mix_taken(units, it, j):
                dve.wait_ge(mix_free[units.bank(j)], units.nth(it, j) + 1)

            def proj_taken(use):
                for b in range(3):
                    dve.wait_ge(proj_free[b], use + 1)

            dve.wait_ge(filt_in, 32)
            for j in range(6):
                a, e, _ = PIECES[j % 3]
                src, free = take_mix(u_setup, 0, FILT_UNIT[j])
                if j >= 3:
                    dve.wait_ge(sin_ready, j - 2)
                layer = j // 3
                x, n = arg[:, a:e], turns[:, a:e]
                ts(x, src[0:FILT_HID, 0:e - a], f_vec[:, layer:layer + 1], f_vec[:, 2:3], ALU.add,
                   ALU.mult).then_inc(free, 1)
                dve.wait_ge(free, u_setup.nth(0, FILT_UNIT[j]) + 1)
                own(ts(n, x, 1.0 / (2 * math.pi), ROUND, ALU.mult, ALU.add))
                own(ts(n, n, ROUND, None, ALU.subtract))
                for part in TWO_PI:
                    own(stt(x, n, -part, x, ALU.mult, ALU.add))
                ts(x, x, PI_BELOW, -PI_BELOW, ALU.min, ALU.max).then_inc(arg_ready, 1)
            def ada_add(units, it, j, group, n):
                src, free = take_mix(units, it, j)
                tt(mod[:, bass.ds(2 * group, n), :], src[:, 0:2 * n].rearrange("p (a b) -> p a b", a=n),
                   vec[:, bass.ds(2 * group + V_BADA, n)].unsqueeze(2).to_broadcast([P, n, 2]),
                   ALU.add).then_inc(free, 1)
                dve.wait_ge(free, units.nth(it, j) + 1)
                dve.sem_inc(mod_ready, 1)

            def softplus():
                dve.wait_ge(vec_in, 16)
                lam = vec[:, V_LAM:V_LAM + 16]
                w = [sp_w[:, n, :] for n in range(6)]
                own(ts(w[0], lam, -1.0, None, ALU.mult))
                own(tt(w[1], lam, w[0], ALU.min))
                own(ts(w[0], w[0], 0.0, None, ALU.max))
                dve.sem_inc(sp_ready, 1)
                dve.wait_ge(sp_e, 1)
                own(ts(w[3], w[2], 1.0, None, ALU.add))
                dve.sem_inc(sp_ready, 1)
                own(ts(w[5], w[3], 1.0, None, ALU.subtract))
                own(ts(sp_pos[:], w[5], 0.0, None, ALU.is_equal))
                own(tt(w[5], w[5], sp_pos[:], ALU.add))
                own(nc.vector.reciprocal(w[5], w[5]))
                dve.wait_ge(sp_l, 1)
                own(tt(w[4], w[4], sp_pos[:], ALU.add))
                own(tt(w[4], w[4], w[5], ALU.mult))
                own(tt(w[4], w[4], w[2], ALU.mult))
                own(tt(w[4], w[4], w[0], ALU.add))
                own(ts(sp_pos[:], w[4], RG_C, None, ALU.mult))
                own(ts(sp_neg[:], w[4], -RG_C, None, ALU.mult))

            for g in range(ADA_FIRST):
                for k in SQUARES_AT[g]:
                    if k:
                        dve.wait_ge(sq_ready, k + 1)
                        if k >= 2:
                            dve.wait_ge(x_sq_summed, k - 1)
                        tt(x_sq_sum[:], x_sq_sum[:], x_sq[:], ALU.add).then_inc(x_sq_summed, 1)
                if g == 3:
                    softplus()
                if g == ADA_FIRST - 2:
                    for p, (a, e, _) in enumerate(PIECES):
                        dve.wait_ge(proj_free[p], 1)
                        own(nc.vector.reciprocal(rstd0[:, a:e], rstd0[:, a:e]))
                ada_add(u_setup, 0, TURN_UNIT[g], g, 2)

            def norm_scale(gain, scale_chunk):
                for s in range(2):
                    own(stt(norm_a[:, :, s], mod[:, scale_chunk:scale_chunk + KD, s], 1.0,
                            vec[:, gain:gain + KD], ALU.add, ALU.mult))

            def norm_piece(p, x, root, u_at, shift_chunk, made, rounded, ready):
                a, e, seq = PIECES[p]
                for k in range(KD + 1):
                    if k < KD:
                        if KD * p + k >= 2:
                            dve.wait_ge(ready, KD * p + k - 1)
                        stt(u_at(k, a, e), x[:, k, a:e], norm_a[:, k, seq:seq + 1], root, ALU.mult,
                            ALU.mult).then_inc(made, 1)
                    if k:
                        dve.wait_ge(rounded, KD * p + k)
                        stt(h_lo[:, k - 1, a:e], u_at(k - 1, a, e), mod[:, shift_chunk + k - 1, seq:seq + 1],
                            h_hi[:, k - 1, a:e].bitcast(F32), ALU.add, ALU.subtract).then_inc(ready, 1)

            norm_scale(V_N1, KD)
            for p, (a, e, _) in enumerate(PIECES):
                norm_piece(p, x_in, rstd0[:, a:e], norm1_u, 0, u_ready, hi_ready, h_ready)
            dve.wait_ge(h_ready, 3 * KD)
            own.settle()
            for a, e in ((0, PAD_LAT), (PAD_LAT + LAT, PAD_CTX), (PAD_CTX + CTX, PAD_T)):
                own(nc.vector.memset(hin[:, a:e], 0.0))
            dve.sem_inc(hin_zero, 1)
            own.restart()

            def depthwise(out, src, taps_at, bias, count, left, last_sem):
                for a, e, seq in SEQS:
                    at = (PAD_CTX if seq else PAD_LAT) - left
                    own.add(ts(out[:, a:e], src[:, at:at + e - a], taps_at(0), bias, ALU.mult, ALU.add))
                own.settle()
                for k in range(1, count):
                    for a, e, seq in SEQS:
                        at = (PAD_CTX if seq else PAD_LAT) - left + k
                        own.add(stt(out[:, a:e], src[:, at:at + e - a], taps_at(k), out[:, a:e],
                                    ALU.mult, ALU.add))
                    own.settle()
                dve.sem_inc(last_sem, 1)

            def first_stage(src, dst, tmp):
                out = spectrum_places(dst)
                real_dft_even(bf, places(src, P), places(tmp, P), out)
                real_dft_odd(bf, places(src, P), places(tmp, P), out)
                real_dft_context(bf, places(src, P, NL), out)
                own.settle()

            def take_k(i, units, it, unit, j, imag):
                if not imag and j == 0:
                    dve.wait_ge(k_stored, 16 * i + 16)
                src, free = take_mix(units, it, unit)
                base = FH * imag + 4 * j
                v = src[:, :].rearrange("p (a c) -> p a c", a=4)
                cuts = [(0, 4, 0)] if j < 2 else [(0, 1, 0), (1, 4, 1)]
                for n, (a, e, seq) in enumerate(cuts):
                    ins = tt(kstage[:, base + a:base + e, :], v[:, a:e, :],
                             rs_k[:, seq, :].unsqueeze(1).to_broadcast([P, e - a, P]), ALU.mult)
                    if n < len(cuts) - 1:
                        own(ins)
                ins.then_inc(free, 1)

            def make_taps(units, it, j0, loads):
                dve.wait_ge(decay_in, loads)
                for j in range(5):
                    src, free = take_mix(units, it, j0 + j)
                    for s in range(2):
                        tile = 2 * j + s
                        ins = tt(taps[:, tile, :, :], src[:, 256 * s:256 * s + 256].rearrange("p (d c) -> p d c", d=2),
                                 decay[:, tile, :].unsqueeze(1).to_broadcast([P, 2, P]), ALU.mult)
                        if s == 0:
                            own(ins)
                    ins.then_inc(free, 1)
                for j in range(5):
                    mix_taken(units, it, j0 + j)
                own(nc.vector.memset(taps[0:1, 0, 1, :], 0.0))
                own(nc.vector.memset(taps[0:1, NL, 1, :], 0.0))
                dve.sem_inc(taps_ready, 1)

            def l1_pass(i, units, it, last):
                own(tt(tsum[:, :, :], taps[:, :, 0, :], taps[:, :, 1, :], ALU.add))
                dve.wait_ge(taps_sq, i + 1)
                for seq, (a, e) in enumerate(((0, 2 * NL), (2 * NL, 2 * NT))):
                    own(nc.vector.tensor_reduce(ss_k[:, seq, :], f_a[:, a:e, :].rearrange("p n c -> p c n"),
                                                AX_X, ALU.add))
                dve.sem_inc(ss_ready, 1)
                first_stage(tsum, f_a, f_t)
                dve.sem_inc(fa_ready, 1)
                own(tt(tsum[:, :, :], taps[:, :, 0, :], taps[:, :, 1, :], ALU.subtract))
                mix_taken(units, it, 1)
                own(nc.vector.reciprocal(rs_k[:, :, :], rs_k[:, :, :]))
                for j in range(3):
                    take_k(i, units, it, 2 + j, j, 0)
                for j in range(3):
                    mix_taken(units, it, 2 + j)
                first_stage(tsum, f_a, f_t)
                dve.sem_inc(fa_ready, 1)
                j0 = 5 if last else 10
                if not last:
                    make_taps(units, it, 5, 16 * i + 32)
                for j in range(3):
                    take_k(i, units, it, j0 + j, j, 1)
                ada_add(units, it, j0 + 3, 2 * i + ADA_FIRST, 4)
                for j in range(3):
                    mix_taken(units, it, j0 + j)
                dve.sem_inc(k_ready, 1)
                tile = 2 * i + 1
                proj_taken(tile + 1)
                dve.wait_ge(hy_stored, 16 * tile)
                depthwise(hout, hin, lambda k: vec[:, bass.ds(4 * tile + (V_HY + k), 1)],
                          vec[:, bass.ds(4 * tile + (V_HY + 3), 1)], 3, 1, hy_conved)
                own.restart()

            make_taps(u_taps, 0, 0, 16)
            own.restart()
            with dve.Fori(0, 7) as i:
                l1_pass(i, u1, i, False)
            l1_pass(7, u1_last, 0, True)

            for a, e in ((0, PAD_LAT), (PAD_LAT + LAT, PAD_CTX), (PAD_CTX + CTX, PAD_T)):
                own(nc.vector.memset(rin[:, a:e], 0.0))
            dve.sem_inc(hin_zero, 1)
            own.restart()

            def fnet_first_stage(c):
                dve.wait_ge(fn_in, 16 * c + 16)
                out = spectrum_places(fn_a)
                real_dft_even(bf, places(fn_u, P), places(fn_tmp, P), out)
                bf.add(fn_a[:, 9, :], fn_u[:, NL, :], fn_u[:, NL + 1, :])
                bf.sub(fn_a[:, 10, :], fn_u[:, NL, :], fn_u[:, NL + 1, :])
                own.settle()
                dve.sem_inc(fna_ready, 1)

            with dve.Fori(0, KD // 2) as m:
                for s in range(2):
                    n = 2 * m + s
                    proj_taken(2 * n + (L2_TILE0 + 1))
                    dve.wait_ge(rpack_in[s], 16 * m + 16)
                    pack = rpack[s]
                    depthwise(xr, rin, lambda k: pack[:, R_CONV + k:R_CONV + k + 1],
                              pack[:, R_CONVB:R_CONVB + 1], 4, 2, xr_ready)
                    if s == 0:
                        fnet_first_stage(m)
                    for d in range(2):
                        for j in range(3):
                            mix_taken(u2, m, RG_UNIT[s] + 6 * d + 3 + j)
                        own.add(tt(i_b[d][:], i_b[d][:], xr[:], ALU.mult))
                        dve.wait_ge(a2_ready, 2 * n + (d + 1))
                        stt(r_b[d][:], r_b[d][:], 1.0, t_b[d][:], ALU.add, ALU.mult).then_inc(m2_ready, 1)
                    for d in range(2):
                        dve.wait_ge(root_ready, 2 * n + (d + 1))
                        first = LAT if d == 0 else T - 1
                        own(nc.vector.memset(r_b[d][:, first:first + 1], 1.0))
                        own(tt(i_b[d][:], r_b[d][:], i_b[d][:], ALU.mult))
                        for a, e, seq in SEQS:
                            step = slice(a, e) if d == 0 else (slice(e - 1, a - 1, -1) if a else slice(e - 1, None, -1))
                            start = 0.0 if seq else pack[:, R_ST + d:R_ST + d + 1]
                            own.add(nc.vector.tensor_tensor_scan(t_b[d][:, step], a_b[d][:, step], i_b[d][:, step],
                                                                 start, ALU.mult, ALU.add))
                    own.settle()
                    own.add(nc.vector.tensor_copy(fin[:, bass.ds(n, 1), 0], t_b[0][:, T - 1:T]))
                    own.add(nc.vector.tensor_copy(fin[:, bass.ds(n, 1), 1], t_b[1][:, LAT:LAT + 1]))
                    own(tt(r_b[0][:], t_b[0][:], t_b[1][:], ALU.add))
                    proj_taken(2 * n + (L2_TILE0 + 2))
                    own(tt(r_b[0][:], r_b[0][:], g_ry[:], ALU.mult))
                    dve.sem_inc(zc_ready, 1)
                    own.restart()

            with dve.Fori(0, CH) as c:
                for order in range(2):
                    j0 = 14 * order
                    for j in range(3):
                        mix_taken(u3, c, j0 + j)
                    first_stage(ztok, hy_a, hy_z)
                    dve.sem_inc(hya_ready, 1)
                    for j in range(6):
                        mix_taken(u3, c, j0 + 3 + j)
                    dve.wait_ge(k_in, 32 * c + 16 * (order + 1))
                    re, im = slice(0, FH), slice(FH, 2 * FH)
                    own.add(tt(hy_a[:, re, :], hy_z[:, re, :], hy_k[:, re, :], ALU.mult))
                    own.add(tt(ztok[:, :, :], hy_z[:, im, :], hy_k[:, im, :], ALU.mult))
                    own(tt(hy_a[:, im, :], hy_z[:, re, :], hy_k[:, im, :], ALU.mult))
                    own(tt(hy_a[:, re, :], hy_a[:, re, :], ztok[:, :, :], ALU.subtract))
                    own(tt(ztok[:, :, :], hy_z[:, im, :], hy_k[:, re, :], ALU.mult))
                    own(tt(hy_a[:, im, :], hy_a[:, im, :], ztok[:, :, :], ALU.add))
                    dve.sem_inc(y_ready, 1)
                    for j in range(5):
                        mix_taken(u3, c, j0 + 9 + j)
                    b_at = inverse_places(hy_z)
                    inverse_latent(bf, b_at, places(hy_a, P), places(ztok, P))
                    inverse_context(bf, b_at, places(hy_a, P), places(ztok, P, NL))
                    own.settle()
                    dve.wait_ge(xg_in, 32 * c + 16 * (order + 1))
                    if order == 0:
                        dve.wait_ge(hbias_in, 16 * c + 16)
                        dve.wait_ge(v_in, 16 * c + 16)
                        dve.wait_ge(za_stored, 16 * c + 16)
                    y = ztok[:, 0:NT, :].rearrange("p a c -> p (a c)")
                    own(stt(z_b[:], (v_b, z_b)[order][:], hbias[:, order:order + 1], y, ALU.mult, ALU.add))
                    own(tt(z_b[:], z_b[:], x_b[:], ALU.mult))
                    dve.sem_inc(z_ready, 1)
                own.restart()

            use0 = OUT_TILE0 + 1

            def split_z(n):
                dve.wait_ge(zhi_ready, n + 1)
                if 4 <= n < 12:
                    hi, lo = h_hi[:, n - 4, :], h_lo[:, n - 4, :]
                else:
                    hi, lo = z2_hi[:, n % 12, :], z2_lo[:, n % 12, :]
                tt(lo, raw_z(n)[0][:], hi.bitcast(F32), ALU.subtract).then_inc(z_split, 1)

            def take_branch(job, m):
                dve.wait_ge(side_in[job % 2], 16 * (job // 2 + 1))
                for b, (a, e, _) in enumerate(PIECES):
                    dve.wait_ge(proj_done[b], use0 + job + 1)
                    dst = x1[:, m, a:e] if job < 8 else side[job % 2][:, a:e]
                    tt(dst, ps[b][:, 0:e - a], side[job % 2][:, a:e], ALU.mult).then_inc(proj_free[b], 1)
                if job >= 8:
                    proj_taken(use0 + job)
                    tt(x1[:, m, :], x1[:, m, :], side[job % 2][:], ALU.add).then_inc(side_used, 1)

            def split_merged(m):
                dve.wait_ge(mhi_ready, m + 1)
                tt(h_lo[:, m, :], x1[:, m, :], h_hi[:, m, :].bitcast(F32), ALU.subtract).then_inc(m_split, 1)

            for n in range(4):
                split_z(n)
            for n in range(4, 12):
                split_z(n)
                take_branch(n - 4, n - 4)
            for n in range(12, 16):
                split_z(n)
            for m in range(KD):
                if m == 0:
                    proj_taken(use0 + 7)
                take_branch(8 + m, m)
            for m in range(KD):
                if m == 0:
                    dve.wait_ge(side_used, KD)
                take_branch(16 + m, m)
                if m:
                    split_merged(m - 1)
            split_merged(KD - 1)
            dve.wait_ge(m_split, KD)

            def add_square(k, b):
                a, e, _ = PIECES[b]
                dve.wait_ge(sq1_ready, 3 * k + b + 1)
                if k >= 2:
                    dve.wait_ge(sq_summed, 3 * (k - 2) + b + 1)
                tt(sq_sum[:, a:e], sq_sum[:, a:e], sq_o[:, a:e], ALU.add).then_inc(sq_summed, 1)

            for m in range(KD):
                job = 24 + m
                dve.wait_ge(side_in[job % 2], 16 * (job // 2 + 1))
                for b, (a, e, seq) in enumerate(PIECES):
                    dve.wait_ge(proj_done[b], use0 + job + 1)
                    stt(x1[:, m, a:e], ps[b][:, 0:e - a], mod[:, 2 * KD + m, seq:seq + 1], side[job % 2][:, a:e],
                        ALU.mult, ALU.add).then_inc(proj_free[b], 1)
                    if m >= 2:
                        add_square(m - 1, b)
            for b in range(3):
                add_square(KD - 1, b)
            norm_scale(V_N2, 4 * KD)

            def norm2_piece(p):
                a, e, _ = PIECES[p]
                b = NORM_BANKS[p]
                dve.wait_ge(mix_free[b], out_base[b] + 1)
                own(nc.vector.reciprocal(mix(b)[:, 0:e - a], mix(b)[:, 0:e - a]))
                norm_piece(p, x1, mix(b)[:, 0:e - a], norm2_u, 3 * KD, u2_ready, h2_hi, h2_ready)

            norm2_piece(0)
            norm2_piece(1)

            def gated_unit(s, n):
                a, e, _ = PIECES[n // 2]
                gb, gn = 2 * n % 4, 2 * n // 4
                ub, un = (2 * n + 1) % 4, (2 * n + 1) // 4
                dve.wait_ge(f_free[gb], 3 * s + (gn + 2))
                dve.wait_ge(f_done[ub], 3 * s + (un + 1))
                if n >= 2:
                    dve.wait_ge(act_ready, 6 * s + (n - 1))
                tt(a32[n % 2][:, 0:e - a], sil[n % 2][:, 0:e - a], ps[ub][:, 0:e - a],
                   ALU.mult).then_inc(f_free[ub], 1)

            def gated_remainder(s, n):
                a, e, _ = PIECES[n // 2]
                dve.wait_ge(ahi_ready, 6 * s + (n + 1))
                tt(act_lo[:, n % 2, a:e], a32[n % 2][:, 0:e - a], act_hi[:, n % 2, a:e].bitcast(F32),
                   ALU.subtract).then_inc(act_ready, 1)

            def add_square_end(p, k):
                dve.wait_ge(sq3_ready, KD * p + k + 1)
                if k >= 2:
                    dve.wait_ge(sq3_summed, (KD - 1) * p + k - 1)
                a, e, _ = PIECES[p]
                tt(sq_end_sum[p], sq_end_sum[p], sq_end[k % 2][:, 0:e - a], ALU.add).then_inc(sq3_summed, 1)

            def ffn_step(s, first=False, last=False):
                for n in range(7):
                    if first and n == 2:
                        norm2_piece(2)
                    if n < 6:
                        gated_unit(s, n)
                    if n:
                        gated_remainder(s, n - 1)
                dve.wait_ge(act_ready, 6 * s + 6)
                for p, (a, e, seq) in enumerate(PIECES):
                    for m in range(KD):
                        v = KD * p + m
                        b = 4 + v % 4
                        dve.wait_ge(f_done[b], 6 * s + (v // 4 + 1))
                        stt(x1[:, m, a:e], ps[b][:, 0:e - a], mod[:, 5 * KD + m, seq:seq + 1], x1[:, m, a:e],
                            ALU.mult, ALU.add).then_inc(f_free[b], 1)
                        if last and m >= 2:
                            add_square_end(p, m - 1)
                    if last:
                        add_square_end(p, KD - 1)

            ffn_step(0, first=True)
            own.restart()
            with dve.Fori(1, FFN_STEPS - 1) as s:
                ffn_step(s)
            ffn_step(FFN_STEPS - 1, last=True)
            for p, (a, e, _) in enumerate(PIECES):
                dve.wait_ge(root3_ready, p + 1)
                root = ps[p][:, 0:e - a]
                own(nc.vector.reciprocal(root, root))
                for k in range(KD):
                    stt(x1[:, k, a:e], x1[:, k, a:e], vec[:, V_FG + k:V_FG + k + 1], root, ALU.mult,
                        ALU.mult).then_inc(y_out, 1)


def dft_constants():
    f64 = np.float64
    p = np.arange(P, dtype=f64)
    fwd = np.zeros((P, FH, 3, P))
    inv = np.zeros((P, FH, 3, P))
    for q in range(FH):
        n, f1 = (2 * LAT, q) if q < 9 else (2 * CTX, q - 9)
        radix = n // P
        angle = 2 * np.pi * np.outer(p, f1 + radix * p) / n
        fwd[:, q] = np.stack([np.cos(angle), np.sin(angle), -np.sin(angle)], axis=1)
        weight = (1.0 if f1 in (0, radix // 2) else 2.0) / n
        back = angle.T
        inv[:, q] = weight * np.stack([-np.sin(back), np.cos(back), np.sin(back)], axis=1)
    angle = 2 * np.pi * np.outer(p, p) / P
    fn_ch = np.stack([np.sin(angle), np.cos(angle), -np.sin(angle), -np.cos(angle)], axis=1)
    fn_t = np.zeros((P, NT, 2, P))
    for m in range(NT):
        length, f1 = (LAT, m) if m < NL else (CTX, m - NL)
        radix = length // P
        angle = 2 * np.pi * np.outer(p, f1 + radix * p) / length
        fn_t[:, m] = np.stack([np.cos(angle), np.sin(angle)], axis=1) / np.sqrt(length * P)
    return [a.astype(np.float32) for a in (fwd, inv, fn_ch, fn_t)]


def filter_constants():
    f32 = np.float32
    feats, windows = [], []
    deltas = np.linspace(-math.log(1e-2) / 1.5, -math.log(1e-2) / 0.3, D_HY).astype(f32)
    for length in (LAT, CTX):
        t = np.arange(length, dtype=f32) / f32(length)
        ang = f32(2.0 * math.pi) * t[:, None] * np.arange(1, 9, dtype=f32)
        feats.append(np.concatenate([t[:, None], np.sin(ang), np.cos(ang)], axis=-1).T)
        window = np.exp(-t[:, None] * deltas)
        windows.append(window.reshape(length // P, P, CH, P).transpose(2, 1, 0, 3))
    decay = np.concatenate(windows, axis=2).astype(f32)
    return np.concatenate(feats, axis=1).astype(f32), np.concatenate([decay, decay], axis=0)


def columns(v):
    return np.ascontiguousarray(v.reshape(-1, P).T)


def tiles(w):
    n = w.shape[1] // P
    return w.reshape(KD, P, n, P).transpose(2, 1, 0, 3).reshape(n, P, D)


def kernel(x_prompt, x_sample, c, state_rglru, c_ctx, norm1_g, norm2_g, w_ada, b_ada, w_in,
           hy_conv_w, hy_conv_b, hy_f_w1, hy_f_b1, hy_f_w2, hy_f_b2, hy_f_w3, hy_f_freq, hy_bias,
           w_a, w_b, rg_conv_w, rg_conv_b, rg_wr, rg_br, rg_wi, rg_bi, rg_lam, w_c, w_o,
           w_gu, w_down, final_g):
    import concourse.bacc as bacc
    from concourse.bass_utils import run_bass_kernel_spmd

    fwd, inv, fn_ch, fn_t = dft_constants()
    feats, decay = filter_constants()

    tokens = np.concatenate([np.asarray(x_sample)[0], np.asarray(x_prompt)[0]], axis=0)
    cond = np.stack([np.asarray(c)[0], np.asarray(c_ctx)])

    t_in = tiles(np.asarray(w_in)[0])
    order = list(range(16)) + [x for n in range(8) for x in (16 + n, 24 + n)] + list(range(32, 56))
    def narrow(w):
        return w.reshape(4, P, 4, 2, P).transpose(2, 1, 3, 0, 4).reshape(4, P, D)
    t_gu, t_down = tiles(np.asarray(w_gu)[0]), np.asarray(w_down)[0].reshape(FF, P, D)
    ffn = [x for s in range(FFN_STEPS) for x in
           (t_gu[2 * s], t_gu[FF + 2 * s], t_gu[2 * s + 1], t_gu[FF + 2 * s + 1], t_down[2 * s], t_down[2 * s + 1])]
    weights = np.concatenate([t_in[order], narrow(np.asarray(w_b)[0]), tiles(np.asarray(w_c)[0]),
                              narrow(np.asarray(w_a)[0]), tiles(np.asarray(w_o)[0]), np.stack(ffn)], axis=0)

    hy = np.concatenate([np.asarray(hy_conv_w)[0], np.asarray(hy_conv_b)], axis=0)
    hy = hy.reshape(4, 12, P).transpose(2, 1, 0)
    plain = np.broadcast_to(np.array([0, 1, 0, 0], np.float32), (P, 4, 4))
    hy = np.concatenate([hy, plain], axis=1).reshape(P, 64)
    lam = np.asarray(rg_lam)[0].reshape(2, KD, P).transpose(2, 1, 0).reshape(P, 16)
    vec = np.concatenate([columns(np.asarray(norm1_g)[0]), columns(np.asarray(norm2_g)[0]),
                          columns(np.asarray(final_g)), columns(np.asarray(b_ada)[0]), hy, lam], axis=1)

    wr, wi = np.asarray(rg_wr)[0], np.asarray(rg_wi)[0]
    mats = np.stack([wr[0], wi[0], wr[1], wi[1]], axis=0).transpose(1, 2, 0, 3).reshape(KD, P, 4 * P)
    per_chunk = [np.asarray(rg_conv_w)[0], np.asarray(rg_conv_b), np.asarray(rg_br)[0], np.asarray(rg_bi)[0],
                 np.asarray(state_rglru)[0, 0]]
    vectors = np.concatenate(per_chunk, axis=0).reshape(-1, KD, P).transpose(1, 2, 0)
    rpack = np.concatenate([mats, vectors], axis=2)

    w3 = np.asarray(hy_f_w3)[0].reshape(FILT_HID, 2, 2, CH, P).transpose(1, 3, 0, 2, 4).reshape(8, FILT_HID, 2 * P)
    arrays = {
        "x": tokens.T.reshape(KD, P, T),
        "cvec": cond.reshape(2, KD, P).transpose(2, 1, 0),
        "w_ada": np.asarray(w_ada)[0].reshape(KD, P, HALF_GROUPS, 256).transpose(2, 1, 0, 3)
                 .reshape(HALF_GROUPS, P, KD * 256),
        "weights": weights,
        "vec": vec,
        "rpack": rpack,
        "f_w1": np.asarray(hy_f_w1)[0],
        "f_w2": np.asarray(hy_f_w2)[0],
        "f_vec": np.stack([np.asarray(hy_f_b1)[0], np.asarray(hy_f_b2)[0], np.asarray(hy_f_freq)[0]], axis=1),
        "w3": w3,
        "hbias": np.asarray(hy_bias)[0].reshape(2, CH, P).transpose(1, 2, 0),
        "feats": feats,
        "decay": decay,
        "ident": np.eye(P, dtype=np.float32),
        "fwd": fwd,
        "inv": inv,
        "fn_ch": fn_ch,
        "fn_t": fn_t,
    }
    arrays = {k: np.ascontiguousarray(v) for k, v in arrays.items()}
    nc = bacc.Bacc("TRN2", target_bir_lowering=False, num_devices=1)
    dr = {k: nc.dram_tensor(f"in_{k}", v.shape, F32, kind="ExternalInput").ap() for k, v in arrays.items()}
    for name, shape in (("y", (P, KD, T)), ("state_out", (P, KD, 2))):
        dr[name] = nc.dram_tensor(f"out_{name}", shape, F32, kind="ExternalOutput").ap()
    for name, shape in SCRATCH:
        dr[name] = nc.dram_tensor(f"scratch_{name}", shape, F32).ap()
    build_program(nc, dr)
    got = run_bass_kernel_spmd(nc, [{f"in_{k}": v for k, v in arrays.items()}], core_ids=[0]).results[0]
    y = got["out_y"].transpose(1, 0, 2).reshape(D, T).T
    state = got["out_state_out"].transpose(2, 1, 0).reshape(1, 1, 2, D)
    return (np.ascontiguousarray(y[LAT:])[None], np.ascontiguousarray(y[:LAT])[None], np.ascontiguousarray(state))
```
